# Optimizing a Trainium2 kernel written in Bass

```python
import jax, jax.numpy as jnp
from jax import lax
import numpy as np
import math

D_MODEL = 1024
BATCH = 1
SEQ = 256
DEPTH = 2

N_MIXERS = 2
N_HEADS = 16
HEAD_DIM = D_MODEL // N_HEADS
MOBA_BLOCK = 256
MOBA_TOPK = 3
Q_CHUNK = 32
ROPE_THETA = 10000.0
CONV_WIDTH = 3
D_FF = 2816
RMS_EPS = 1e-6
NEG_INF = -1e30
N_CONV_LAYERS = (DEPTH + 1) // 2
N_ATTN_LAYERS = DEPTH // 2


def rmsnorm(x, g):
    xf = x.astype(jnp.float32)
    var = jnp.mean(xf * xf, axis=-1, keepdims=True)
    return (xf * lax.rsqrt(var + RMS_EPS)).astype(x.dtype) * g

def causal_dwconv(x, w):
    S = x.shape[1]
    xp = jnp.pad(x, ((0, 0), (CONV_WIDTH - 1, 0), (0, 0)))
    y = xp[:, 0:S] * w[0]
    for j in range(1, CONV_WIDTH):
        y = y + xp[:, j:j + S] * w[j]
    return y

def short_conv_mixer(h, w_in, w_conv, w_out):
    bcv = h @ w_in
    b, c, v = jnp.split(bcv, 3, axis=-1)
    return (b * causal_dwconv(c * v, w_conv)) @ w_out

def rope(x, pos):
    half = HEAD_DIM // 2
    inv = ROPE_THETA ** (-jnp.arange(half, dtype=jnp.float32) / half)
    ang = pos.astype(jnp.float32)[:, None] * inv[None, :]
    cos = jnp.cos(ang).astype(x.dtype)
    sin = jnp.sin(ang).astype(x.dtype)
    x1, x2 = x[..., :half], x[..., half:]
    return jnp.concatenate([x1 * cos - x2 * sin, x2 * cos + x1 * sin], axis=-1)

def moba_attention(h, w_qkv, w_o):
    Bsz, S, _ = h.shape
    qkv = (h @ w_qkv).reshape(Bsz, S, 3, N_HEADS, HEAD_DIM)
    q = jnp.transpose(qkv[:, :, 0], (0, 2, 1, 3))
    k = jnp.transpose(qkv[:, :, 1], (0, 2, 1, 3))
    v = jnp.transpose(qkv[:, :, 2], (0, 2, 1, 3))
    pos = jnp.arange(S, dtype=jnp.int32)
    q = rope(q, pos) * (HEAD_DIM ** -0.5)
    k = rope(k, pos)

    n_blocks = -(-S // MOBA_BLOCK)
    pad = n_blocks * MOBA_BLOCK - S
    k = jnp.pad(k, ((0, 0), (0, 0), (0, pad), (0, 0)))
    v = jnp.pad(v, ((0, 0), (0, 0), (0, pad), (0, 0)))
    k_blocks = k.reshape(Bsz, N_HEADS, n_blocks, MOBA_BLOCK, HEAD_DIM)
    v_blocks = v.reshape(Bsz, N_HEADS, n_blocks, MOBA_BLOCK, HEAD_DIM)
    k_mean = jnp.mean(k_blocks.astype(jnp.float32), axis=3).astype(k.dtype)

    topk = min(MOBA_TOPK, n_blocks)
    b_idx = jnp.arange(Bsz)[:, None, None, None]
    h_idx = jnp.arange(N_HEADS)[None, :, None, None]
    block_ids = jnp.arange(n_blocks)
    key_off = jnp.arange(MOBA_BLOCK)
    q_off = jnp.arange(Q_CHUNK)

    def chunk(c):
        q0 = c * Q_CHUNK
        qc = lax.dynamic_slice_in_dim(q, q0, Q_CHUNK, axis=2)
        qpos = q0 + q_off
        own = q0 // MOBA_BLOCK
        gate = jnp.einsum('bhqd,bhnd->bhqn', qc, k_mean).astype(jnp.float32)
        gate = jnp.where((block_ids < own)[None, None, None, :], gate, NEG_INF)
        _, top_i = lax.top_k(gate, topk)
        rank_valid = jnp.arange(topk) < jnp.minimum(own, MOBA_TOPK)
        kg = k_blocks[b_idx, h_idx, top_i]
        vg = v_blocks[b_idx, h_idx, top_i]
        s_sel = jnp.einsum('bhqd,bhqnjd->bhqnj', qc, kg).astype(jnp.float32)
        s_sel = jnp.where(rank_valid[:, None], s_sel, NEG_INF)
        s_sel = s_sel.reshape(Bsz, N_HEADS, Q_CHUNK, topk * MOBA_BLOCK)
        ko = lax.dynamic_slice_in_dim(k, own * MOBA_BLOCK, MOBA_BLOCK, axis=2)
        vo = lax.dynamic_slice_in_dim(v, own * MOBA_BLOCK, MOBA_BLOCK, axis=2)
        s_own = jnp.einsum('bhqd,bhjd->bhqj', qc, ko).astype(jnp.float32)
        kpos = own * MOBA_BLOCK + key_off
        s_own = jnp.where(kpos[None, :] <= qpos[:, None], s_own, NEG_INF)
        p = jax.nn.softmax(jnp.concatenate([s_sel, s_own], axis=-1), axis=-1).astype(v.dtype)
        p_sel = p[..., :topk * MOBA_BLOCK].reshape(Bsz, N_HEADS, Q_CHUNK, topk, MOBA_BLOCK)
        p_own = p[..., topk * MOBA_BLOCK:]
        return (jnp.einsum('bhqnj,bhqnjd->bhqd', p_sel, vg)
                + jnp.einsum('bhqj,bhjd->bhqd', p_own, vo))

    o = lax.map(chunk, jnp.arange(S // Q_CHUNK))
    o = jnp.transpose(o, (1, 0, 3, 2, 4)).reshape(Bsz, S, N_HEADS * HEAD_DIM)
    return o @ w_o

def conv_ffn(h, w_up, w_conv, w_down):
    gu = causal_dwconv(h @ w_up, w_conv)
    g, u = jnp.split(gu, 2, axis=-1)
    return (jax.nn.silu(g) * u) @ w_down

def first_inputs(seed: int = 0) -> dict:
    key = jax.random.key(seed)
    ks = jax.random.split(key, 16)
    D = D_MODEL
    f32 = jnp.float32

    def nrm(k, shape, scale):
        return jax.random.normal(k, shape, dtype=f32) * scale

    return {
        "x": nrm(ks[0], (BATCH, SEQ, D), 1.0),
        "mix_norm": 1.0 + nrm(ks[1], (DEPTH, D), 0.02),
        "sc_w_in": nrm(ks[2], (N_CONV_LAYERS, D, 3 * D), D ** -0.5),
        "sc_w_conv": nrm(ks[3], (N_CONV_LAYERS, CONV_WIDTH, D), CONV_WIDTH ** -0.5),
        "sc_w_out": nrm(ks[4], (N_CONV_LAYERS, D, D), D ** -0.5),
        "moba_w_qkv": nrm(ks[5], (N_ATTN_LAYERS, D, 3 * D), D ** -0.5),
        "moba_w_o": nrm(ks[6], (N_ATTN_LAYERS, D, D), D ** -0.5),
        "ffn_norm": 1.0 + nrm(ks[7], (DEPTH, D), 0.02),
        "ffn_w_up": nrm(ks[8], (DEPTH, D, 2 * D_FF), D ** -0.5),
        "ffn_w_conv": nrm(ks[9], (DEPTH, CONV_WIDTH, 2 * D_FF), CONV_WIDTH ** -0.5),
        "ffn_w_down": nrm(ks[10], (DEPTH, D_FF, D), D_FF ** -0.5),
        "final_norm": 1.0 + nrm(ks[11], (D,), 0.02),
    }

def first_block(x, mix_norm, sc_w_in, sc_w_conv, sc_w_out, moba_w_qkv, moba_w_o,
              ffn_norm, ffn_w_up, ffn_w_conv, ffn_w_down, final_norm):
    for i in range(DEPTH):
        h = rmsnorm(x, mix_norm[i])
        j = i // N_MIXERS
        if i % N_MIXERS == 0:
            x = x + short_conv_mixer(h, sc_w_in[j], sc_w_conv[j], sc_w_out[j])
        else:
            x = x + moba_attention(h, moba_w_qkv[j], moba_w_o[j])
        x = x + conv_ffn(rmsnorm(x, ffn_norm[i]), ffn_w_up[i], ffn_w_conv[i], ffn_w_down[i])
    return rmsnorm(x, final_norm)


POOL_WINDOWS = (2, 4, 8, 16)
POOL_GROUP = D_MODEL // 8
POOL_WIDTH = POOL_GROUP * len(POOL_WINDOWS)
SSM_D_INNER = D_MODEL
SSM_HEAD_DIM = 64
SSM_HEADS = SSM_D_INNER // SSM_HEAD_DIM
SSM_GROUPS = 2
SSM_STATE = 128
SSM_CONV = 4
SSM_CHUNK = 128
SSM_CONV_DIM = SSM_D_INNER + 2 * SSM_GROUPS * SSM_STATE
EVEN_IN = POOL_WIDTH + SSM_D_INNER + SSM_CONV_DIM + SSM_HEADS
EVEN_MIX = POOL_WIDTH + SSM_D_INNER
FOX_HEADS = 8
FOX_HEAD_DIM = 64
FOX_WIDTH = FOX_HEADS * FOX_HEAD_DIM
MLA_HEADS = 8
MLA_NOPE = 64
MLA_ROPE = 32
MLA_V = 64
MLA_Q_RANK = 512
MLA_KV_RANK = 256
ODD_IN = 3 * FOX_WIDTH + FOX_HEADS + MLA_Q_RANK + MLA_KV_RANK + MLA_ROPE
ODD_MIX = FOX_WIDTH + MLA_HEADS * MLA_V
ATTN_BLOCK = 128
D_FF_2 = -(-8 * D_MODEL // (3 * 256)) * 256
DEEPNORM_ALPHA = (2 * DEPTH) ** 0.25
DEEPNORM_BETA = (8 * DEPTH) ** -0.25
N_EVEN = (DEPTH + 1) // 2
N_ODD = DEPTH // 2
LN_EPS = 1e-5


F32 = jnp.float32

def layer_norm(x, g, b):
    xf = x.astype(F32)
    mu = jnp.mean(xf, axis=-1, keepdims=True)
    var = jnp.mean(jnp.square(xf - mu), axis=-1, keepdims=True)
    return ((xf - mu) * lax.rsqrt(var + LN_EPS) * g + b).astype(x.dtype)

def rms_norm(x, g):
    xf = x.astype(F32)
    return (xf * lax.rsqrt(jnp.mean(jnp.square(xf), axis=-1, keepdims=True) + RMS_EPS) * g).astype(x.dtype)

def rope_2(x, pos):
    half = x.shape[-1] // 2
    freqs = jnp.power(ROPE_THETA, -jnp.arange(half, dtype=F32) / half)
    ang = pos.astype(F32)[:, None] * freqs[None, :]
    cos, sin = jnp.cos(ang), jnp.sin(ang)
    x1 = x[..., :half].astype(F32)
    x2 = x[..., half:].astype(F32)
    return jnp.concatenate([x1 * cos - x2 * sin, x2 * cos + x1 * sin], axis=-1).astype(x.dtype)

def multiscale_pool(u, pool_w, pool_scale):
    b, s, _ = u.shape
    ng = len(POOL_WINDOWS)
    ug = u.reshape(b, s, ng, POOL_GROUP).astype(F32)
    cs = jnp.cumsum(ug, axis=1)
    pos = jnp.arange(s)
    means = []
    for g, w in enumerate(POOL_WINDOWS):
        c = cs[:, :, g]
        lagged = jnp.pad(c, ((0, 0), (w, 0), (0, 0)))[:, :s]
        count = jnp.minimum(pos + 1, w).astype(F32)[None, :, None]
        means.append((c - lagged) / count)
    diff = (jnp.stack(means, axis=2) - ug).astype(u.dtype)
    y = jnp.einsum('bsgc,gcd->bsgd', diff, pool_w).reshape(b, s, POOL_WIDTH)
    return y * pool_scale

def causal_dwconv_2(u, w, bias):
    c = u.shape[-1]
    out = lax.conv_general_dilated(
        u, w[:, None, :].astype(u.dtype), window_strides=(1,),
        padding=[(SSM_CONV - 1, 0)], dimension_numbers=('NWC', 'WIO', 'NWC'),
        feature_group_count=c)
    return out + bias

def mamba2_ssd(z, xbc, dt, conv_w, conv_b, dt_bias, a_log, d_skip, norm_w):
    b, s, _ = z.shape
    G, E, P, N, L = SSM_GROUPS, SSM_HEADS // SSM_GROUPS, SSM_HEAD_DIM, SSM_STATE, SSM_CHUNK
    nc = s // L
    xbc = jax.nn.silu(causal_dwconv_2(xbc, conv_w, conv_b))
    xs, bm, cm = jnp.split(xbc, [SSM_D_INNER, SSM_D_INNER + G * N], axis=-1)
    dt = jax.nn.softplus(dt.astype(F32) + dt_bias)
    a = -jnp.exp(a_log.astype(F32))
    xh = xs.reshape(b, nc, L, G, E, P).astype(F32)
    dtc = dt.reshape(b, nc, L, G, E)
    xdt = xh * dtc[..., None]
    da = dtc * a.reshape(G, E)
    bc = bm.reshape(b, nc, L, G, N).astype(F32)
    cc = cm.reshape(b, nc, L, G, N).astype(F32)
    acs = jnp.cumsum(da, axis=2).transpose(0, 1, 3, 4, 2)
    seg = acs[..., :, None] - acs[..., None, :]
    tri = jnp.tril(jnp.ones((L, L), dtype=bool))
    lmat = jnp.exp(jnp.where(tri, seg, -jnp.inf))
    cb = jnp.einsum('bclgn,bcsgn->bcgls', cc, bc)
    y_diag = jnp.einsum('bcgls,bcgels,bcsgep->bclgep', cb, lmat, xdt)
    decay_states = jnp.exp(acs[..., -1:] - acs)
    states = jnp.einsum('bclgn,bcgel,bclgep->bcgepn', bc, decay_states, xdt)
    chunk_decay = jnp.exp(acs[..., -1])

    def step(h, inp):
        st, dec = inp
        return h * dec[..., None, None] + st, h

    h0 = jnp.zeros((b, G, E, P, N), F32)
    _, prev = lax.scan(step, h0, (jnp.moveaxis(states, 1, 0), jnp.moveaxis(chunk_decay, 1, 0)))
    prev = jnp.moveaxis(prev, 0, 1)
    y_off = jnp.einsum('bclgn,bcgepn,bcgel->bclgep', cc, prev, jnp.exp(acs))
    y = y_diag + y_off + xh * d_skip.astype(F32).reshape(G, E)[:, :, None]
    y = y.reshape(b, s, SSM_D_INNER) * jax.nn.silu(z.astype(F32))
    return rms_norm(y, norm_w).astype(z.dtype)

def block_causal_attention(q, k, v, log_decay_cum):
    b, h, s, dk = q.shape
    nb = s // ATTN_BLOCK
    scale = dk ** -0.5
    qb = q.reshape(b, h, nb, ATTN_BLOCK, dk).transpose(2, 0, 1, 3, 4)
    fb = None if log_decay_cum is None else log_decay_cum.reshape(b, h, nb, ATTN_BLOCK).transpose(2, 0, 1, 3)
    kpos = jnp.arange(s)

    def one_block(args):
        qi, fi, i = args
        sc = jnp.einsum('bhqd,bhkd->bhqk', qi, k).astype(F32) * scale
        if fi is not None:
            sc = sc + fi[..., :, None] - log_decay_cum[:, :, None, :]
        qpos = i * ATTN_BLOCK + jnp.arange(ATTN_BLOCK)
        sc = jnp.where(kpos[None, :] <= qpos[:, None], sc, -jnp.inf)
        p = jax.nn.softmax(sc, axis=-1).astype(v.dtype)
        return jnp.einsum('bhqk,bhkd->bhqd', p, v)

    o = lax.map(one_block, (qb, fb, jnp.arange(nb)))
    return o.transpose(1, 0, 3, 2, 4).reshape(b, s, h * v.shape[-1])

def even_mixer(x, w_in, pool_w, pool_scale, conv_w, conv_b, dt_bias, a_log, d_skip, norm_w, w_out):
    proj = x @ w_in
    c1 = POOL_WIDTH
    c2 = c1 + SSM_D_INNER
    c3 = c2 + SSM_CONV_DIM
    u, z, xbc, dt = jnp.split(proj, [c1, c2, c3], axis=-1)
    y_pool = multiscale_pool(u, pool_w, pool_scale)
    y_ssm = mamba2_ssd(z, xbc, dt, conv_w, conv_b, dt_bias, a_log, d_skip, norm_w)
    return jnp.concatenate([y_pool, y_ssm], axis=-1) @ w_out

def odd_mixer(x, w_in, fgate_b, q_norm_w, w_uq, kv_norm_w, w_ukv, w_out):
    b, s, _ = x.shape
    proj = x @ w_in
    cuts = np.cumsum([FOX_WIDTH, FOX_WIDTH, FOX_WIDTH, FOX_HEADS, MLA_Q_RANK, MLA_KV_RANK]).tolist()
    qf, kf, vf, fl, cq, ckv, kr = jnp.split(proj, cuts, axis=-1)

    def heads(t, nh):
        return t.reshape(b, s, nh, -1).transpose(0, 2, 1, 3)

    log_f = jax.nn.log_sigmoid(fl.astype(F32) + fgate_b)
    fcum = jnp.cumsum(log_f, axis=1).transpose(0, 2, 1)
    o_fox = block_causal_attention(heads(qf, FOX_HEADS), heads(kf, FOX_HEADS), heads(vf, FOX_HEADS), fcum)

    pos = jnp.arange(s)
    q = heads(rms_norm(cq, q_norm_w) @ w_uq, MLA_HEADS)
    q = jnp.concatenate([q[..., :MLA_NOPE], rope_2(q[..., MLA_NOPE:], pos)], axis=-1)
    kv = heads(rms_norm(ckv, kv_norm_w) @ w_ukv, MLA_HEADS)
    k_rope = jnp.broadcast_to(rope_2(kr[:, None], pos), (b, MLA_HEADS, s, MLA_ROPE))
    k = jnp.concatenate([kv[..., :MLA_NOPE], k_rope], axis=-1)
    o_mla = block_causal_attention(q, k, kv[..., MLA_NOPE:], None)
    return jnp.concatenate([o_fox, o_mla], axis=-1) @ w_out

def swiglu(x, w_gate, w_up, w_down):
    return (jax.nn.silu(x @ w_gate) * (x @ w_up)) @ w_down

def second_inputs(seed: int = 0) -> dict:
    key = jax.random.key(seed)
    ks = iter(jax.random.split(key, 40))

    def nrm(shape, std):
        return jax.random.normal(next(ks), shape, F32) * std

    def gain(shape):
        return 1.0 + 0.1 * jax.random.normal(next(ks), shape, F32)

    dt0 = jnp.exp(jax.random.uniform(next(ks), (N_EVEN, SSM_HEADS), F32, math.log(1e-3), math.log(1e-1)))
    return {
        "x": jax.random.normal(next(ks), (BATCH, SEQ, D_MODEL), F32),
        "even_w_in": nrm((N_EVEN, D_MODEL, EVEN_IN), D_MODEL ** -0.5),
        "pool_w": nrm((N_EVEN, len(POOL_WINDOWS), POOL_GROUP, POOL_GROUP), POOL_GROUP ** -0.5),
        "pool_scale": gain((N_EVEN, POOL_WIDTH)),
        "conv_w": nrm((N_EVEN, SSM_CONV, SSM_CONV_DIM), SSM_CONV ** -0.5),
        "conv_b": nrm((N_EVEN, SSM_CONV_DIM), 0.01),
        "dt_bias": dt0 + jnp.log(-jnp.expm1(-dt0)),
        "a_log": jnp.log(jax.random.uniform(next(ks), (N_EVEN, SSM_HEADS), F32, 1.0, 16.0)),
        "d_skip": gain((N_EVEN, SSM_HEADS)),
        "ssm_norm_w": gain((N_EVEN, SSM_D_INNER)),
        "even_w_out": nrm((N_EVEN, EVEN_MIX, D_MODEL), EVEN_MIX ** -0.5 * DEEPNORM_BETA),
        "odd_w_in": nrm((N_ODD, D_MODEL, ODD_IN), D_MODEL ** -0.5),
        "fgate_b": jax.random.uniform(next(ks), (N_ODD, FOX_HEADS), F32, 1.0, 5.0),
        "q_norm_w": gain((N_ODD, MLA_Q_RANK)),
        "w_uq": nrm((N_ODD, MLA_Q_RANK, MLA_HEADS * (MLA_NOPE + MLA_ROPE)), MLA_Q_RANK ** -0.5),
        "kv_norm_w": gain((N_ODD, MLA_KV_RANK)),
        "w_ukv": nrm((N_ODD, MLA_KV_RANK, MLA_HEADS * (MLA_NOPE + MLA_V)), MLA_KV_RANK ** -0.5),
        "odd_w_out": nrm((N_ODD, ODD_MIX, D_MODEL), ODD_MIX ** -0.5 * DEEPNORM_BETA),
        "ffn_w_gate": nrm((DEPTH, D_MODEL, D_FF_2), D_MODEL ** -0.5),
        "ffn_w_up": nrm((DEPTH, D_MODEL, D_FF_2), D_MODEL ** -0.5),
        "ffn_w_down": nrm((DEPTH, D_FF_2, D_MODEL), D_FF_2 ** -0.5 * DEEPNORM_BETA),
        "ln_mix_g": gain((DEPTH, D_MODEL)),
        "ln_mix_b": nrm((DEPTH, D_MODEL), 0.02),
        "ln_ffn_g": gain((DEPTH, D_MODEL)),
        "ln_ffn_b": nrm((DEPTH, D_MODEL), 0.02),
    }

def second_block(x, even_w_in, pool_w, pool_scale, conv_w, conv_b, dt_bias, a_log, d_skip, ssm_norm_w,
              even_w_out, odd_w_in, fgate_b, q_norm_w, w_uq, kv_norm_w, w_ukv, odd_w_out,
              ffn_w_gate, ffn_w_up, ffn_w_down, ln_mix_g, ln_mix_b, ln_ffn_g, ln_ffn_b):
    for l in range(DEPTH):
        i = l // 2
        if l % 2 == 0:
            h = even_mixer(x, even_w_in[i], pool_w[i], pool_scale[i], conv_w[i], conv_b[i], dt_bias[i],
                           a_log[i], d_skip[i], ssm_norm_w[i], even_w_out[i])
        else:
            h = odd_mixer(x, odd_w_in[i], fgate_b[i], q_norm_w[i], w_uq[i], kv_norm_w[i], w_ukv[i], odd_w_out[i])
        x = layer_norm(DEEPNORM_ALPHA * x + h, ln_mix_g[l], ln_mix_b[l])
        x = layer_norm(DEEPNORM_ALPHA * x + swiglu(x, ffn_w_gate[l], ffn_w_up[l], ffn_w_down[l]),
                       ln_ffn_g[l], ln_ffn_b[l])
    return x


def setup_inputs(seed=0):
    out = dict(first_inputs(seed))
    for name, value in second_inputs(seed + 1).items():
        if name != "x":
            out[name + "_2"] = value
    return out


def reference(
    x, mix_norm, sc_w_in, sc_w_conv, sc_w_out, moba_w_qkv, moba_w_o, ffn_norm, ffn_w_up,
    ffn_w_conv, ffn_w_down, final_norm, even_w_in_2, pool_w_2, pool_scale_2, conv_w_2, conv_b_2,
    dt_bias_2, a_log_2, d_skip_2, ssm_norm_w_2, even_w_out_2, odd_w_in_2, fgate_b_2, q_norm_w_2,
    w_uq_2, kv_norm_w_2, w_ukv_2, odd_w_out_2, ffn_w_gate_2, ffn_w_up_2, ffn_w_down_2,
    ln_mix_g_2, ln_mix_b_2, ln_ffn_g_2, ln_ffn_b_2,
):
    x = first_block(
        x, mix_norm, sc_w_in, sc_w_conv, sc_w_out, moba_w_qkv, moba_w_o, ffn_norm, ffn_w_up,
        ffn_w_conv, ffn_w_down, final_norm,
    )
    return second_block(
        x, even_w_in_2, pool_w_2, pool_scale_2, conv_w_2, conv_b_2, dt_bias_2, a_log_2,
        d_skip_2, ssm_norm_w_2, even_w_out_2, odd_w_in_2, fgate_b_2, q_norm_w_2, w_uq_2,
        kv_norm_w_2, w_ukv_2, odd_w_out_2, ffn_w_gate_2, ffn_w_up_2, ffn_w_down_2, ln_mix_g_2,
        ln_mix_b_2, ln_ffn_g_2, ln_ffn_b_2,
    )


_drawn_inputs = setup_inputs


def setup_inputs(seed=0):
    import zlib

    import numpy as np

    out = dict(_drawn_inputs(seed))
    spreads = {}
    factors = {'ffn_norm': 3.149,
     'pool_scale_2': 3.271,
     'conv_b_2': 8.0,
     'q_norm_w_2': 8.0,
     'kv_norm_w_2': 8.0,
     'fgate_b_2': 36.136}
    for name, (base, spread) in spreads.items():
        noise = np.random.default_rng([zlib.crc32(name.encode()), seed]).standard_normal(out[name].shape)
        drawn = base * np.exp(spread * noise) if base else spread * noise
        out[name] = __import__('jax').numpy.asarray(drawn.astype(out[name].dtype))
    for name, factor in factors.items():
        out[name] = (out[name] * factor).astype(out[name].dtype)
    return out
```

```python
from contextlib import ExitStack

import numpy as np

import concourse.bass as bass
from concourse import mybir

F32 = mybir.dt.float32
F32R = mybir.dt.float32r
ACT = mybir.ActivationFunctionType
ALU = mybir.AluOpType
AX_X = mybir.AxisListType.X

D, S, FF = 1024, 256, 2816
CW = 2048
NRAW, NSPLIT = 5, 3
NEG = -1.0e30
ALPHA = float((2 * 2) ** 0.25)
RMS_EPS, LN_EPS = 1e-6, 1e-5



def weight_plan():
    plan = []

    def f(tag, name, layer, c0, n=256, pad=None):
        plan.append((tag, "F", name, layer, [(c0, n)], pad or n, 8, 0))

    def t(tag, name, layer, c0, n, kts, per):
        for k in range(0, kts, per):
            plan.append((tag, "T", name, layer, [(c0, n)], n, per, k))

    def ffn(up_g, up_u, g0, u0, down, layer):
        for m in range(11):
            f("g", up_g, layer, g0 + 256 * m)
            f("u", up_u, layer, u0 + 256 * m)
        t("down", down, layer, 0, 1024, 22, 2)

    for m in range(4):
        f("c", "sc_w_in", 0, 1024 + 256 * m)
        f("v", "sc_w_in", 0, 2048 + 256 * m)
        f("b", "sc_w_in", 0, 256 * m)
    t("sc_out", "sc_w_out", 0, 0, 1024, 8, 2)
    ffn("ffn_w_up", "ffn_w_up", 0, FF, "ffn_w_down", 0)
    for part in range(3):
        t("qkv", "moba_w_qkv", 0, 1024 * part, 1024, 8, 2)
    t("moba_out", "moba_w_o", 0, 0, 1024, 8, 2)
    ffn("ffn_w_up", "ffn_w_up", 0, FF, "ffn_w_down", 1)

    for m in range(2):
        f("pool", "even_w_in_2", 0, 256 * m)
    for m in range(6):
        f("xbc", "even_w_in_2", 0, 1536 + 256 * m)
    f("dt", "even_w_in_2", 0, 3072, 16, 128)
    t("z", "even_w_in_2", 0, 512, 1024, 8, 2)
    t("even_out", "even_w_out_2", 0, 0, 1024, 12, 2)
    ffn("ffn_w_gate_2", "ffn_w_up_2", 0, 0, "ffn_w_down_2", 0)
    plan.append(("flkr", "F", "odd_w_in_2", 0, [(1536, 8), (2312, 32)], 128, 8, 0))
    for m in range(2):
        f("qf", "odd_w_in_2", 0, 256 * m)
    for m in range(2):
        f("kf", "odd_w_in_2", 0, 512 + 256 * m)
    t("vf", "odd_w_in_2", 0, 1024, 512, 8, 4)
    t("cq", "odd_w_in_2", 0, 1544, 512, 8, 4)
    t("ckv", "odd_w_in_2", 0, 2056, 256, 8, 8)
    t("uq", "w_uq_2", 0, 0, 768, 4, 2)
    t("ukv", "w_ukv_2", 0, 0, 1024, 2, 2)
    t("odd_out", "odd_w_out_2", 0, 0, 1024, 8, 2)
    ffn("ffn_w_gate_2", "ffn_w_up_2", 0, 0, "ffn_w_down_2", 1)
    return plan


VEC = {}
_n = 0
for _name, _cols in (("mix_norm", 16), ("ffn_norm", 16), ("sc_w_conv", 24), ("ffn_w_conv", 264),
                     ("pool_scale_2", 4), ("conv_w_2", 48), ("conv_b_2", 12), ("ssm_norm_w_2", 8),
                     ("q_norm_w_2", 4), ("kv_norm_w_2", 2)):
    VEC[_name] = _n
    _n += _cols
NVEC = _n

CST = {}
_n = 0
for _name, _cols in (("ident", 128), ("uo", 256), ("gt", 128), ("mask", 256), ("rope", 128),
                     ("rope2", 64), ("cnt", 64)):
    CST[_name] = _n
    _n += _cols
NCST = _n


def constants():
    c = np.zeros((128, NCST), np.float32)
    i = np.arange(128)
    c[:, CST["ident"]:CST["ident"] + 128] = np.eye(128, dtype=np.float32)
    c[:, CST["uo"]:CST["uo"] + 128] = (i[:, None] <= i[None, :])
    c[:, CST["uo"] + 128:CST["uo"] + 256] = 1.0
    c[:, CST["gt"]:CST["gt"] + 128] = (i[:, None] > i[None, :])
    m = np.where(i[None, :] > i[:, None], np.float32(NEG), np.float32(0))
    c[:, CST["mask"]:CST["mask"] + 256] = np.concatenate([m, m], 1)
    for name, half in (("rope", 32), ("rope2", 16)):
        inv = np.power(np.float32(10000.0), -np.arange(half, dtype=np.float32) / np.float32(half),
                       dtype=np.float32)
        ang = np.arange(S, dtype=np.float32)[:, None] * inv[None, :]
        t = np.stack([np.cos(ang).reshape(2, 128, half), np.sin(ang).reshape(2, 128, half)], 1)
        c[:, CST[name]:CST[name] + 4 * half] = t.transpose(2, 0, 1, 3).reshape(128, 4 * half)
    for g in range(4):
        w = 2 << g
        c[:, CST["cnt"] + 16 * g:CST["cnt"] + 16 * g + 16] = (
            np.float32(1.0) / np.minimum(np.arange(16) + 1, w).astype(np.float32))
    oh = np.zeros((2, 104, 4, 256), np.float32)
    for h in range(8):
        oh[0, 64 * (h % 2) + h, h // 2, :] = 1.0
        oh[1, 64 * (h % 2) + 32 + h, h // 2, :] = 1.0
    return c, oh.reshape(2, 104, 1024)




class Engine:

    def __init__(self, eng, sem):
        self.eng, self.sem, self.n, self.waited = eng, sem, 0, {}

    def wait(self, *points):
        for p in points:
            if isinstance(p, list):
                self.wait(*p)
            elif p is not None and self.waited.get(p[0].name, 0) < p[1]:
                self.waited[p[0].name] = p[1]
                self.eng.wait_ge(p[0], p[1])

    def do(self, fn, *points):
        self.wait(*points)
        self.n += 1
        fn().then_inc(self.sem, 1)
        return (self.sem, self.n)

    def quiet(self, fn, *points):
        self.wait(*points)
        fn()

    def dma(self, fn, sem, *points):
        self.wait(*points)
        fn().then_inc(sem[0], 16)
        sem[1] += 16
        return (sem[0], sem[1])


def build(nc, wts, vec, cst, onehot, rows, small, pw, x_in, out):
    plan = weight_plan()
    with ExitStack() as ctx:
        sem = lambda name: ctx.enter_context(nc.semaphore(name))
        base = (nc.sbuf_base + 63) // 64 * 64
        limit = nc.sbuf_usable_end

        P, A, V, G, SP = (Engine(e, sem(n)) for e, n in (
            (nc.tensor, "s_pe"), (nc.scalar, "s_act"), (nc.vector, "s_dve"), (nc.gpsimd, "s_pool"),
            (nc.sync, "s_sp")))
        names = [0]

        class Area:

            def __init__(self, start):
                self.at = start

            def take(self, shape, dt=F32):
                n = 4
                for d in shape[1:]:
                    n *= d
                names[0] += 1
                t = nc.alloc_sbuf_tensor_at(f"t{names[0]}", shape, dt, offset=self.at)
                self.at += (n + 31) // 32 * 32
                assert self.at <= limit, (self.at, limit)
                return t

        fixed = Area(base)
        wraw = fixed.take([128, NRAW, CW])
        wh = fixed.take([128, NSPLIT, CW], F32R)
        wl = fixed.take([128, NSPLIT, CW], F32R)
        X = fixed.take([128, 2, D])
        XN = fixed.take([128, 2, D])
        XTh = fixed.take([128, 8, S], F32R)
        XTl = fixed.take([128, 8, S], F32R)
        vecs = fixed.take([128, NVEC])
        cs = fixed.take([128, NCST])
        sm = fixed.take([128, 56])
        grow = fixed.take([128, 1024])
        brow = fixed.take([128, 1024])
        st = fixed.take([128, 64])
        mhalf = fixed.take([128, 2])
        mix_base = fixed.at

        ps = ctx.enter_context(nc.psum_tensor("ps", [128, 8, 512], F32))
        free = [[] for _ in range(8)]

        class Ring:
            def __init__(self, banks):
                self.banks, self.i = banks, 0

            def take(self):
                b = self.banks[self.i % len(self.banks)]
                self.i += 1
                return b

        up_ring = Ring([4, 5, 6, 7])
        all_ring = Ring([4, 5, 6, 7, 0, 1, 2, 3])

        ident = cs[:, CST["ident"]:CST["ident"] + 128]
        UO = cs[:, CST["uo"]:CST["uo"] + 256]
        U = cs[:, CST["uo"]:CST["uo"] + 128]
        GT = cs[:, CST["gt"]:CST["gt"] + 128]
        MASK = cs[:, CST["mask"]:CST["mask"] + 256]
        ROPE = cs[:, CST["rope"]:CST["rope"] + 128].rearrange("p (t c d) -> p t c d", t=2, c=2)
        ROPE2 = cs[:, CST["rope2"]:CST["rope2"] + 64].rearrange("p (t c d) -> p t c d", t=2, c=2)

        def vcol(name, i, j=0):
            return vecs[:, VEC[name] + i + j:VEC[name] + i + j + 1]

        sem_in = [sem("s_in"), 0]
        sem_x = [sem("s_x"), 0]
        x_loaded = [A.dma(lambda t=t: nc.scalar.dma_start(X[:, t, :], x_in[0, t * 128:(t + 1) * 128, :]),
                          sem_x) for t in range(2)][-1]
        A.dma(lambda: nc.scalar.dma_start(vecs[:], vec), sem_in)
        A.dma(lambda: nc.scalar.dma_start(cs[:], cst), sem_in)
        consts = A.dma(lambda: nc.scalar.dma_start(sm[:], small.partition_broadcast(128)), sem_in)
        half = V.do(lambda: nc.vector.memset(mhalf[:], -0.5))
        sem_row = [sem("s_row"), 0]

        class Weights:
            def __init__(self):
                self.sems = [[sem(f"s_w{i}"), 0] for i in range(NRAW)]
                self.raw, self.hi, self.lo, self.used = [], [], [], []
                for i in range(NRAW):
                    self.load(i)
                for i in range(NSPLIT):
                    self.split(i)
                self.i = 0

            def width(self, i):
                return plan[i][5] * plan[i][6]

            def load(self, i):
                if i >= len(plan):
                    return
                w, k = self.width(i), i % NRAW
                old = [self.hi[i - NRAW], self.lo[i - NRAW]] if i >= NRAW else []
                self.raw.append(SP.dma(lambda: nc.sync.dma_start(wraw[:, k, 0:w], wts[i, :, 0:w]),
                                       self.sems[k], *old))

            def split(self, i):
                if i >= len(plan):
                    return
                w, r, k = self.width(i), i % NRAW, i % NSPLIT
                old = self.used[i - NSPLIT] if i >= NSPLIT else None
                self.hi.append(A.do(lambda: nc.scalar.copy(wh[:, k, 0:w], wraw[:, r, 0:w]),
                                    self.raw[i], old))
                self.lo.append(V.do(lambda: nc.vector.tensor_tensor(
                    wl[:, k, 0:w], wraw[:, r, 0:w], wh[:, k, 0:w].bitcast(F32), ALU.subtract),
                    self.hi[i], old))
                self.load(i + NRAW)

            def use(self, tag):
                i = self.i
                assert plan[i][0] == tag, (plan[i][0], tag)
                n, kk = plan[i][5], plan[i][6]
                view = lambda t: t[:, i % NSPLIT, 0:n * kk].rearrange("p (k n) -> p k n", k=kk)
                return view(wh), view(wl), self.lo[i]

            def done(self, point):
                self.used.append(point)
                self.i += 1

            def next_split(self):
                self.split(self.i - 1 + NSPLIT)

        W = Weights()

        def mm(o, a, b, start, stop):
            return lambda: nc.tensor.matmul(o, a, b, start=start, stop=stop)

        def f_chunk(tag, nblk, xready):
            H, L, ready = W.use(tag)
            b = up_ring.take()
            P.wait(ready, free[b])
            for blk in range(nblk):
                o = ps[:, b, blk * S:(blk + 1) * S]
                c = slice(blk * 128, (blk + 1) * 128)
                for kt in range(8):
                    P.quiet(mm(o, H[:, kt, c], XTh[:, kt, :], kt == 0, False), xready(kt))
                    P.quiet(mm(o, H[:, kt, c], XTl[:, kt, :], False, False))
                    m = mm(o, L[:, kt, c], XTh[:, kt, :], False, kt == 7)
                    if kt == 7 and blk == nblk - 1:
                        point = P.do(m)
                    else:
                        P.quiet(m)
            W.done(point)
            return b, point

        def t_chunk(tag, hi, lo, kt0, cols, dst, start, stop, xready):
            H, L, ready = W.use(tag)
            P.wait(ready)
            nk = H.shape[1]
            for k in range(nk):
                for t in range(2):
                    tt = slice(t * 128, (t + 1) * 128)
                    P.wait(xready(kt0 + k))
                    for n, (a, w, s0) in enumerate(((hi, H, True), (hi, L, False), (lo, H, False))):
                        for j, (c0, c1) in enumerate(cols):
                            last = n == 2 and stop and k == nk - 1
                            m = mm(dst(t, j), a(kt0 + k)[:, tt], w[:, k, c0:c1],
                                   start and k == 0 and s0, last)
                            if n == 2 and k == nk - 1 and t == 1 and j == len(cols) - 1:
                                point = P.do(m)
                            else:
                                P.quiet(m)
            W.done(point)
            return point

        HALVES = [(0, 512), (512, 1024)]

        def acc(t, j):
            return ps[:, 2 * t + j, :]

        def t_proj(tag, nchunks, hi, lo, cols, dst, banks, xready, per=2, after=None):
            for b in banks:
                P.wait(free[b])
            for i in range(nchunks):
                point = t_chunk(tag, hi, lo, i * per, cols, dst, i == 0, i == nchunks - 1, xready)
                if after:
                    after(i)
                W.next_split()
            return point

        def split_out(src, hi, lo, scale, *points):
            return split_bank([(src, hi, lo, scale)], *points)[0]

        def split_bank(parts, *points):
            for src, hi, lo, scale in parts:
                if scale is None:
                    a = A.do(lambda: nc.scalar.copy(hi, src), *points)
                else:
                    a = A.do(lambda: nc.scalar.activation(hi, src, ACT.Copy, scale=scale), *points)
            done = []
            for src, hi, lo, scale in parts:
                if scale is None:
                    done.append(V.do(lambda: nc.vector.tensor_tensor(
                        lo, src, hi.bitcast(F32), ALU.subtract), a, *points))
                else:
                    done.append(V.do(lambda: nc.vector.scalar_tensor_tensor(
                        out=lo, in0=src, scalar=scale, in1=hi.bitcast(F32), op0=ALU.mult,
                        op1=ALU.subtract), a, *points))
            return done

        def to_feature(src, nkt, hi, lo, scale, ready, old=()):
            points = []
            for k0 in range(0, nkt, 2):
                b = up_ring.take()
                P.wait(free[b])
                for kt in (k0, k0 + 1):
                    for t in range(2):
                        o = ps[:, b, (kt - k0) * S + t * 128:(kt - k0) * S + (t + 1) * 128]
                        fn = lambda o=o, t=t, kt=kt: nc.tensor.transpose(o, src(t, kt), ident)
                        if kt == k0 + 1 and t == 1:
                            p = P.do(fn, ready[t], consts)
                        else:
                            P.quiet(fn, ready[t], consts)
                if scale is None:
                    v = split_out(ps[:, b, :], hi(k0, 2), lo(k0, 2), None, p, *old)
                    points += [v, v]
                else:
                    points += split_bank(
                        [(ps[:, b, (kt - k0) * S:(kt - k0 + 1) * S], hi(kt, 1), lo(kt, 1), scale(kt))
                         for kt in (k0, k0 + 1)], p, *old)
                    v = points[-1]
                free[b] = [v]
            return points

        def xt(t_):
            return lambda kt, n=1: t_[:, kt, :] if n == 1 else t_[:, kt:kt + n, :].rearrange(
                "p k s -> p (k s)")

        def inv_rms(ssq, n, eps, dst, *points):
            a = V.do(lambda: nc.vector.tensor_scalar(dst, ssq, 1.0 / n, eps, ALU.mult, ALU.add), *points)
            return G.do(lambda: nc.gpsimd.tensor_tensor(dst, dst, mhalf[:, 0:1], ALU.pow), a, half)

        def rms(src, dst, n, col, points, reader=None):
            done = []
            for t in range(2):
                c = st[:, col + t:col + t + 1]
                a = A.do(lambda t=t, c=c: nc.scalar.activation(dst(t), src(t), ACT.Square, accum_out=c),
                         points[t], reader)
                g = inv_rms(c, n, RMS_EPS, c, a)
                done.append(V.do(lambda t=t, c=c: nc.vector.tensor_scalar(
                    dst(t), src(t), c, None, ALU.mult), g))
            return done

        def residual(point):
            done = []
            for t in range(2):
                for j in range(2):
                    xs = X[:, t, j * 512:(j + 1) * 512]
                    v = V.do(lambda t=t, j=j, xs=xs: nc.vector.tensor_tensor(xs, acc(t, j), xs, ALU.add),
                             point)
                    free[2 * t + j] = [v]
                done.append(v)
            return done

        def prenorm(name, layer, points):
            done = rms(lambda t: X[:, t, :], lambda t: XN[:, t, :], D, 0, points)
            r = to_feature(lambda t, kt: XN[:, t, kt * 128:(kt + 1) * 128], 8, xt(XTh), xt(XTl),
                           lambda kt: vcol(name, 8 * layer + kt), done)
            return lambda kt: r[kt]

        def load_rows(g, b=None, *points):
            p = SP.dma(lambda: nc.sync.dma_start(grow[:], rows[g:g + 1, :].partition_broadcast(128)), sem_row,
                       *points)
            if b is not None:
                p = SP.dma(lambda: nc.sync.dma_start(
                    brow[:], rows[b:b + 1, :].partition_broadcast(128)), sem_row, *points)
            return p

        def postnorm(point, rp):
            done = []
            for t in range(2):
                for j in range(2):
                    xs = X[:, t, j * 512:(j + 1) * 512]
                    rs = XN[:, t, j * 512:(j + 1) * 512]
                    v = V.do(lambda t=t, j=j, xs=xs, rs=rs: nc.vector.scalar_tensor_tensor(
                        out=rs, in0=xs, scalar=ALPHA, in1=acc(t, j), op0=ALU.mult, op1=ALU.add,
                        accum_out=st[:, 8 * t + j:8 * t + j + 1]), point)
                    free[2 * t + j] = [v]
                s0, s1, nm, sq = (st[:, 8 * t + i:8 * t + i + 1] for i in range(4))
                v = V.do(lambda s0=s0, s1=s1: nc.vector.tensor_tensor(s0, s0, s1, ALU.add), v)
                v = V.do(lambda s0=s0, nm=nm: nc.vector.tensor_scalar(
                    nm, s0, -1.0 / D, None, ALU.mult), v)
                a = A.do(lambda t=t, nm=nm, sq=sq: nc.scalar.activation(
                    X[:, t, :], XN[:, t, :], ACT.Square, bias=nm, accum_out=sq), v)
                g = inv_rms(sq, D, LN_EPS, sq, a)
                v = V.do(lambda t=t, nm=nm, sq=sq: nc.vector.tensor_scalar(
                    XN[:, t, :], XN[:, t, :], nm, sq, ALU.add, ALU.mult), g)
                v = V.do(lambda t=t: nc.vector.tensor_tensor(XN[:, t, :], XN[:, t, :], grow[:], ALU.mult),
                         v, rp)
                v = V.do(lambda t=t: nc.vector.tensor_tensor(X[:, t, :], XN[:, t, :], brow[:], ALU.add), v)
                done.append(v)
            return done

        def x_to_feature(done):
            r = to_feature(lambda t, kt: X[:, t, kt * 128:(kt + 1) * 128], 8, xt(XTh), xt(XTl), None, done)
            return lambda kt: r[kt]

        def conv(src, dst, name, col, stride, taps, bias, *points):
            for blk in range(2):
                sl = slice(blk * S, (blk + 1) * S)
                w = vcol(name, col + blk + (taps - 1) * stride)
                if bias is None:
                    a = A.do(lambda: nc.scalar.activation(dst[:, sl], src[:, sl], ACT.Copy, scale=w),
                             *points)
                else:
                    a = A.do(lambda: nc.scalar.activation(dst[:, sl], src[:, sl], ACT.Identity, scale=w,
                                                          bias=vcol(*bias, blk)), *points)
            v = [a, a]
            for s_ in range(1, taps):
                for blk in range(2):
                    w = vcol(name, col + blk + (taps - 1 - s_) * stride)
                    o = dst[:, blk * S + s_:(blk + 1) * S]
                    v[blk] = V.do(lambda: nc.vector.scalar_tensor_tensor(
                        out=o, in0=src[:, blk * S:(blk + 1) * S - s_], scalar=w, in1=o, op0=ALU.mult,
                        op1=ALU.add), v[blk], *points)
            return v

        ffn_area = Area(mix_base)
        HTh = ffn_area.take([128, 22, S], F32R)
        HTl = ffn_area.take([128, 22, S], F32R)
        yg = ffn_area.take([128, 2, 512])
        yu = ffn_area.take([128, 2, 512])
        sg = ffn_area.take([128, 2, 512])
        pr = ffn_area.take([128, 2, 512])

        def ffn(layer, with_conv, xready):
            ready = {}
            read = {"yg": [None, None], "yu": [None, None], "sg": [None, None], "pr": [None, None]}
            for m in range(11):
                k = m % 2
                b, p = f_chunk("g", 2, xready)
                if with_conv:
                    v = conv(ps[:, b, :], yg[:, k, :], "ffn_w_conv", 132 * layer + 2 * m, 44, 3, None, p,
                             read["yg"][k])
                    free[b] = v
                    a = A.do(lambda: nc.scalar.activation(sg[:, k, :], yg[:, k, :], ACT.Silu), v,
                             read["sg"][k])
                    read["yg"][k] = a
                else:
                    a = A.do(lambda: nc.scalar.activation(sg[:, k, :], ps[:, b, :], ACT.Silu), p,
                             read["sg"][k])
                    free[b] = [a]
                W.next_split()
                b, p = f_chunk("u", 2, xready)
                if with_conv:
                    v = conv(ps[:, b, :], yu[:, k, :], "ffn_w_conv", 132 * layer + 22 + 2 * m, 44, 3, None,
                             p, read["yu"][k])
                    usrc, free[b] = yu[:, k, :], v
                else:
                    usrc, v = ps[:, b, :], p
                v = V.do(lambda: nc.vector.tensor_tensor(pr[:, k, :], usrc, sg[:, k, :], ALU.mult), v, a,
                         read["pr"][k])
                if not with_conv:
                    free[b] = [v]
                read["yu"][k] = read["sg"][k] = v
                h2, l2 = (t_[:, 2 * m:2 * m + 2, :].rearrange("p k s -> p (k s)") for t_ in (HTh, HTl))
                v = split_out(pr[:, k, :], h2, l2, None, v)
                read["pr"][k] = v
                ready[2 * m] = ready[2 * m + 1] = v
                W.next_split()
            return t_proj("down", 11, xt(HTh), xt(HTl), HALVES, acc, range(4), lambda kt: ready[kt])

        def attention(heads, dk, scale, qT, kT, v_of, bias, oh, ol, area, ready):
            NB = 3
            Pb = area.take([128, NB, 384])
            PT = area.take([128, NB, 384])
            sc = area.take([128, NB, 8])
            n = len(heads)
            exps, pts, trs, pvs = {}, {}, {}, {}
            obank = {}
            outs = {}

            def scores(i):
                h, k = heads[i], i % NB
                b = all_ring.take()
                P.wait(free[b], ready)
                blocks = ((0, 0, 0), (1, 1, 1), (2, 1, 0))
                for c, tq, tk in blocks:
                    o = ps[:, b, c * 128:(c + 1) * 128]
                    m = mm(o, qT(h)[:, tq * 128:(tq + 1) * 128], kT(h)[:, tk * 128:(tk + 1) * 128], True,
                           bias is None)
                    if bias is None and c == 2:
                        p = P.do(m)
                    else:
                        P.quiet(m)
                    if bias is not None:
                        q2, k2 = bias(h)
                        m = mm(o, q2[:, tq * 128:(tq + 1) * 128], k2[:, tk * 128:(tk + 1) * 128], False,
                               True)
                        if c == 2:
                            p = P.do(m)
                        else:
                            P.quiet(m)
                s2 = ps[:, b, 0:256]
                v = V.do(lambda: nc.vector.tensor_tensor(s2, s2, MASK, ALU.add), p, consts)
                V.do(lambda: nc.vector.reduce_max(sc[:, k, 0:1], ps[:, b, 0:128], AX_X), v,
                     pts.get(i - NB))
                v = V.do(lambda: nc.vector.reduce_max(sc[:, k, 1:2], ps[:, b, 128:384], AX_X), v)
                v = V.do(lambda: nc.vector.tensor_scalar(sc[:, k, 2:4], sc[:, k, 0:2], -scale, None,
                                                         ALU.mult), v)
                A.do(lambda: nc.scalar.activation(Pb[:, k, 0:128], ps[:, b, 0:128], ACT.Exp,
                                                  bias=sc[:, k, 2:3], scale=scale,
                                                  accum_out=sc[:, k, 4:5]), v, trs.get(i - NB))
                a = A.do(lambda: nc.scalar.activation(Pb[:, k, 128:384], ps[:, b, 128:384], ACT.Exp,
                                                      bias=sc[:, k, 3:4], scale=scale,
                                                      accum_out=sc[:, k, 5:6]))
                free[b] = [a]
                v = V.do(lambda: nc.vector.reciprocal(sc[:, k, 6:8], sc[:, k, 4:6]), a)
                V.do(lambda: nc.vector.tensor_scalar(Pb[:, k, 0:128], Pb[:, k, 0:128], sc[:, k, 6:7],
                                                     None, ALU.mult), v)
                pts[i] = V.do(lambda: nc.vector.tensor_scalar(
                    Pb[:, k, 128:384], Pb[:, k, 128:384], sc[:, k, 7:8], None, ALU.mult), v)

            def turn(i):
                k = i % NB
                b = all_ring.take()
                P.wait(free[b], pts[i])
                for c, src in ((0, 0), (1, 2), (2, 1)):
                    fn = lambda c=c, src=src: nc.tensor.transpose(
                        ps[:, b, c * 128:(c + 1) * 128], Pb[:, k, src * 128:(src + 1) * 128], ident)
                    if c == 2:
                        p = P.do(fn)
                    else:
                        P.quiet(fn)
                trs[i] = p
                a = A.do(lambda: nc.scalar.copy(PT[:, k, :], ps[:, b, 0:384]), p, pvs.get(i - NB))
                free[b] = [a]
                exps[i] = a

            def values(i):
                h, k = heads[i], i % NB
                if i % 2 == 0:
                    obank[i // 2] = all_ring.take()
                    P.wait(free[obank[i // 2]])
                b, r = obank[i // 2], 64 * (i % 2)
                P.quiet(mm(ps[r:r + 64, b, 0:256], v_of(h, 0), PT[:, k, 0:256], True, False), exps[i])
                pvs[i] = P.do(mm(ps[r:r + 64, b, 128:256], v_of(h, 1), PT[:, k, 256:384], False, True))
                if i % 2 == 1:
                    kt = h // 2
                    v = split_out(ps[:, b, 0:256], oh(kt), ol(kt), None, pvs[i])
                    free[b] = [v]
                    outs[kt] = v

            for i in range(n + 3):
                if i < n:
                    scores(i)
                if 2 <= i < n + 2:
                    turn(i - 2)
                if i >= 3:
                    values(i - 3)
            return outs

        def turn_heads(src, dk, n, dst, points, per):
            done = None
            for i0 in range(0, n, 2):
                b = all_ring.take()
                P.wait(free[b], *points, consts)
                for i in (i0, i0 + 1):
                    for t in range(2):
                        o = ps[0:dk, b, (i - i0) * S + t * 128:(i - i0) * S + (t + 1) * 128]
                        p = P.do(lambda o=o, i=i, t=t: nc.tensor.transpose(o, src(t, i), ident))
                e = A if (i0 // 2) % 2 == 0 else V
                cp = nc.scalar.copy if e is A else nc.vector.tensor_copy
                d2 = dst(i0)
                done = e.do(lambda cp=cp, d2=d2, b=b: cp(d2, ps[0:dk, b, :]), p)
                free[b] = [done]
                if e is A:
                    adone = done
            return [done, adone]

        def rope_half(src, dst, heads, half, tab, t, points, tmp, tmp_free):
            x1, x2 = src[:, :, 0:half], src[:, :, half:2 * half]
            o1, o2 = dst[:, :, 0:half], dst[:, :, half:2 * half]
            cos = tab[:, t, 0, :].unsqueeze(1).to_broadcast([128, heads, half])
            sin = tab[:, t, 1, :].unsqueeze(1).to_broadcast([128, heads, half])
            t1, t2 = tmp[0][:, 0:heads, :], tmp[1][:, 0:heads, :]
            V.do(lambda: nc.vector.tensor_tensor(t1, x2, sin, ALU.mult), *points, tmp_free)
            V.do(lambda: nc.vector.tensor_tensor(o1, x1, cos, ALU.mult))
            V.do(lambda: nc.vector.tensor_tensor(t2, x1, sin, ALU.mult))
            v = V.do(lambda: nc.vector.tensor_tensor(o2, x2, cos, ALU.mult))
            V.do(lambda: nc.vector.tensor_tensor(o1, o1, t1, ALU.subtract), v)
            return V.do(lambda: nc.vector.tensor_tensor(o2, o2, t2, ALU.add))

        def short_conv(xready):
            area = Area(mix_base)
            Mh, Ml = area.take([128, 8, S], F32R), area.take([128, 8, S], F32R)
            cS, cv, y, prod = (area.take([128, 2, 512]) for _ in range(4))
            ready, prod_read = {}, [None, None]
            for m in range(4):
                k = m % 2
                b, p = f_chunk("c", 2, xready)
                a = A.do(lambda: nc.scalar.copy(cS[:, k, :], ps[:, b, :]), p, prod_read[k])
                free[b] = [a]
                W.next_split()
                b, p = f_chunk("v", 2, xready)
                v = V.do(lambda: nc.vector.tensor_tensor(cv[:, k, :], ps[:, b, :], cS[:, k, :], ALU.mult),
                         a, p, prod_read[k])
                free[b] = [v]
                c = conv(cv[:, k, :], y[:, k, :], "sc_w_conv", 2 * m, 8, 3, None, v, prod_read[k])
                W.next_split()
                b, p = f_chunk("b", 2, xready)
                v = V.do(lambda: nc.vector.tensor_tensor(prod[:, k, :], ps[:, b, :], y[:, k, :], ALU.mult),
                         c, p, prod_read[k])
                free[b] = [v]
                h2, l2 = (t_[:, 2 * m:2 * m + 2, :].rearrange("p k s -> p (k s)") for t_ in (Mh, Ml))
                v = split_out(prod[:, k, :], h2, l2, None, v)
                prod_read[k] = v
                ready[2 * m] = ready[2 * m + 1] = v
                W.next_split()
            return t_proj("sc_out", 4, xt(Mh), xt(Ml), HALVES, acc, range(4), lambda kt: ready[kt])

        def moba(xready):
            area = Area(mix_base)
            qt, kt_, vt = (area.take([128, 2, D]) for _ in range(3))
            qT, kT = (area.take([128, 8, S]) for _ in range(2))
            tmp = [area.take([128, 16, 32]) for _ in range(2)]
            tf = None
            turned = []
            for part, (dst, bank0) in enumerate(((qt, 0), (kt_, 4), (vt, 0))):
                d = lambda t, j: ps[:, bank0 + 2 * t + j, :]
                p = t_proj("qkv", 4, xt(XTh), xt(XTl), HALVES, d, range(bank0, bank0 + 4), xready)
                for t in range(2):
                    if part == 2:
                        v = A.do(lambda: nc.scalar.copy(
                            vt[:, t, :], ps[:, 2 * t:2 * t + 2, :].rearrange("p a b -> p (a b)")), p)
                        free[2 * t] = free[2 * t + 1] = [v]
                        continue
                    src = ps[:, bank0 + 2 * t:bank0 + 2 * t + 2, :].rearrange(
                        "p a (h d) -> p (a h) d", d=64)
                    v = rope_half(src, dst[:, t, :].rearrange("p (h d) -> p h d", d=64), 16, 32, ROPE, t,
                                  [p, consts], tmp, tf)
                    tf = v
                    free[bank0 + 2 * t] = free[bank0 + 2 * t + 1] = [v]
                if part < 2:
                    turned.append((dst, v))
                else:
                    vready = v
            ready = [vready]
            for (src, v), dst in zip(turned, (qT, kT)):
                ready += turn_heads(lambda t, i: src[:, t, i * 128:(i + 1) * 128], 128, 8,
                                    lambda i: dst[:, i:i + 2, :].rearrange("p a b -> p (a b)"), [v], 2)

            def head(t_):
                return lambda h: t_[64 * (h % 2):64 * (h % 2) + 64, h // 2, :]

            outs = attention(list(range(16)), 64, 0.125, head(qT), head(kT),
                             lambda h, kt: vt[:, kt, h * 64:(h + 1) * 64], None,
                             xt(XTh), xt(XTl), area, ready)
            return t_proj("moba_out", 4, xt(XTh), xt(XTl), HALVES, acc, range(4), lambda kt: outs[kt])

        def log1pexp(x, area, n, *points):
            e, u, d, z, l = (area.take([128, n]) for _ in range(5))
            v = V.do(lambda: nc.vector.tensor_scalar(e[:], x, -1.0, None, ALU.mult), *points)
            v = V.do(lambda: nc.vector.tensor_tensor(e[:], e[:], x, ALU.min), v)
            a = A.do(lambda: nc.scalar.activation(e[:], e[:], ACT.Exp), v)
            v = V.do(lambda: nc.vector.tensor_scalar(u[:], e[:], 1.0, None, ALU.add), a)
            a = A.do(lambda: nc.scalar.activation(l[:], u[:], ACT.Ln), v)
            v = V.do(lambda: nc.vector.tensor_scalar(d[:], u[:], -1.0, None, ALU.add), v)
            v = V.do(lambda: nc.vector.tensor_scalar(z[:], d[:], 0.0, None, ALU.is_equal), v)
            v = V.do(lambda: nc.vector.tensor_tensor(d[:], d[:], z[:], ALU.add), v)
            v = V.do(lambda: nc.vector.reciprocal(d[:], d[:]), v)
            v = V.do(lambda: nc.vector.tensor_tensor(d[:], d[:], e[:], ALU.mult), v)
            v = V.do(lambda: nc.vector.tensor_tensor(l[:], l[:], z[:], ALU.add), a, v)
            v = V.do(lambda: nc.vector.tensor_tensor(l[:], l[:], d[:], ALU.mult), v)
            return l, v

        def even(xready, rp):
            area = Area(mix_base)
            Ph, Pl = area.take([128, 4, S], F32R), area.take([128, 4, S], F32R)
            xb = area.take([128, 12, S])
            xtok, xdt, zS = (area.take([128, 2, D]) for _ in range(3))
            xdec, prev = area.take([128, D]), area.take([128, D])
            Btok, CBm = area.take([128, 256]), area.take([128, 4, 128])
            gda, ex = area.take([128, 2, 4, 128]), area.take([128, 2, 4, 128])
            dtT = area.take([16, S])
            dt_, da, E1, D0 = (area.take([128, n]) for n in (32, 32, 16, 16))
            ah = area.take([128, 16])
            u0, u1, u2 = gda[:, 0, :, :], gda[:, 1, :, :], ex[:, 0, :, :]
            pwt = ex[:, 1, :, :]
            sem_p = [sem("s_pw"), 0]
            pwl = SP.dma(lambda: nc.sync.dma_start(pwt, pw), sem_p, xready(7))
            y = XN
            ready = {}
            last = None
            for m in range(2):
                b, p = f_chunk("pool", 2, xready)
                for blk in range(2):
                    g = 2 * m + blk
                    us, s0, s1 = (t_.rearrange("p a b -> p (a b)")[:, 0:S] for t_ in (u0, u1, u2))
                    a = A.do(lambda: nc.scalar.copy(us, ps[:, b, blk * S:(blk + 1) * S]), p, last)
                    v, src = a, us
                    bufs = [s0, s1]
                    for i in range(g + 1):
                        sh, dst = 1 << i, bufs[i % 2]
                        V.do(lambda src=src, dst=dst, sh=sh: nc.vector.tensor_copy(
                            dst[:, 0:sh], src[:, 0:sh]), v, last)
                        v = V.do(lambda src=src, dst=dst, sh=sh: nc.vector.tensor_tensor(
                            dst[:, sh:S], src[:, sh:S], src[:, 0:S - sh], ALU.add), v)
                        src = dst
                    cnt = cs[:, CST["cnt"] + 16 * g:CST["cnt"] + 16 * g + 16]
                    dst = bufs[(g + 1) % 2]
                    v = V.do(lambda: nc.vector.tensor_tensor(dst[:, 0:16], src[:, 0:16], cnt, ALU.mult), v)
                    V.do(lambda: nc.vector.tensor_tensor(dst[:, 0:16], dst[:, 0:16], us[:, 0:16],
                                                         ALU.subtract), v)
                    v = V.do(lambda: nc.vector.scalar_tensor_tensor(
                        out=dst[:, 16:S], in0=src[:, 16:S], scalar=1.0 / (2 << g), in1=us[:, 16:S],
                        op0=ALU.mult, op1=ALU.subtract))
                    if blk == 1:
                        free[b] = [a]
                    b2 = up_ring.take()
                    p2 = P.do(mm(ps[:, b2, 0:S], pwt[:, g, :], dst, True, True), v, pwl, free[b2])
                    last = split_out(ps[:, b2, 0:S], Ph[:, g, :], Pl[:, g, :], vcol("pool_scale_2", g), p2)
                    free[b2] = [last]
                    ready[g] = last
                W.next_split()
            for m in range(6):
                b, p = f_chunk("xbc", 2, xready)
                v = conv(ps[:, b, :], xb[:, 2 * m:2 * m + 2, :].rearrange("p a b -> p (a b)"), "conv_w_2",
                         2 * m, 12, 4, ("conv_b_2", 2 * m), p)
                free[b] = v
                xready2 = A.do(lambda: nc.scalar.activation(
                    xb[:, 2 * m:2 * m + 2, :], xb[:, 2 * m:2 * m + 2, :], ACT.Silu), v)
                W.next_split()
            b, p = f_chunk("dt", 1, xready)
            a = A.do(lambda: nc.scalar.copy(dtT[:], ps[0:16, b, 0:S]), p)
            free[b] = [a]
            W.next_split()
            b = up_ring.take()
            P.wait(a, free[b])
            P.quiet(lambda: nc.tensor.transpose(ps[:, b, 0:16], dtT[:, 0:128], ident[0:16, 0:16]))
            p = P.do(lambda: nc.tensor.transpose(ps[:, b, 16:32], dtT[:, 128:256], ident[0:16, 0:16]))
            two = lambda ap: ap.unsqueeze(1).to_broadcast([128, 2, 16])
            v3 = lambda t_: t_[:].rearrange("p (t e) -> p t e", t=2)
            v = V.do(lambda: nc.vector.tensor_tensor(v3(da), ps[:, b, 0:32].rearrange(
                "p (t e) -> p t e", t=2), two(sm[:, 0:16]), ALU.add), p, consts)
            free[b] = [v]
            l, v2 = log1pexp(da[:], area, 32, v)
            v = V.do(lambda: nc.vector.tensor_scalar(dt_[:], da[:], 0.0, None, ALU.max), v2)
            v = V.do(lambda: nc.vector.tensor_tensor(dt_[:], dt_[:], l[:], ALU.add), v)
            a = A.do(lambda: nc.scalar.activation(ah[:], sm[:, 16:32], ACT.Exp), consts)
            v = V.do(lambda: nc.vector.scalar_tensor_tensor(
                out=v3(da), in0=v3(dt_), scalar=-1.0, in1=two(ah[:]), op0=ALU.mult, op1=ALU.mult), v, a)
            dready = v
            p = t_proj("z", 4, xt(XTh), xt(XTl), HALVES, acc, range(4), xready)
            for t in range(2):
                zr = A.do(lambda: nc.scalar.activation(
                    zS[:, t, :], ps[:, 2 * t:2 * t + 2, :].rearrange("p a b -> p (a b)"), ACT.Silu), p)
                free[2 * t] = free[2 * t + 1] = [zr]
            xr = []
            bc = lambda ap, n=64: ap.unsqueeze(2).to_broadcast([128, ap.shape[1], n])
            by = lambda ap: ap.rearrange("p (e d) -> p e d", d=64)
            for t in range(2):
                for j in range(2):
                    b = all_ring.take()
                    P.wait(free[b], xready2)
                    for i in range(4):
                        p = P.do(lambda i=i: nc.tensor.transpose(
                            ps[:, b, i * 128:(i + 1) * 128], xb[:, 4 * j + i, t * 128:(t + 1) * 128], ident))
                    a = A.do(lambda: nc.scalar.copy(xtok[:, t, j * 512:(j + 1) * 512], ps[:, b, :]), p)
                    free[b] = [a]
                xr.append(V.do(lambda: nc.vector.tensor_tensor(
                    by(xdt[:, t, :]), by(xtok[:, t, :]), bc(dt_[:, 16 * t:16 * t + 16]), ALU.mult), a, dready))
            b = all_ring.take()
            P.wait(free[b])
            for g in range(2):
                p = P.do(lambda: nc.tensor.transpose(ps[:, b, g * 128:(g + 1) * 128], xb[:, 8 + g, 0:128],
                                                     ident))
            bt = A.do(lambda: nc.scalar.copy(Btok[:], ps[:, b, 0:256]), p)
            free[b] = [bt]
            b = all_ring.take()
            P.wait(free[b])
            for c in range(2):
                for g in range(2):
                    i, sl = 2 * c + g, slice(c * 128, (c + 1) * 128)
                    p = P.do(mm(ps[:, b, i * 128:(i + 1) * 128], xb[:, 8 + g, sl], xb[:, 10 + g, sl], True,
                                True))
            cb = V.do(lambda: nc.vector.tensor_tensor(
                CBm[:], ps[:, b, :].rearrange("p (i l) -> p i l", i=4),
                U.unsqueeze(1).to_broadcast([128, 4, 128]), ALU.mult), p)
            free[b] = [cb]
            b = all_ring.take()
            P.wait(free[b], dready)
            P.quiet(mm(ps[:, b, 0:16], GT, da[:, 0:16], True, True))
            p = P.do(mm(ps[:, b, 16:32], U, da[:, 16:32], True, True))
            A.do(lambda: nc.scalar.activation(D0[:], ps[:, b, 0:16], ACT.Exp), p)
            a = A.do(lambda: nc.scalar.activation(E1[:], ps[:, b, 16:32], ACT.Exp))
            free[b] = [a]
            xd = V.do(lambda: nc.vector.tensor_tensor(by(xdec[:]), by(xdt[:, 0, :]), bc(D0[:]), ALU.mult),
                      a, xr[0])
            for g in range(2):
                b = all_ring.take()
                p = P.do(mm(ps[:, b, :], Btok[:, g * 128:(g + 1) * 128], xdec[:, g * 512:(g + 1) * 512],
                            True, True), xd, bt, free[b])
                pv = A.do(lambda: nc.scalar.copy(prev[:, g * 512:(g + 1) * 512], ps[:, b, :]), p)
                free[b] = [pv]
            n, ys = 0, [[], []]
            gread, eread = [last, last], [last, last]
            for c in range(2):
                for g in range(2):
                    yb = all_ring.take()
                    P.wait(free[yb])
                    for q in range(2):
                        k, e0 = n % 2, 8 * g + 4 * q
                        n += 1
                        v = V.do(lambda: nc.vector.tensor_tensor(
                            gda[:, k], GT.unsqueeze(1).to_broadcast([128, 4, 128]),
                            bc(da[:, 16 * c + e0:16 * c + e0 + 4], 128), ALU.mult), dready, gread[k])
                        b = all_ring.take()
                        if b == yb:
                            b = all_ring.take()
                        P.wait(v, free[b])
                        for i in range(4):
                            p = P.do(mm(ps[:, b, i * 128:(i + 1) * 128], gda[:, k, i, :], U, True, True))
                        gread[k] = p
                        a = A.do(lambda: nc.scalar.activation(
                            ex[:, k], ps[:, b, :].rearrange("p (i l) -> p i l", i=4), ACT.Exp), p, eread[k])
                        free[b] = [a]
                        v = V.do(lambda: nc.vector.tensor_tensor(
                            ex[:, k], ex[:, k], CBm[:, 2 * c + g, :].unsqueeze(1).to_broadcast(
                                [128, 4, 128]), ALU.mult), a, cb)
                        P.wait(v, xr[c])
                        for i in range(4):
                            e = 4 * q + i
                            p = P.do(mm(ps[:, yb, e * 64:(e + 1) * 64], ex[:, k, i, :],
                                        xdt[:, c, (8 * g + e) * 64:(8 * g + e + 1) * 64], True, True))
                        eread[k] = p
                    yc = y[:, c, g * 512:(g + 1) * 512]
                    xc = xtok[:, c, g * 512:(g + 1) * 512]
                    v = V.do(lambda: nc.vector.tensor_tensor(
                        by(xc), by(xc), bc(sm[:, 32 + 8 * g:32 + 8 * g + 8]), ALU.mult), xr[c])
                    v = V.do(lambda: nc.vector.tensor_tensor(yc, ps[:, yb, :], xc, ALU.add), v, p)
                    free[yb] = [v]
                    if c == 1:
                        b = all_ring.take()
                        p = P.do(mm(ps[:, b, :], xb[:, 10 + g, 128:256], prev[:, g * 512:(g + 1) * 512],
                                    True, True), pv, free[b])
                        v2 = V.do(lambda: nc.vector.tensor_tensor(
                            by(xc), by(ps[:, b, :]), bc(E1[:, 8 * g:8 * g + 8]), ALU.mult), p, v)
                        free[b] = [v2]
                        v = V.do(lambda: nc.vector.tensor_tensor(yc, yc, xc, ALU.add), v2)
                    v = V.do(lambda: nc.vector.tensor_tensor(yc, yc, zS[:, c, g * 512:(g + 1) * 512],
                                                             ALU.mult), v, zr)
                    ys[c] = v
            done = rms(lambda t: y[:, t, :], lambda t: xtok[:, t, :], D, 0, ys)
            r = to_feature(lambda t, kt: xtok[:, t, kt * 128:(kt + 1) * 128], 8, xt(XTh), xt(XTl),
                           lambda kt: vcol("ssm_norm_w_2", kt), done)
            for kt in range(8):
                ready[4 + kt] = r[kt]
            hi = lambda kt: Ph[:, kt, :] if kt < 4 else XTh[:, kt - 4, :]
            lo = lambda kt: Pl[:, kt, :] if kt < 4 else XTl[:, kt - 4, :]
            return t_proj("even_out", 6, hi, lo, HALVES, acc, range(4), lambda kt: ready[kt])

        def odd(xready):
            area = Area(mix_base)
            qf, kf = area.take([128, 4, S]), area.take([128, 4, S])
            vf = area.take([128, 2, 512])
            cq, ckv = area.take([128, 2, 512]), area.take([128, 2, 256])
            CQh, CQl = area.take([128, 4, S], F32R), area.take([128, 4, S], F32R)
            CKh, CKl = area.take([128, 2, S], F32R), area.take([128, 2, S], F32R)
            FL, FR = area.take([104, 4, S]), area.take([104, 4, S])
            fk = area.take([40, S])
            krt, lf = area.take([128, 2, 32]), area.take([128, 16])
            sem_o = [sem("s_oh"), 0]
            ohl = None
            for i, t_ in enumerate((FL, FR)):
                ohl = SP.dma(lambda i=i, t_=t_: nc.sync.dma_start(
                    t_[:].rearrange("p h s -> p (h s)"), onehot[i]), sem_o, xready(7))
            b, p = f_chunk("flkr", 1, xready)
            a = A.do(lambda: nc.scalar.copy(fk[:], ps[0:40, b, 0:S]), p)
            free[b] = [a]
            W.next_split()
            b = up_ring.take()
            P.wait(a, free[b])
            for t in range(2):
                p = P.do(lambda: nc.tensor.transpose(ps[:, b, t * 40:t * 40 + 40],
                                                     fk[:, t * 128:(t + 1) * 128], ident[0:40, 0:40]))
            v80 = ps[:, b, 0:80].rearrange("p (t c) -> p t c", t=2)
            lf3 = lf[:].rearrange("p (t c) -> p t c", t=2)
            V.do(lambda: nc.vector.tensor_copy(krt[:], v80[:, :, 8:40]), p)
            v = V.do(lambda: nc.vector.tensor_tensor(
                lf3, v80[:, :, 0:8], sm[:, 48:56].unsqueeze(1).to_broadcast([128, 2, 8]), ALU.add), p)
            free[b] = [v]
            l, v2 = log1pexp(lf[:], area, 16, v)
            v = V.do(lambda: nc.vector.tensor_scalar(lf[:], lf[:], 0.0, None, ALU.min), v2)
            v = V.do(lambda: nc.vector.tensor_tensor(lf[:], lf[:], l[:], ALU.subtract), v)
            b = up_ring.take()
            P.wait(v, free[b])
            P.quiet(mm(ps[0:8, b, 0:S], lf[:, 0:8], UO, True, False))
            p = P.do(mm(ps[0:8, b, 128:S], lf[:, 8:16], U, False, True))
            br = ps[0:8, b, 0:S].unsqueeze(1).to_broadcast([8, 4, S])
            for r in (0, 64):
                V.do(lambda: nc.vector.tensor_scalar(FL[r + 32:r + 40, :, :], br, 8.0, None, ALU.mult), p,
                     ohl)
                fready = V.do(lambda: nc.vector.tensor_scalar(FR[r:r + 8, :, :], br, -8.0, None,
                                                              ALU.mult), p)
            free[b] = [fready]
            for tag, dst in (("qf", qf), ("kf", kf)):
                for m in range(2):
                    b, p = f_chunk(tag, 2, xready)
                    qk = A.do(lambda: nc.scalar.copy(
                        dst[:, 2 * m:2 * m + 2, :].rearrange("p a b -> p (a b)"), ps[:, b, :]), p)
                    free[b] = [qk]
                    W.next_split()
            p = t_proj("vf", 2, xt(XTh), xt(XTl), [(0, 512)], lambda t, j: ps[:, t, :], (0, 1), xready,
                       per=4)
            for t in range(2):
                vr = A.do(lambda: nc.scalar.copy(vf[:, t, :], ps[:, t, :]), p)
                free[t] = [vr]
            p = t_proj("cq", 2, xt(XTh), xt(XTl), [(0, 512)], lambda t, j: ps[:, 2 + t, :], (2, 3), xready,
                       per=4)
            d1 = rms(lambda t: ps[:, 2 + t, :], lambda t: cq[:, t, :], 512, 8, [p, p])
            free[2] = free[3] = [d1[1]]
            p = t_proj("ckv", 1, xt(XTh), xt(XTl), [(0, 256)], lambda t, j: ps[:, t, 0:256], (0, 1), xready,
                       per=8)
            d2 = rms(lambda t: ps[:, t, 0:256], lambda t: ckv[:, t, :], 256, 10, [p, p])
            free[0] = free[1] = [d2[1]]
            r1 = to_feature(lambda t, kt: cq[:, t, kt * 128:(kt + 1) * 128], 4, xt(CQh), xt(CQl),
                            lambda kt: vcol("q_norm_w_2", kt), d1)
            r2 = to_feature(lambda t, kt: ckv[:, t, kt * 128:(kt + 1) * 128], 2, xt(CKh), xt(CKl),
                            lambda kt: vcol("kv_norm_w_2", kt), d2)
            head = lambda t_: (lambda h: t_[64 * (h % 2):64 * (h % 2) + 64, h // 2, :])
            attn_base = area.at
            outs = attention(list(range(8)), 64, 0.125, head(qf), head(kf),
                             lambda h, kt: vf[:, kt, h * 64:(h + 1) * 64],
                             lambda h: tuple(t_[64 * (h % 2):64 * (h % 2) + 40, h // 2, :]
                                             for t_ in (FL, FR)),
                             xt(XTh), xt(XTl), area, [qk, vr, fready])
            area2 = Area(mix_base)
            qm, km = area2.take([128, 2, 768]), area2.take([128, 2, 768])
            area2 = Area(area.at)
            vm = area2.take([128, 2, 512])
            tmp = [area2.take([128, 8, 16]) for _ in range(2)]
            kr2 = area2.take([128, 2, 32])
            p = t_proj("uq", 2, xt(CQh), xt(CQl), [(0, 384), (384, 768)],
                       lambda t, j: ps[:, 2 * t + j, 0:384], range(4), lambda kt: r1[kt])
            tf = None
            for t in range(2):
                qh = qm[:, t, :].rearrange("p (h d) -> p h d", d=96)
                sv = ps[:, 2 * t:2 * t + 2, 0:384].rearrange("p a (h d) -> p a h d", d=96)
                qa = A.do(lambda: nc.scalar.copy(
                    qm[:, t, :].rearrange("p (a h d) -> p a h d", a=2, d=96)[:, :, :, 0:64],
                    sv[:, :, :, 0:64]), p, outs[3])
                for a_ in range(2):
                    tf = rope_half(sv[:, a_, :, 64:96], qh[:, 4 * a_:4 * a_ + 4, 64:96], 4, 16, ROPE2, t,
                                   [qa, outs[3]], tmp, tf)
                free[2 * t] = free[2 * t + 1] = [qa, tf]
            qready = [qa, tf]
            p = t_proj("ukv", 1, xt(CKh), xt(CKl), HALVES, acc, range(4), lambda kt: r2[kt])
            for t in range(2):
                tf = rope_half(krt[:, t:t + 1, :], kr2[:, t:t + 1, :], 1, 16, ROPE2, t, [], tmp, tf)
                kh = km[:, t, :].rearrange("p (h d) -> p h d", d=96)
                sv = ps[:, 2 * t:2 * t + 2, :].rearrange("p a (h c d) -> p (a h) c d", c=2, d=64)
                ka = A.do(lambda: nc.scalar.copy(kh[:, :, 0:64], sv[:, :, 0, :]), p, outs[3])
                va = A.do(lambda: nc.scalar.copy(vm[:, t, :].rearrange("p (h d) -> p h d", d=64),
                                                 sv[:, :, 1, :]))
                kv_ = V.do(lambda: nc.vector.tensor_copy(
                    kh[:, :, 64:96], kr2[:, t, :].unsqueeze(1).to_broadcast([128, 8, 32])), tf, outs[3])
                free[2 * t] = free[2 * t + 1] = [va]
            kready = [ka, kv_]
            area3 = Area(area2.at)
            area4 = Area(mix_base + 2 * 6144)
            qmT, kmT = area4.take([96, 8, S]), area4.take([96, 8, S])
            assert area4.at <= attn_base
            tr = []
            for src, dst, rd in ((qm, qmT, qready), (km, kmT, kready)):
                tr += turn_heads(lambda t, i: src[:, t, i * 96:(i + 1) * 96], 96, 8,
                                 lambda i: dst[:, i:i + 2, :].rearrange("p a b -> p (a b)"), rd, 2)
            outs2 = attention(list(range(8)), 96, float(96) ** -0.5, lambda h: qmT[:, h, :],
                              lambda h: kmT[:, h, :], lambda h, kt: vm[:, kt, h * 64:(h + 1) * 64], None,
                              lambda kt: XTh[:, 4 + kt, :], lambda kt: XTl[:, 4 + kt, :], area3, tr + [va])
            for kt in range(4):
                outs[4 + kt] = outs2[kt]
            return t_proj("odd_out", 4, xt(XTh), xt(XTl), HALVES, acc, range(4), lambda kt: outs[kt])

        V.wait(x_loaded)
        A.wait(x_loaded)
        rp = load_rows(0)
        xr = prenorm("mix_norm", 0, [x_loaded, x_loaded])
        xs = residual(short_conv(xr))
        xs = residual(ffn(0, True, prenorm("ffn_norm", 0, xs)))
        xs = residual(moba(prenorm("mix_norm", 1, xs)))
        xs = residual(ffn(1, True, prenorm("ffn_norm", 1, xs)))
        done = rms(lambda t: X[:, t, :], lambda t: XN[:, t, :], D, 0, xs)
        for t in range(2):
            done[t] = V.do(lambda: nc.vector.tensor_tensor(X[:, t, :], XN[:, t, :], grow[:], ALU.mult),
                           done[t], rp)
        rp = load_rows(1, 2, done)
        xs = postnorm(even(x_to_feature(done), None), rp)
        rp = load_rows(3, 4, xs)
        xs = postnorm(ffn(0, False, x_to_feature(xs)), rp)
        rp = load_rows(5, 6, xs)
        xs = postnorm(odd(x_to_feature(xs)), rp)
        rp = load_rows(7, 8, xs)
        xs = postnorm(ffn(1, False, x_to_feature(xs)), rp)
        sem_out = [sem("s_out"), 0]
        for t in range(2):
            stored = SP.dma(lambda t=t: nc.sync.dma_start(out[0, t * 128:(t + 1) * 128, :], X[:, t, :]),
                            sem_out, xs[t])
        SP.wait(stored)
        assert W.i == len(plan)


def layout(i):
    plan = weight_plan()
    wts = np.zeros((len(plan), 128, CW), np.float32)
    for n, (_, _, name, layer, cols, width, nk, k0) in enumerate(plan):
        w = i[name][layer]
        dst = wts[n, :, 0:width * nk].reshape(128, nk, width)
        at = 0
        for c0, m in cols:
            blk = w[k0 * 128:(k0 + nk) * 128, c0:c0 + m]
            dst[:, :, at:at + m] = blk.reshape(nk, 128, m).transpose(1, 0, 2)
            at += m
    vec = np.zeros((128, NVEC), np.float32)
    for name, c in VEC.items():
        a = i[name].reshape(-1, 128)
        vec[:, c:c + a.shape[0]] = a.T
    rows = np.stack([i["final_norm"], i["ln_mix_g_2"][0], i["ln_mix_b_2"][0], i["ln_ffn_g_2"][0],
                     i["ln_ffn_b_2"][0], i["ln_mix_g_2"][1], i["ln_mix_b_2"][1], i["ln_ffn_g_2"][1],
                     i["ln_ffn_b_2"][1]])
    small = np.concatenate([i["dt_bias_2"][0], i["a_log_2"][0], i["d_skip_2"][0], i["fgate_b_2"][0]])
    pw = np.ascontiguousarray(i["pool_w_2"][0].transpose(1, 0, 2))
    cst, oh = constants()
    return dict(wts=wts, vec=vec, cst=cst, onehot=oh, rows=rows, small=small, pw=pw,
                x_in=np.ascontiguousarray(i["x"]))


def kernel(**inputs):
    import concourse.bacc as _bacc
    from concourse.bass_utils import run_bass_kernel_spmd as _run

    nc = _bacc.Bacc("TRN2", target_bir_lowering=False, num_devices=1)
    arrays = layout({k: np.asarray(v) for k, v in inputs.items()})
    args = {k: nc.dram_tensor("in_" + k, a.shape, mybir.dt.from_np(a.dtype), kind="ExternalInput").ap()
            for k, a in arrays.items()}
    out = nc.dram_tensor("out_0", (1, S, D), F32, kind="ExternalOutput").ap()
    build(nc, out=out, **args)
    r = _run(nc, [{"in_" + k: a for k, a in arrays.items()}], core_ids=[0])
    return r.results[0]["out_0"]
```

```python
from contextlib import ExitStack

import numpy as np

import concourse.bass as bass
from concourse import mybir

F32 = mybir.dt.float32
F32R = mybir.dt.float32r
ACT = mybir.ActivationFunctionType
ALU = mybir.AluOpType
AX_X = mybir.AxisListType.X

D, S, FF = 1024, 256, 2816
CW = 2048
NRAW, NHI, NLO = 4, 5, 4
NEG = -1.0e30
ALPHA = float((2 * 2) ** 0.25)
RMS_EPS, LN_EPS = 1e-6, 1e-5
RATE_MOBA_V, RATE_MOBA_O, RATE_EVEN, RATE_ODD, RATE_ODD_OUT = 1.6, 2.0, 1.8, 1.5, 3.0



def weight_plan():
    plan = []

    def f(tag, name, layer, c0, n=256, pad=None):
        plan.append((tag, "F", name, layer, [(c0, n)], pad or n, 8, 0))

    def t(tag, name, layer, c0, n, kts, per):
        for k in range(0, kts, per):
            plan.append((tag, "T", name, layer, [(c0, n)], n, per, k))

    def ffn(up_g, up_u, g0, u0, down, layer):
        for m in range(11):
            f("g", up_g, layer, g0 + 256 * m)
            f("u", up_u, layer, u0 + 256 * m)
        t("down", down, layer, 0, 1024, 22, 2)

    for m in range(4):
        f("c", "sc_w_in", 0, 1024 + 256 * m)
        f("v", "sc_w_in", 0, 2048 + 256 * m)
        f("b", "sc_w_in", 0, 256 * m)
    t("sc_out", "sc_w_out", 0, 0, 1024, 8, 2)
    ffn("ffn_w_up", "ffn_w_up", 0, FF, "ffn_w_down", 0)
    for part in range(3):
        t("qkv", "moba_w_qkv", 0, 1024 * part, 1024, 8, 2)
    t("moba_out", "moba_w_o", 0, 0, 1024, 8, 2)
    ffn("ffn_w_up", "ffn_w_up", 0, FF, "ffn_w_down", 1)

    f("dt", "even_w_in_2", 0, 3072, 16, 128)
    for m in range(6):
        f("xbc", "even_w_in_2", 0, 1536 + 256 * m)
    for m in range(2):
        f("pool", "even_w_in_2", 0, 256 * m)
    t("z", "even_w_in_2", 0, 512, 1024, 8, 2)
    t("even_out", "even_w_out_2", 0, 0, 1024, 12, 2)
    ffn("ffn_w_gate_2", "ffn_w_up_2", 0, 0, "ffn_w_down_2", 0)
    plan.append(("flkr", "F", "odd_w_in_2", 0, [(1536, 8), (2312, 32)], 128, 8, 0))
    for m in range(2):
        f("qf", "odd_w_in_2", 0, 256 * m)
    for m in range(2):
        f("kf", "odd_w_in_2", 0, 512 + 256 * m)
    t("ckv", "odd_w_in_2", 0, 2056, 256, 8, 8)
    t("cq", "odd_w_in_2", 0, 1544, 512, 8, 4)
    t("vf", "odd_w_in_2", 0, 1024, 512, 8, 4)
    t("ukv", "w_ukv_2", 0, 0, 1024, 2, 2)
    t("uq", "w_uq_2", 0, 0, 768, 4, 2)
    t("odd_out", "odd_w_out_2", 0, 0, 1024, 8, 2)
    ffn("ffn_w_gate_2", "ffn_w_up_2", 0, 0, "ffn_w_down_2", 1)
    return plan


VEC = {}
_n = 0
for _name, _cols in (("sc_w_conv", 24), ("ffn_w_conv", 264),
                     ("pool_scale_2", 4), ("conv_w_2", 48), ("conv_b_2", 12), ("ssm_norm_w_2", 8),
                     ("q_norm_w_2", 4), ("kv_norm_w_2", 2)):
    VEC[_name] = _n
    _n += _cols
NVEC = _n

CST = {}
_n = 0
for _name, _cols in (("ident", 128), ("uo", 256), ("gt", 128), ("mask", 256), ("rope", 128),
                     ("rope2", 64), ("cnt", 64)):
    CST[_name] = _n
    _n += _cols
NCST = _n


def constants():
    c = np.zeros((128, NCST), np.float32)
    i = np.arange(128)
    c[:, CST["ident"]:CST["ident"] + 128] = np.eye(128, dtype=np.float32)
    c[:, CST["uo"]:CST["uo"] + 128] = (i[:, None] <= i[None, :])
    c[:, CST["uo"] + 128:CST["uo"] + 256] = 1.0
    c[:, CST["gt"]:CST["gt"] + 128] = (i[:, None] > i[None, :])
    m = np.where(i[None, :] > i[:, None], np.float32(NEG), np.float32(0))
    c[:, CST["mask"]:CST["mask"] + 256] = np.concatenate([m, m], 1)
    for name, half in (("rope", 32), ("rope2", 16)):
        inv = np.power(np.float32(10000.0), -np.arange(half, dtype=np.float32) / np.float32(half),
                       dtype=np.float32)
        ang = np.arange(S, dtype=np.float32)[:, None] * inv[None, :]
        t = np.stack([np.cos(ang).reshape(2, 128, half), np.sin(ang).reshape(2, 128, half)], 1)
        c[:, CST[name]:CST[name] + 4 * half] = t.transpose(2, 0, 1, 3).reshape(128, 4 * half)
    for g in range(4):
        w = 2 << g
        c[:, CST["cnt"] + 16 * g:CST["cnt"] + 16 * g + 16] = (
            np.float32(1.0) / np.minimum(np.arange(16) + 1, w).astype(np.float32))
    return c




class Engine:

    def __init__(self, eng, sem):
        self.eng, self.sem, self.n, self.waited = eng, sem, 0, {}

    def wait(self, *points):
        for p in points:
            if isinstance(p, list):
                self.wait(*p)
            elif p is not None and self.waited.get(p[0].name, 0) < p[1]:
                self.waited[p[0].name] = p[1]
                self.eng.wait_ge(p[0], p[1])

    def do(self, fn, *points):
        self.wait(*points)
        self.n += 1
        fn().then_inc(self.sem, 1)
        return (self.sem, self.n)

    def quiet(self, fn, *points):
        self.wait(*points)
        fn()

    def dma(self, fn, sem, *points):
        self.wait(*points)
        fn().then_inc(sem[0], 16)
        sem[1] += 16
        return (sem[0], sem[1])


def build(nc, wts, vec, cst, rows, small, pw, x_in, out):
    plan = weight_plan()
    with ExitStack() as ctx:
        sem = lambda name: ctx.enter_context(nc.semaphore(name))
        base = (nc.sbuf_base + 63) // 64 * 64
        limit = nc.sbuf_usable_end

        P, A, V, G, SP = (Engine(e, sem(n)) for e, n in (
            (nc.tensor, "s_pe"), (nc.scalar, "s_act"), (nc.vector, "s_dve"), (nc.gpsimd, "s_pool"),
            (nc.sync, "s_sp")))
        names = [0]

        class Area:

            def __init__(self, start):
                self.at = start

            def take(self, shape, dt=F32):
                n = 4
                for d in shape[1:]:
                    n *= d
                names[0] += 1
                t = nc.alloc_sbuf_tensor_at(f"t{names[0]}", shape, dt, offset=self.at)
                self.at += (n + 31) // 32 * 32
                assert self.at <= limit, (self.at, limit)
                return t

        fixed = Area(base)
        wraw = fixed.take([128, NRAW, CW])
        wh = fixed.take([128, NHI, CW], F32R)
        wl = fixed.take([128, NLO, CW], F32R)
        X = fixed.take([128, 2, D])
        XN = fixed.take([128, 2, D])
        xt_at = [fixed.at, fixed.at + 8192]
        XTh = fixed.take([128, 8, S], F32R)
        XTl = fixed.take([128, 8, S], F32R)
        vecs = fixed.take([128, NVEC])
        cs = fixed.take([128, NCST])
        sm = fixed.take([128, 56])
        grow = fixed.take([128, 1024])
        brow = fixed.take([128, 1024])
        st = fixed.take([128, 64])
        mhalf = fixed.take([128, 2])
        mix_base = fixed.at

        ps = ctx.enter_context(nc.psum_tensor("ps", [128, 8, 512], F32))
        free = [[] for _ in range(8)]

        class Ring:
            def __init__(self, banks):
                self.banks, self.i = banks, 0

            def take(self):
                b = self.banks[self.i % len(self.banks)]
                self.i += 1
                return b

        f_ring = Ring([4, 5, 6, 7])
        bg_ring = Ring([6, 7])

        ident = cs[:, CST["ident"]:CST["ident"] + 128]
        UO = cs[:, CST["uo"]:CST["uo"] + 256]
        U = cs[:, CST["uo"]:CST["uo"] + 128]
        GT = cs[:, CST["gt"]:CST["gt"] + 128]
        MASK = cs[:, CST["mask"]:CST["mask"] + 256]
        ROPE = cs[:, CST["rope"]:CST["rope"] + 128].rearrange("p (t c d) -> p t c d", t=2, c=2)
        ROPE2 = cs[:, CST["rope2"]:CST["rope2"] + 64].rearrange("p (t c d) -> p t c d", t=2, c=2)

        def vcol(name, i, j=0):
            return vecs[:, VEC[name] + i + j:VEC[name] + i + j + 1]

        sem_in = [sem("s_in"), 0]
        sem_x = [sem("s_x"), 0]
        x_loaded = [A.dma(lambda t=t: nc.scalar.dma_start(X[:, t, :], x_in[0, t * 128:(t + 1) * 128, :]),
                          sem_x) for t in range(2)][-1]
        A.dma(lambda: nc.scalar.dma_start(vecs[:], vec), sem_in)
        A.dma(lambda: nc.scalar.dma_start(cs[:], cst), sem_in)
        consts = A.dma(lambda: nc.scalar.dma_start(sm[:], small.partition_broadcast(128)), sem_in)
        half = V.do(lambda: nc.vector.memset(mhalf[:], -0.5))
        sem_row = [sem("s_row"), 0]

        class Weights:
            def __init__(self):
                self.sems = [[sem(f"s_w{i}"), 0] for i in range(NRAW)]
                self.raw, self.hi, self.lo, self.used = [], [], [], []
                for i in range(NRAW):
                    self.load(i)
                for i in range(NLO):
                    self.split_hi(i)
                    self.split_lo(i)
                for i in range(NLO, NHI):
                    self.split_hi(i)
                self.i, self.pumped = 0, 0

            def width(self, i):
                return plan[i][5] * plan[i][6]

            def load(self, i):
                if i >= len(plan):
                    return
                w, k = self.width(i), i % NRAW
                old = [self.hi[i - NRAW], self.lo[i - NRAW]] if i >= NRAW else []
                self.raw.append(SP.dma(lambda: nc.sync.dma_start(wraw[:, k, 0:w], wts[i, :, 0:w]),
                                       self.sems[k], *old))

            def split_hi(self, i):
                if i >= len(plan):
                    return
                w, r, k = self.width(i), i % NRAW, i % NHI
                old = self.used[i - NHI] if i >= NHI else None
                self.hi.append(A.do(lambda: nc.scalar.copy(wh[:, k, 0:w], wraw[:, r, 0:w]),
                                    self.raw[i], old))

            def split_lo(self, i):
                if i >= len(plan):
                    return
                w, r, h, k = self.width(i), i % NRAW, i % NHI, i % NLO
                old = self.used[i - NLO] if i >= NLO else None
                self.lo.append(V.do(lambda: nc.vector.tensor_tensor(
                    wl[:, k, 0:w], wraw[:, r, 0:w], wh[:, h, 0:w].bitcast(F32), ALU.subtract),
                    self.hi[i], old))
                self.load(i + NRAW)

            def use(self, tag):
                i = self.i
                assert plan[i][0] == tag, (plan[i][0], tag)
                n, kk = plan[i][5], plan[i][6]
                view = lambda t, m: t[:, i % m, 0:n * kk].rearrange("p (k n) -> p k n", k=kk)
                self.i += 1
                return view(wh, NHI), view(wl, NLO), self.lo[i]

            def done(self, point, n=1):
                self.used += [point] * n

            def pump(self):
                if self.pumped < len(self.used):
                    self.split_hi(self.pumped + NHI)
                    self.split_lo(self.pumped + NLO)
                    self.pumped += 1

        W = Weights()

        def mm(o, a, b, start, stop):
            return lambda: nc.tensor.matmul(o, a, b, start=start, stop=stop)

        class Background:
            def __init__(self):
                self.tasks, self.rate, self.due = [], 0.0, 0.0

            def step(self):
                while self.tasks:
                    try:
                        return not next(self.tasks[0])
                    except StopIteration:
                        self.tasks.pop(0)
                return False

            def tick(self):
                self.due += self.rate
                while self.due >= 1:
                    self.due -= 1
                    if not self.step():
                        self.due = 0

            def until(self, cond):
                while not cond():
                    assert self.step()

            def finish(self):
                while self.step():
                    pass
                self.rate = self.due = 0.0

        bg = Background()

        def f_chunk(tag, nblk, xready):
            H, L, ready = W.use(tag)
            b = f_ring.take()
            P.wait(ready, free[b])
            for blk in range(nblk):
                o = ps[:, b, blk * S:(blk + 1) * S]
                c = slice(blk * 128, (blk + 1) * 128)
                for kt in range(8):
                    P.quiet(mm(o, H[:, kt, c], XTh[:, kt, :], kt == 0, False), xready(kt))
                    P.quiet(mm(o, H[:, kt, c], XTl[:, kt, :], False, False))
                    m = mm(o, L[:, kt, c], XTh[:, kt, :], False, kt == 7)
                    if kt == 7 and blk == nblk - 1:
                        point = P.do(m)
                    else:
                        P.quiet(m)
                if blk < nblk - 1:
                    bg.tick()
            W.done(point)
            return b, point

        HALVES = [(0, 512), (512, 1024)]

        def t_part(parts, hi, lo, t, js, dst, bank, xready):
            tt = slice(t * 128, (t + 1) * 128)
            for H, L, k, kt, cols, first, last in parts:
                P.wait(xready(kt))
                for n, (a, w) in enumerate(((hi, H), (hi, L), (lo, H))):
                    for j in js:
                        if first and n == 0:
                            P.wait(free[bank(t, j)])
                        m = mm(dst(t, j), a(kt)[:, tt], w[:, k, cols[j][0]:cols[j][1]], first and n == 0,
                               last and n == 2)
                        if n == 2 and j == js[-1]:
                            point = P.do(m)
                        else:
                            P.quiet(m)
            return point

        def t_proj(tag, nchunks, hi, lo, cols, dst, bank, xready, per=2, split_end=False):
            js = list(range(len(cols)))
            body = nchunks - 2 if split_end else nchunks
            for i in range(body):
                H, L, ready = W.use(tag)
                P.wait(ready)
                for k in range(per):
                    kt = i * per + k
                    for t in range(2):
                        point = t_part([(H, L, k, kt, cols, kt == 0, kt == nchunks * per - 1)], hi, lo, t,
                                       js, dst, bank, xready)
                    if k < per - 1:
                        bg.tick()
                W.done(point)
                W.pump()
                bg.tick()
            if not split_end:
                return {(t, j): point for t in range(2) for j in js}
            parts = []
            for i in range(body, nchunks):
                H, L, ready = W.use(tag)
                parts += [(H, L, k, i * per + k, cols, i * per + k == 0, i * per + k == nchunks * per - 1)
                          for k in range(per)]
            P.wait(ready)
            points = {}
            for t in range(2):
                for j in js:
                    points[t, j] = t_part(parts, hi, lo, t, [j], dst, bank, xready)
            W.done(points[1, js[-1]], 2)
            return points

        def acc(t, j):
            return ps[:, 2 * t + j, :]

        def acc_bank(t, j):
            return 2 * t + j

        def split_out(src, hi, lo, scale, *points):
            return split_bank([(src, hi, lo, scale)], *points)[0]

        def split_bank(parts, *points):
            for src, hi, lo, scale in parts:
                if scale is None:
                    a = A.do(lambda: nc.scalar.copy(hi, src), *points)
                else:
                    a = A.do(lambda: nc.scalar.activation(hi, src, ACT.Copy, scale=scale), *points)
            done = []
            for src, hi, lo, scale in parts:
                if scale is None:
                    done.append(V.do(lambda: nc.vector.tensor_tensor(
                        lo, src, hi.bitcast(F32), ALU.subtract), a, *points))
                else:
                    done.append(V.do(lambda: nc.vector.scalar_tensor_tensor(
                        out=lo, in0=src, scalar=scale, in1=hi.bitcast(F32), op0=ALU.mult,
                        op1=ALU.subtract), a, *points))
            return done

        def to_feature(src, nkt, hi, lo, scale, ready):
            points = []
            for k0 in range(0, nkt, 2):
                b = bg_ring.take()
                P.wait(free[b])
                for kt in (k0, k0 + 1):
                    for t in range(2):
                        o = ps[:, b, (kt - k0) * S + t * 128:(kt - k0) * S + (t + 1) * 128]
                        fn = lambda: nc.tensor.transpose(o, src(t, kt), ident)
                        if kt == k0 + 1 and t == 1:
                            p = P.do(fn, ready[t], consts)
                        else:
                            P.quiet(fn, ready[t], consts)
                points += split_bank(
                    [(ps[:, b, (kt - k0) * S:(kt - k0 + 1) * S], hi(kt), lo(kt), scale(kt))
                     for kt in (k0, k0 + 1)], p)
                free[b] = [points[-1]]
                yield
            return points

        def xt(t_):
            return lambda kt: t_[:, kt, :]

        def fill(parts, *points):
            done = []
            for dst, value in parts:
                done.append(G.do(lambda: nc.gpsimd.memset(dst, value), *points, *done[-1:]))
            return done

        def pow_rms(c, *points):
            return G.do(lambda: nc.gpsimd.tensor_tensor(c, c, mhalf[:, 0:1], ALU.pow), half, *points)

        def rms(src, dst, n, col, points):
            done = []
            for t in range(2):
                c = st[:, col + t:col + t + 1]
                a = A.do(lambda: nc.scalar.activation(dst(t), src(t), ACT.Square, accum_out=c), points[t])
                v = V.do(lambda: nc.vector.tensor_scalar(c, c, 1.0 / n, RMS_EPS, ALU.mult, ALU.add), a)
                g = pow_rms(c, v)
                done.append(V.do(lambda: nc.vector.tensor_scalar(dst(t), src(t), c, None, ALU.mult), g))
            return done

        rows_at = [0]

        def load_rows(n, *points):
            for dst in (grow, brow)[:n]:
                i = rows_at[0]
                rows_at[0] += 1
                p = SP.dma(lambda: nc.sync.dma_start(
                    dst[:], rows[i:i + 1, :].partition_broadcast(128)), sem_row, *points)
            return p

        def turn_x(src, t, j, ready):
            b = 4 + 2 * t + j
            P.wait(free[b], consts)
            for i in range(4):
                fn = lambda: nc.tensor.transpose(ps[:, b, i * 128:(i + 1) * 128],
                                                 src[:, i * 128:(i + 1) * 128], ident)
                if i == 3:
                    p = P.do(fn, ready)
                else:
                    P.quiet(fn, ready)
            s3 = ps[:, b, :].rearrange("p (k s) -> p k s", k=4)
            h3, l3 = (t_[:, 4 * j:4 * j + 4, t * 128:(t + 1) * 128] for t_ in (XTh, XTl))
            v = split_out(s3, h3, l3, None, p)
            free[b] = [v]
            return v

        def x_ready(r):
            return lambda kt: [r[0, kt // 4], r[1, kt // 4]]

        def rms_end(points, rp, in_place):
            r, done = {}, []
            dst = X if in_place else XN
            for t in range(2):
                c = [st[:, 4 * t + i:4 * t + i + 1] for i in range(2)]
                v = None
                for j in range(2):
                    xs = X[:, t, j * 512:(j + 1) * 512]
                    b = acc_bank(t, j)
                    if points is not None:
                        v = V.do(lambda: nc.vector.tensor_tensor(xs, acc(t, j), xs, ALU.add),
                                 points[t, j])
                    a = A.do(lambda: nc.scalar.activation(ps[:, b, :], xs, ACT.Square, accum_out=c[j]), v,
                             x_loaded)
                    free[b] = [a]
                    if j == 0:
                        v = V.do(lambda: nc.vector.tensor_scalar(c[0], c[0], 1.0 / D, RMS_EPS, ALU.mult,
                                                                 ALU.add), a)
                    else:
                        v = V.do(lambda: nc.vector.scalar_tensor_tensor(
                            out=c[1], in0=c[1], scalar=1.0 / D, in1=c[0], op0=ALU.mult, op1=ALU.add), a,
                            v)
                g = pow_rms(c[1], v)
                for j in range(2):
                    sl = slice(j * 512, (j + 1) * 512)
                    v = V.do(lambda: nc.vector.scalar_tensor_tensor(
                        out=dst[:, t, sl], in0=X[:, t, sl], scalar=c[1], in1=grow[:, sl], op0=ALU.mult,
                        op1=ALU.mult), g, rp)
                    r[t, j] = turn_x(dst[:, t, sl], t, j, v)
                done.append(v)
            W.pump()
            W.pump()
            return x_ready(r), done

        def ln_end(points, rp, store=None):
            r, done = {}, []
            for t in range(2):
                s0, s1, nm, sq = (st[:, 8 * t + i:8 * t + i + 1] for i in range(4))
                for j, sj in enumerate((s0, s1)):
                    xs = X[:, t, j * 512:(j + 1) * 512]
                    rs = XN[:, t, j * 512:(j + 1) * 512]
                    v = V.do(lambda: nc.vector.scalar_tensor_tensor(
                        out=rs, in0=xs, scalar=ALPHA, in1=acc(t, j), op0=ALU.mult, op1=ALU.add,
                        accum_out=sj), points[t, j])
                v = V.do(lambda: nc.vector.tensor_tensor(nm, s0, s1, ALU.add), v)
                v = V.do(lambda: nc.vector.tensor_scalar(nm, nm, -1.0 / D, None, ALU.mult), v)
                a = A.do(lambda: nc.scalar.activation(
                    ps[:, 2 * t:2 * t + 2, :].rearrange("p a b -> p (a b)"), XN[:, t, :], ACT.Square,
                    bias=nm, accum_out=sq), v)
                free[2 * t] = free[2 * t + 1] = [a]
                v2 = V.do(lambda: nc.vector.scalar_tensor_tensor(
                    out=X[:, t, :], in0=XN[:, t, :], scalar=nm, in1=grow[:], op0=ALU.add, op1=ALU.mult), v,
                    rp)
                v = V.do(lambda: nc.vector.tensor_scalar(sq, sq, 1.0 / D, LN_EPS, ALU.mult, ALU.add), a)
                g = pow_rms(sq, v)
                for j in range(2):
                    sl = slice(j * 512, (j + 1) * 512)
                    v = V.do(lambda: nc.vector.scalar_tensor_tensor(
                        out=X[:, t, sl], in0=X[:, t, sl], scalar=sq, in1=brow[:, sl], op0=ALU.mult,
                        op1=ALU.add), g, v2, rp)
                    if store:
                        store(t, j, v)
                    else:
                        r[t, j] = turn_x(X[:, t, sl], t, j, v)
                done.append(v)
            W.pump()
            W.pump()
            return x_ready(r), done

        def conv(src, dst, name, col, stride, taps, bias, *points):
            for blk in range(2):
                sl = slice(blk * S, (blk + 1) * S)
                w = vcol(name, col + blk + (taps - 1) * stride)
                if bias is None:
                    a = A.do(lambda: nc.scalar.activation(dst[:, sl], src[:, sl], ACT.Copy, scale=w),
                             *points)
                else:
                    a = A.do(lambda: nc.scalar.activation(dst[:, sl], src[:, sl], ACT.Identity, scale=w,
                                                          bias=vcol(*bias, blk)), *points)
            v = [a, a]
            for s_ in range(1, taps):
                for blk in range(2):
                    w = vcol(name, col + blk + (taps - 1 - s_) * stride)
                    o = dst[:, blk * S + s_:(blk + 1) * S]
                    v[blk] = V.do(lambda: nc.vector.scalar_tensor_tensor(
                        out=o, in0=src[:, blk * S:(blk + 1) * S - s_], scalar=w, in1=o, op0=ALU.mult,
                        op1=ALU.add), v[blk], *points)
            return v

        ffn_area = Area(mix_base)
        HTh = ffn_area.take([128, 22, S], F32R)
        HTl = ffn_area.take([128, 22, S], F32R)
        yg = ffn_area.take([128, 2, 512])
        yu = ffn_area.take([128, 2, 512])
        sg = ffn_area.take([128, 2, 512])

        def ffn(layer, with_conv, xready):
            ready = {}
            yg_read, yu_read, sg_read = [None, None], [None, None], [None, None]

            def product(k, m, a, v):
                v = V.do(lambda: nc.vector.tensor_tensor(yu[:, k, :], usrc, sg[:, k, :], ALU.mult), v, a,
                         yu_read[k])
                sg_read[k] = v
                h2, l2 = (t_[:, 2 * m:2 * m + 2, :].rearrange("p k s -> p (k s)") for t_ in (HTh, HTl))
                yu_read[k] = ready[2 * m] = ready[2 * m + 1] = split_out(yu[:, k, :], h2, l2, None, v)
                return v

            for m in range(11):
                k = m % 2
                b, p = f_chunk("g", 2, xready)
                if with_conv:
                    v = conv(ps[:, b, :], yg[:, k, :], "ffn_w_conv", 132 * layer + 2 * m, 44, 3, None, p,
                             yg_read[k])
                    free[b] = v
                    W.pump()
                    a = A.do(lambda: nc.scalar.activation(sg[:, k, :], yg[:, k, :], ACT.Silu), v,
                             sg_read[k])
                    yg_read[k] = a
                else:
                    a = A.do(lambda: nc.scalar.activation(sg[:, k, :], ps[:, b, :], ACT.Silu), p,
                             sg_read[k])
                    free[b] = [a]
                    W.pump()
                b, p = f_chunk("u", 2, xready)
                if with_conv:
                    v = conv(ps[:, b, :], yu[:, k, :], "ffn_w_conv", 132 * layer + 22 + 2 * m, 44, 3, None,
                             p, yu_read[k])
                    usrc, free[b] = yu[:, k, :], v
                    W.pump()
                    product(k, m, a, v)
                else:
                    usrc = ps[:, b, :]
                    free[b] = [product(k, m, a, p)]
                    W.pump()
            return t_proj("down", 11, xt(HTh), xt(HTl), HALVES, acc, acc_bank, lambda kt: ready[kt],
                          split_end=True)

        def attention(n, scale, q_of, k_of, v_of, oh, ol, area, ready, vready, outs, prob=4, turned=3):
            Pb = area.take([128, prob, 384])
            PT = area.take([128, turned, 384])
            sc = area.take([128, prob, 8])
            normed, exps, trs, pvs, obank = {}, {}, {}, {}, {}

            def scores(h):
                k = h % prob
                b = bg_ring.take()
                P.wait(free[b], ready)
                for c, tq, tk in ((0, 0, 0), (1, 1, 1), (2, 1, 0)):
                    m = mm(ps[:, b, c * 128:(c + 1) * 128], q_of(h)[:, tq * 128:(tq + 1) * 128],
                           k_of(h)[:, tk * 128:(tk + 1) * 128], True, True)
                    if c == 2:
                        p = P.do(m)
                    else:
                        P.quiet(m)
                s2 = ps[:, b, 0:256]
                v = V.do(lambda: nc.vector.tensor_tensor(s2, s2, MASK, ALU.add), p, consts)
                V.do(lambda: nc.vector.reduce_max(sc[:, k, 0:1], ps[:, b, 0:128], AX_X), v,
                     normed.get(h - prob))
                v = V.do(lambda: nc.vector.reduce_max(sc[:, k, 1:2], ps[:, b, 128:384], AX_X), v)
                v = V.do(lambda: nc.vector.tensor_scalar(sc[:, k, 2:4], sc[:, k, 0:2], -scale, None,
                                                         ALU.mult), v)
                A.do(lambda: nc.scalar.activation(Pb[:, k, 0:128], ps[:, b, 0:128], ACT.Exp,
                                                  bias=sc[:, k, 2:3], scale=scale,
                                                  accum_out=sc[:, k, 4:5]), v, trs.get(h - prob))
                exps[h] = A.do(lambda: nc.scalar.activation(
                    Pb[:, k, 128:384], ps[:, b, 128:384], ACT.Exp, bias=sc[:, k, 3:4], scale=scale,
                    accum_out=sc[:, k, 5:6]))
                free[b] = [exps[h]]

            def normalise(h):
                k = h % prob
                v = V.do(lambda: nc.vector.reciprocal(sc[:, k, 6:8], sc[:, k, 4:6]), exps[h])
                V.do(lambda: nc.vector.tensor_scalar(Pb[:, k, 0:128], Pb[:, k, 0:128], sc[:, k, 6:7],
                                                     None, ALU.mult), v)
                normed[h] = V.do(lambda: nc.vector.tensor_scalar(
                    Pb[:, k, 128:384], Pb[:, k, 128:384], sc[:, k, 7:8], None, ALU.mult), v)

            def turn(h):
                k, k2 = h % prob, h % turned
                b = bg_ring.take()
                P.wait(free[b], normed[h])
                for c, src in ((0, 0), (1, 2), (2, 1)):
                    fn = lambda: nc.tensor.transpose(
                        ps[:, b, c * 128:(c + 1) * 128], Pb[:, k, src * 128:(src + 1) * 128], ident)
                    if c == 2:
                        trs[h] = P.do(fn)
                    else:
                        P.quiet(fn)
                a = A.do(lambda: nc.scalar.copy(PT[:, k2, :], ps[:, b, 0:384]), trs[h],
                         pvs.get(h - turned))
                free[b] = [a]
                return a

            def values(h, a):
                k2 = h % turned
                if h % 2 == 0:
                    obank[h // 2] = bg_ring.take()
                    P.wait(free[obank[h // 2]], vready())
                b = obank[h // 2]
                P.quiet(mm(ps[:, b, 0:256], v_of(h, 0), PT[:, k2, 0:256], h % 2 == 0, False), a)
                pvs[h] = P.do(mm(ps[:, b, 128:256], v_of(h, 1), PT[:, k2, 256:384], False, h % 2 == 1))
                if h % 2 == 1:
                    outs[h // 2] = split_out(ps[:, b, 0:256], oh(h // 2), ol(h // 2), None, pvs[h])
                    free[b] = [outs[h // 2]]

            tr = {}
            for i in range(n + 4):
                if 1 <= i < n + 1:
                    normalise(i - 1)
                if i < n:
                    scores(i)
                if 2 <= i < n + 2:
                    tr[i - 2] = turn(i - 2)
                if 3 <= i < n + 3:
                    while not vready():
                        yield True
                    values(i - 3, tr[i - 3])
                yield

        def rope_half(src, dst, heads, half, tab, t, points, tmp, tmp_free):
            x1, x2 = src[:, :, 0:half], src[:, :, half:2 * half]
            o1, o2 = dst[:, :, 0:half], dst[:, :, half:2 * half]
            cos = tab[:, t, 0, :].unsqueeze(1).to_broadcast([128, heads, half])
            sin = tab[:, t, 1, :].unsqueeze(1).to_broadcast([128, heads, half])
            t1, t2 = tmp[0][:, 0:heads, :], tmp[1][:, 0:heads, :]
            V.do(lambda: nc.vector.tensor_tensor(t1, x2, sin, ALU.mult), *points, tmp_free)
            V.do(lambda: nc.vector.tensor_tensor(o1, x1, cos, ALU.mult))
            V.do(lambda: nc.vector.tensor_tensor(t2, x1, sin, ALU.mult))
            v = V.do(lambda: nc.vector.tensor_tensor(o2, x2, cos, ALU.mult))
            V.do(lambda: nc.vector.tensor_tensor(o1, o1, t1, ALU.subtract), v)
            return V.do(lambda: nc.vector.tensor_tensor(o2, o2, t2, ALU.add))

        def short_conv(xready):
            area = Area(mix_base)
            Mh, Ml = area.take([128, 8, S], F32R), area.take([128, 8, S], F32R)
            cS, cv, y, prod = (area.take([128, 2, 512]) for _ in range(4))
            ready, prod_read = {}, [None, None]
            for m in range(4):
                k = m % 2
                b, p = f_chunk("c", 2, xready)
                a = A.do(lambda: nc.scalar.copy(cS[:, k, :], ps[:, b, :]), p, prod_read[k])
                free[b] = [a]
                W.pump()
                b, p = f_chunk("v", 2, xready)
                v = V.do(lambda: nc.vector.tensor_tensor(cv[:, k, :], ps[:, b, :], cS[:, k, :], ALU.mult),
                         a, p, prod_read[k])
                free[b] = [v]
                W.pump()
                c = conv(cv[:, k, :], y[:, k, :], "sc_w_conv", 2 * m, 8, 3, None, v, prod_read[k])
                b, p = f_chunk("b", 2, xready)
                v = V.do(lambda: nc.vector.tensor_tensor(prod[:, k, :], ps[:, b, :], y[:, k, :], ALU.mult),
                         c, p, prod_read[k])
                free[b] = [v]
                h2, l2 = (t_[:, 2 * m:2 * m + 2, :].rearrange("p k s -> p (k s)") for t_ in (Mh, Ml))
                v = split_out(prod[:, k, :], h2, l2, None, v)
                prod_read[k] = v
                ready[2 * m] = ready[2 * m + 1] = v
                W.pump()
            return t_proj("sc_out", 4, xt(Mh), xt(Ml), HALVES, acc, acc_bank, lambda kt: ready[kt],
                          split_end=True)

        def moba(xready):
            area = Area(mix_base)
            qT = area.take([128, 8, S])
            kT = area.take([128, 2, 8, S])
            vp = area.take([128, 2, 2, 8, 128])
            attn = Area(area.at)
            kt_ = area.take([128, 2, D])
            tmp = [area.take([128, 16, 32]) for _ in range(2)]
            qt = XN
            xdone = [xready(7)]
            z = fill([(kT[64:128, 0], 0.0), (kT[0:64, 1], 0.0), (vp[:, :, 0, :, 64:128], 0.0),
                      (vp[:, :, 1, :, 0:64], 0.0)], *xdone)
            state = {"tf": None}
            turned = []

            def rope_turn(points, bank0, src_t, is_q):
                for t in range(2):
                    src = ps[:, bank0 + 2 * t:bank0 + 2 * t + 2, :].rearrange("p a (h d) -> p (a h) d", d=64)
                    v = rope_half(src, src_t[:, t, :].rearrange("p (h d) -> p h d", d=64), 16, 32, ROPE, t,
                                  [points[t, 0], points[t, 1], consts], tmp, state["tf"])
                    state["tf"] = v
                    free[bank0 + 2 * t] = free[bank0 + 2 * t + 1] = [v]
                    yield
                for i0 in range(0, 8, 2):
                    b = bg_ring.take()
                    P.wait(free[b], v)
                    for i in (i0, i0 + 1):
                        for t in range(2):
                            o = ps[:, b, (i - i0) * S + t * 128:(i - i0) * S + (t + 1) * 128]
                            p = P.do(lambda: nc.tensor.transpose(o, src_t[:, t, i * 128:(i + 1) * 128],
                                                                 ident))
                    s3 = ps[:, b, :].rearrange("p (a b) -> p a b", a=2)
                    if is_q:
                        done = A.do(lambda: nc.scalar.copy(qT[:, i0:i0 + 2, :], s3), p)
                    else:
                        A.do(lambda: nc.scalar.copy(kT[0:64, 0, i0:i0 + 2, :], s3[0:64]), p, *z)
                        done = A.do(lambda: nc.scalar.copy(kT[64:128, 1, i0:i0 + 2, :], s3[64:128]))
                    free[b] = [done]
                    yield
                turned.append(done)
                attn_free.append(p)

            attn_free, vready, outs = [], [], {}
            qd = lambda t, j: ps[:, 2 * t + j, :]
            kd = lambda t, j: ps[:, 4 + 2 * t + j, :]
            p = t_proj("qkv", 4, xt(XTh), xt(XTl), HALVES, qd, acc_bank, xready)
            bg_ring.banks = [0, 1, 2, 3]
            bg.tasks.append(rope_turn(p, 0, qt, True))
            bg.rate = 1.0
            p = t_proj("qkv", 4, xt(XTh), xt(XTl), HALVES, kd, lambda t, j: 4 + 2 * t + j, xready)
            bg.finish()
            bg_ring.banks = [4, 5, 6, 7]
            bg.tasks.append(rope_turn(p, 4, kt_, False))

            def att():
                ready = turned + attn_free + [state["tf"]]
                V.wait(attn_free, state["tf"])
                A.wait(attn_free, state["tf"])
                yield from attention(16, 0.125, lambda h: qT[:, h // 2, :], lambda h: kT[:, h % 2, h // 2, :],
                                     lambda h, kt: vp[:, kt, h % 2, h // 2, :], xt(XTh), xt(XTl), attn,
                                     ready, lambda: vready, outs)

            bg.tasks.append(att())
            bg.rate = RATE_MOBA_V
            p = t_proj("qkv", 4, xt(XTh), xt(XTl), HALVES, acc, acc_bank, xready)
            for t in range(2):
                for par in range(2):
                    v = A.do(lambda: nc.scalar.copy(
                        vp[:, t, par, :, 64 * par:64 * par + 64].rearrange("p (a h) d -> p a h d", a=2),
                        ps[:, 2 * t:2 * t + 2, :].rearrange("p a (h c d) -> p a h c d", c=2, d=64)[
                            :, :, :, par, :]), p[1, 1], *z)
                free[2 * t] = free[2 * t + 1] = [v]
            vready.append(v)
            W.pump()
            bg.rate = RATE_MOBA_O

            def oready(kt):
                bg.until(lambda: kt in outs)
                return outs[kt]

            p = t_proj("moba_out", 4, xt(XTh), xt(XTl), HALVES, acc, acc_bank, oready, split_end=True)
            bg.finish()
            bg_ring.banks = [6, 7]
            return p

        def log1pexp(x, area, n, *points):
            e, u, d, z, l = (area.take([128, n]) for _ in range(5))
            v = V.do(lambda: nc.vector.tensor_scalar(e[:], x, -1.0, None, ALU.mult), *points)
            v = V.do(lambda: nc.vector.tensor_tensor(e[:], e[:], x, ALU.min), v)
            a = A.do(lambda: nc.scalar.activation(e[:], e[:], ACT.Exp), v)
            v = V.do(lambda: nc.vector.tensor_scalar(u[:], e[:], 1.0, None, ALU.add), a)
            a = A.do(lambda: nc.scalar.activation(l[:], u[:], ACT.Ln), v)
            v = V.do(lambda: nc.vector.tensor_scalar(d[:], u[:], -1.0, None, ALU.add), v)
            v = V.do(lambda: nc.vector.tensor_scalar(z[:], d[:], 0.0, None, ALU.is_equal), v)
            v = V.do(lambda: nc.vector.tensor_tensor(d[:], d[:], z[:], ALU.add), v)
            v = V.do(lambda: nc.vector.reciprocal(d[:], d[:]), v)
            v = V.do(lambda: nc.vector.tensor_tensor(d[:], d[:], e[:], ALU.mult), v)
            v = V.do(lambda: nc.vector.tensor_tensor(l[:], l[:], z[:], ALU.add), a, v)
            v = V.do(lambda: nc.vector.tensor_tensor(l[:], l[:], d[:], ALU.mult), v)
            return l, v

        def even(xready, xdone):
            area = Area(mix_base)
            xzS = area.at
            xb = area.take([128, 12, S])
            zS = Area(xzS).take([128, 2, D])
            xd_at = area.at
            Ph, Pl = area.take([128, 4, S], F32R), area.take([128, 4, S], F32R)
            xdec = Area(xd_at).take([128, D])
            xtok, xdt = (area.take([128, 2, D]) for _ in range(2))
            prev = area.take([128, D])
            Btok, CBm = area.take([128, 256]), area.take([128, 4, 128])
            gda, ex = area.take([128, 2, 4, 128]), area.take([128, 2, 4, 128])
            pwt = area.take([128, 4, 128])
            dtT = area.take([16, S])
            dt_, da, E1, D0 = (area.take([128, n]) for n in (32, 32, 16, 16))
            ah = area.take([128, 16])
            y = XN
            us = XN[:, 1, :].rearrange("p (g s) -> p g s", g=4)
            sem_p = [sem("s_pw"), 0]
            pwl = SP.dma(lambda: nc.sync.dma_start(pwt[:], pw), sem_p, xready(7))
            ready = {}
            two = lambda ap: ap.unsqueeze(1).to_broadcast([128, 2, 16])
            v3 = lambda t_: t_[:].rearrange("p (t e) -> p t e", t=2)
            bc = lambda ap, n=64: ap.unsqueeze(2).to_broadcast([128, ap.shape[1], n])
            by = lambda ap: ap.rearrange("p (e d) -> p e d", d=64)
            f_ring.banks = [4, 5]
            bg_ring.banks = [6, 7]
            st_ = {}

            b, p = f_chunk("dt", 1, xready)
            adt = A.do(lambda: nc.scalar.copy(dtT[:], ps[0:16, b, 0:S]), p)
            free[b] = [adt]
            W.pump()

            def dt_task():
                b = bg_ring.take()
                P.wait(adt, free[b])
                P.quiet(lambda: nc.tensor.transpose(ps[:, b, 0:16], dtT[:, 0:128], ident[0:16, 0:16]))
                p = P.do(lambda: nc.tensor.transpose(ps[:, b, 16:32], dtT[:, 128:256], ident[0:16, 0:16]))
                v = V.do(lambda: nc.vector.tensor_tensor(v3(da), ps[:, b, 0:32].rearrange(
                    "p (t e) -> p t e", t=2), two(sm[:, 0:16]), ALU.add), p, consts)
                free[b] = [v]
                l, v2 = log1pexp(da[:], area, 32, v)
                v = V.do(lambda: nc.vector.tensor_scalar(dt_[:], da[:], 0.0, None, ALU.max), v2)
                v = V.do(lambda: nc.vector.tensor_tensor(dt_[:], dt_[:], l[:], ALU.add), v)
                a = A.do(lambda: nc.scalar.activation(ah[:], sm[:, 16:32], ACT.Exp), consts)
                st_["dready"] = V.do(lambda: nc.vector.scalar_tensor_tensor(
                    out=v3(da), in0=v3(dt_), scalar=-1.0, in1=two(ah[:]), op0=ALU.mult, op1=ALU.mult),
                    v, a)
                yield

            bg.tasks.append(dt_task())
            bg.rate = 1.0
            for m in range(6):
                b, p = f_chunk("xbc", 2, xready)
                v = conv(ps[:, b, :], xb[:, 2 * m:2 * m + 2, :].rearrange("p a b -> p (a b)"), "conv_w_2",
                         2 * m, 12, 4, ("conv_b_2", 2 * m), p)
                free[b] = v
                W.pump()
                st_["xb"] = A.do(lambda: nc.scalar.activation(
                    xb[:, 2 * m:2 * m + 2, :], xb[:, 2 * m:2 * m + 2, :], ACT.Silu), v)

            def core():
                dready, xbr = st_["dready"], st_["xb"]
                xr = []
                for t in range(2):
                    for j in range(2):
                        b = bg_ring.take()
                        P.wait(free[b], xbr)
                        for i in range(4):
                            p = P.do(lambda: nc.tensor.transpose(
                                ps[:, b, i * 128:(i + 1) * 128], xb[:, 4 * j + i, t * 128:(t + 1) * 128],
                                ident))
                        a = A.do(lambda: nc.scalar.copy(xtok[:, t, j * 512:(j + 1) * 512], ps[:, b, :]), p)
                        free[b] = [a]
                        if j == 0:
                            yield
                    xr.append(V.do(lambda: nc.vector.tensor_tensor(
                        by(xdt[:, t, :]), by(xtok[:, t, :]), bc(dt_[:, 16 * t:16 * t + 16]), ALU.mult), a,
                        dready))
                    st_["turned"] = p
                    yield
                b = bg_ring.take()
                P.wait(free[b])
                for g in range(2):
                    p = P.do(lambda: nc.tensor.transpose(ps[:, b, g * 128:(g + 1) * 128], xb[:, 8 + g, 0:128],
                                                         ident))
                bt = A.do(lambda: nc.scalar.copy(Btok[:], ps[:, b, 0:256]), p)
                free[b] = [bt]
                b = bg_ring.take()
                P.wait(free[b])
                for c in range(2):
                    for g in range(2):
                        i, sl = 2 * c + g, slice(c * 128, (c + 1) * 128)
                        p = P.do(mm(ps[:, b, i * 128:(i + 1) * 128], xb[:, 8 + g, sl], xb[:, 10 + g, sl],
                                    True, True))
                cb = V.do(lambda: nc.vector.tensor_tensor(
                    CBm[:], ps[:, b, :].rearrange("p (i l) -> p i l", i=4),
                    U.unsqueeze(1).to_broadcast([128, 4, 128]), ALU.mult), p)
                free[b] = [cb]
                yield
                b = bg_ring.take()
                P.wait(free[b], dready)
                P.quiet(mm(ps[:, b, 0:16], GT, da[:, 0:16], True, True))
                p = P.do(mm(ps[:, b, 16:32], U, da[:, 16:32], True, True))
                A.do(lambda: nc.scalar.activation(D0[:], ps[:, b, 0:16], ACT.Exp), p)
                a = A.do(lambda: nc.scalar.activation(E1[:], ps[:, b, 16:32], ACT.Exp))
                free[b] = [a]
                xd = V.do(lambda: nc.vector.tensor_tensor(by(xdec[:]), by(xdt[:, 0, :]), bc(D0[:]),
                                                          ALU.mult), a, xr[0])
                yield
                for g in range(2):
                    b = bg_ring.take()
                    p = P.do(mm(ps[:, b, :], Btok[:, g * 128:(g + 1) * 128],
                                xdec[:, g * 512:(g + 1) * 512], True, True), xd, bt, free[b])
                    pv = A.do(lambda: nc.scalar.copy(prev[:, g * 512:(g + 1) * 512], ps[:, b, :]), p)
                    free[b] = [pv]
                st_["states"] = p
                yield
                gread, eread = [None, None], [None, None]
                quarters = [(c, g, q) for c in range(2) for g in range(2) for q in range(2)]
                made = {}

                def decays(n):
                    c, g, q = quarters[n]
                    k, e0 = n % 2, 8 * g + 4 * q
                    v = V.do(lambda: nc.vector.tensor_tensor(
                        gda[:, k], GT.unsqueeze(1).to_broadcast([128, 4, 128]),
                        bc(da[:, 16 * c + e0:16 * c + e0 + 4], 128), ALU.mult), dready, gread[k])
                    b = bg_ring.take()
                    P.wait(v, free[b])
                    for i in range(4):
                        p = P.do(mm(ps[:, b, i * 128:(i + 1) * 128], gda[:, k, i, :], U, True, True))
                    gread[k] = p
                    a = A.do(lambda: nc.scalar.activation(
                        ex[:, k], ps[:, b, :].rearrange("p (i l) -> p i l", i=4), ACT.Exp), p, eread[k])
                    free[b] = [a]
                    made[n] = V.do(lambda: nc.vector.tensor_tensor(
                        ex[:, k], ex[:, k], CBm[:, 2 * c + g, :].unsqueeze(1).to_broadcast([128, 4, 128]),
                        ALU.mult), a, cb)

                v = None
                for n in range(9):
                    if n < 8:
                        decays(n)
                    if n >= 1:
                        c, g, q = quarters[n - 1]
                        k = (n - 1) % 2
                        yb = bg_ring.take()
                        P.wait(free[yb], made[n - 1], xr[c])
                        for i in range(4):
                            h = 8 * g + 4 * q + i
                            p = P.do(mm(ps[:, yb, i * 64:(i + 1) * 64], ex[:, k, i, :],
                                        xdt[:, c, h * 64:(h + 1) * 64], True, True))
                        eread[k] = p
                        sl = slice(g * 512 + q * 256, g * 512 + (q + 1) * 256)
                        h0 = 8 * g + 4 * q
                        yc, xc = y[:, c, sl], xtok[:, c, sl]
                        v = V.do(lambda: nc.vector.tensor_tensor(
                            by(xc), by(xc), bc(sm[:, 32 + h0:36 + h0]), ALU.mult), xr[c])
                        v = V.do(lambda: nc.vector.tensor_tensor(yc, ps[:, yb, 0:256], xc, ALU.add), v, p,
                                 st_["pooled"] if c == 1 else None)
                        free[yb] = [v]
                        if c == 1:
                            b = bg_ring.take()
                            p = P.do(mm(ps[:, b, 0:256], xb[:, 10 + g, 128:256], prev[:, sl], True, True),
                                     pv, free[b])
                            v2 = V.do(lambda: nc.vector.tensor_tensor(
                                by(xc), by(ps[:, b, 0:256]), bc(E1[:, h0:h0 + 4]), ALU.mult), p, v)
                            free[b] = [v2]
                            v = V.do(lambda: nc.vector.tensor_tensor(yc, yc, xc, ALU.add), v2)
                        st_["y", c] = v
                        st_["xb_read"] = p
                    yield

            def pooling():
                last = [st_["states"], None]
                bufs = [gda2[:, 0:S], gda2[:, S:2 * S]]
                for g in range(4):
                    u, src = us[:, g, :], us[:, g, :]
                    v = st_["us"]
                    for i in range(g + 1):
                        sh, dst = 1 << i, bufs[i % 2]
                        V.do(lambda: nc.vector.tensor_copy(dst[:, 0:sh], src[:, 0:sh]), v, last)
                        v = V.do(lambda: nc.vector.tensor_tensor(
                            dst[:, sh:S], src[:, sh:S], src[:, 0:S - sh], ALU.add), v)
                        src = dst
                    cnt = cs[:, CST["cnt"] + 16 * g:CST["cnt"] + 16 * g + 16]
                    dst = bufs[(g + 1) % 2]
                    v = V.do(lambda: nc.vector.tensor_tensor(dst[:, 0:16], src[:, 0:16], cnt, ALU.mult), v,
                             last)
                    V.do(lambda: nc.vector.tensor_tensor(dst[:, 0:16], dst[:, 0:16], u[:, 0:16],
                                                         ALU.subtract), v)
                    v = V.do(lambda: nc.vector.scalar_tensor_tensor(
                        out=dst[:, 16:S], in0=src[:, 16:S], scalar=1.0 / (2 << g), in1=u[:, 16:S],
                        op0=ALU.mult, op1=ALU.subtract))
                    st_["pooled"] = v
                    yield
                    b2 = bg_ring.take()
                    p2 = P.do(mm(ps[:, b2, 0:S], pwt[:, g, :], dst, True, True), v, pwl, free[b2])
                    last = [p2]
                    ready[g] = split_out(ps[:, b2, 0:S], Ph[:, g, :], Pl[:, g, :],
                                         vcol("pool_scale_2", g), p2)
                    free[b2] = [ready[g]]
                    yield

            gda2 = gda[:].rearrange("p a b c -> p (a b c)")
            cg = core()
            bg.tasks.append(cg)
            bg.rate = 1.0
            for m in range(2):
                b, p = f_chunk("pool", 2, xready)
                st_["us"] = A.do(lambda: nc.scalar.copy(
                    us[:, 2 * m:2 * m + 2, :].rearrange("p a b -> p (a b)"), ps[:, b, :]), p)
                free[b] = [st_["us"]]
                W.pump()
                bg.tick()
            bg.until(lambda: "states" in st_)
            bg.tasks.insert(0, pooling())
            bg_ring.banks = [4, 5, 6, 7]
            bg.rate = RATE_EVEN
            p = t_proj("z", 4, xt(XTh), xt(XTl), HALVES, acc, acc_bank, xready)
            while bg.step():
                pass
            for t in range(2):
                zr = A.do(lambda: nc.scalar.activation(
                    zS[:, t, :], ps[:, 2 * t:2 * t + 2, :].rearrange("p a b -> p (a b)"), ACT.Silu),
                    p[1, 1], st_["turned"], st_["xb_read"])
                free[2 * t] = free[2 * t + 1] = [zr]

            def tail():
                ys = []
                for c in range(2):
                    ys.append(V.do(lambda: nc.vector.tensor_tensor(y[:, c, :], y[:, c, :], zS[:, c, :],
                                                                   ALU.mult), st_["y", c], zr))
                done = rms(lambda t: y[:, t, :], lambda t: xtok[:, t, :], D, 0, ys)
                yield
                r = yield from to_feature(lambda t, kt: xtok[:, t, kt * 128:(kt + 1) * 128], 8, xt(XTh),
                                          xt(XTl), lambda kt: vcol("ssm_norm_w_2", kt), done)
                for kt in range(8):
                    ready[4 + kt] = r[kt]

            bg.tasks.append(tail())
            bg.step()
            bg.rate = 0.0
            hi = lambda kt: Ph[:, kt, :] if kt < 4 else XTh[:, kt - 4, :]
            lo = lambda kt: Pl[:, kt, :] if kt < 4 else XTl[:, kt - 4, :]

            def yready(kt):
                if kt == 3:
                    bg.finish()
                return ready[kt]

            p = t_proj("even_out", 6, hi, lo, HALVES, acc, acc_bank, yready, split_end=True)
            f_ring.banks = [4, 5, 6, 7]
            bg_ring.banks = [6, 7]
            return p

        def odd(xready, xdone):
            area = Area(mix_base)
            qh, kh = area.take([66, 8, S]), area.take([66, 8, S])
            vf = area.take([128, 2, 2, 4, 128])
            CQh, CQl = area.take([128, 4, S], F32R), area.take([128, 4, S], F32R)
            CKh, CKl = area.take([128, 2, S], F32R), area.take([128, 2, S], F32R)
            attn = Area(area.at)
            attn_start = area.at
            area = Area(area.at + 4 * 1536 + 3 * 1536 + 256)
            early = Area(area.at)
            vm = area.take([128, 2, 2, 4, 128])
            krt, kr2, lf = area.take([128, 2, 32]), area.take([128, 2, 32]), area.take([128, 16])
            tmp = [area.take([128, 8, 16]) for _ in range(2)]
            fk = early.take([40, S])
            fc = early.take([8, S])
            fc2 = early.take([8, S])
            cq, ckv = (lambda t: XN[:, t, 0:512]), (lambda t: XN[:, t, 512:768])
            km_area = [Area(xt_at[0] + 4096), Area(xt_at[1] + 4096)]
            km = [km_area[i].take([128, 768]) for i in range(2)]
            qm = [XN[:, t, 0:768] for t in range(2)]
            f_ring.banks = [4, 5]
            bg_ring.banks = [6, 7]
            sem_f = [sem("s_fc"), 0]
            ones = fill([(qh[64:66], 1.0), (kh[64:66], 1.0)], xready(7))
            zf = fill([(vf[:, :, 0, :, 64:128], 0.0), (vf[:, :, 1, :, 0:64], 0.0)], *ones)
            b, p = f_chunk("flkr", 1, xready)
            afk = A.do(lambda: nc.scalar.copy(fk[:], ps[0:40, b, 0:S]), p)
            free[b] = [afk]
            W.pump()
            st_ = {}

            def forget():
                b = bg_ring.take()
                P.wait(afk, free[b])
                for t in range(2):
                    p = P.do(lambda: nc.tensor.transpose(ps[:, b, t * 40:t * 40 + 40],
                                                         fk[:, t * 128:(t + 1) * 128], ident[0:40, 0:40]))
                v80 = ps[:, b, 0:80].rearrange("p (t c) -> p t c", t=2)
                lf3 = lf[:].rearrange("p (t c) -> p t c", t=2)
                st_["krt"] = V.do(lambda: nc.vector.tensor_copy(krt[:], v80[:, :, 8:40]), p)
                v = V.do(lambda: nc.vector.tensor_tensor(
                    lf3, v80[:, :, 0:8], sm[:, 48:56].unsqueeze(1).to_broadcast([128, 2, 8]), ALU.add), p)
                free[b] = [v]
                yield
                l, v2 = log1pexp(lf[:], area, 16, v)
                v = V.do(lambda: nc.vector.tensor_scalar(lf[:], lf[:], 0.0, None, ALU.min), v2)
                v = V.do(lambda: nc.vector.tensor_tensor(lf[:], lf[:], l[:], ALU.subtract), v)
                yield
                b = bg_ring.take()
                P.wait(v, free[b])
                P.quiet(mm(ps[0:8, b, 0:S], lf[:, 0:8], UO, True, False))
                p = P.do(mm(ps[0:8, b, 128:S], lf[:, 8:16], U, False, True))
                V.do(lambda: nc.vector.tensor_scalar(fc[:], ps[0:8, b, 0:S], 8.0, None, ALU.mult), p)
                v = V.do(lambda: nc.vector.tensor_scalar(fc2[:], ps[0:8, b, 0:S], -8.0, None, ALU.mult))
                free[b] = [v]
                for h in range(8):
                    SP.dma(lambda: nc.sync.dma_start(qh[64:65, h, :], fc[h:h + 1, :]), sem_f, v, *ones)
                    st_["f"] = SP.dma(lambda: nc.sync.dma_start(kh[65:66, h, :], fc2[h:h + 1, :]), sem_f)
                yield

            bg.tasks.append(forget())
            bg.rate = 1.0
            for tag, dst in (("qf", qh), ("kf", kh)):
                for m in range(2):
                    b, p = f_chunk(tag, 2, xready)
                    s3 = ps[:, b, :].rearrange("p (a s) -> p a s", a=2)
                    d4 = dst[0:64, 4 * m:4 * m + 4, :].rearrange("p (a c) s -> p a c s", c=2)
                    A.do(lambda: nc.scalar.copy(d4[:, :, 0, :], s3[0:64]), p)
                    qk = A.do(lambda: nc.scalar.copy(d4[:, :, 1, :], s3[64:128]))
                    free[b] = [qk]
                    W.pump()
            bg.finish()
            bg_ring.banks = [4, 5, 6, 7]
            outs, outs2, vready = {}, {}, []
            bg.tasks.append(attention(
                8, 0.125, lambda h: qh[:, h, :], lambda h: kh[:, h, :],
                lambda h, kt: vf[:, kt, h % 2, h // 2, :], xt(XTh), xt(XTl), attn, [qk, st_["f"]],
                lambda: vready, outs))
            d = lambda t, j: ps[:, t, 0:256]
            p = t_proj("ckv", 1, xt(XTh), xt(XTl), [(0, 256)], d, lambda t, j: t, xready, per=8)
            d2 = rms(lambda t: ps[:, t, 0:256], ckv, 256, 10, [p[0, 0], p[1, 0]])
            free[0], free[1] = [d2[0]], [d2[1]]
            p = t_proj("cq", 2, xt(XTh), xt(XTl), [(0, 512)], lambda t, j: ps[:, 2 + t, :],
                       lambda t, j: 2 + t, xready, per=4)
            d1 = rms(lambda t: ps[:, 2 + t, :], cq, 512, 8, [p[0, 0], p[1, 0]])
            free[2], free[3] = [d1[0]], [d1[1]]

            def latents():
                st_["r2"] = yield from to_feature(
                    lambda t, kt: ckv(t)[:, kt * 128:(kt + 1) * 128], 2, xt(CKh), xt(CKl),
                    lambda kt: vcol("kv_norm_w_2", kt), d2)
                st_["r1"] = yield from to_feature(
                    lambda t, kt: cq(t)[:, kt * 128:(kt + 1) * 128], 4, xt(CQh), xt(CQl),
                    lambda kt: vcol("q_norm_w_2", kt), d1)

            def padded(dst, src, t, par, *points):
                return A.do(lambda: nc.scalar.copy(
                    dst[:, t, par, :, 64 * par:64 * par + 64].rearrange("p (a h) d -> p a h d",
                                                                      a=src.shape[1]), src), *points)

            bg.tasks.insert(0, latents())
            bg.rate = 1.0
            p = t_proj("vf", 2, xt(XTh), xt(XTl), [(0, 512)], lambda t, j: ps[:, t, :], lambda t, j: t,
                       xready, per=4)
            xused = p[1, 0]
            for t in range(2):
                for par in range(2):
                    v = padded(vf, ps[:, t:t + 1, :].rearrange("p a (h c d) -> p a h c d", c=2, d=64)[
                        :, :, :, par, :], t, par, p[1, 0], *zf)
                free[t] = [v]
            vready.append(v)
            bg.until(lambda: "r1" in st_)
            bg.rate = RATE_ODD
            p = t_proj("ukv", 1, xt(CKh), xt(CKl), HALVES, acc, acc_bank, lambda kt: st_["r2"][kt])
            zm = fill([(vm[:, :, 0, :, 64:128], 0.0), (vm[:, :, 1, :, 0:64], 0.0)], st_["f"], *zf)
            tf = None
            for t in range(2):
                tf = rope_half(krt[:, t:t + 1, :], kr2[:, t:t + 1, :], 1, 16, ROPE2, t, [st_["krt"]], tmp,
                               tf)
                k3 = km[t][:].rearrange("p (h d) -> p h d", d=96)
                sv = ps[:, 2 * t:2 * t + 2, :].rearrange("p a (h c d) -> p (a h) c d", c=2, d=64)
                ka = A.do(lambda: nc.scalar.copy(k3[:, :, 0:64], sv[:, :, 0, :]), p[1, 1], xused)
                for par in range(2):
                    va = padded(vm, ps[:, 2 * t:2 * t + 2, :].rearrange(
                        "p a (h q c d) -> p a h q c d", q=2, c=2, d=64)[:, :, :, par, 1, :], t, par, *zm)
                kv_ = V.do(lambda: nc.vector.tensor_copy(
                    k3[:, :, 64:96], kr2[:, t, :].unsqueeze(1).to_broadcast([128, 8, 32])), tf, xused)
                free[2 * t] = free[2 * t + 1] = [va]
            kready = [ka, kv_]
            p = t_proj("uq", 2, xt(CQh), xt(CQl), [(0, 384), (384, 768)],
                       lambda t, j: ps[:, 2 * t + j, 0:384], acc_bank, lambda kt: st_["r1"][kt])
            for t in range(2):
                q3 = qm[t].rearrange("p (h d) -> p h d", d=96)
                sv = ps[:, 2 * t:2 * t + 2, 0:384].rearrange("p a (h d) -> p a h d", d=96)
                qa = A.do(lambda: nc.scalar.copy(
                    qm[t].rearrange("p (a h d) -> p a h d", a=2, d=96)[:, :, :, 0:64],
                    sv[:, :, :, 0:64]), p[1, 1])
                for a_ in range(2):
                    tf = rope_half(sv[:, a_, :, 64:96], q3[:, 4 * a_:4 * a_ + 4, 64:96], 4, 16, ROPE2, t,
                                   [qa], tmp, tf)
                free[2 * t] = free[2 * t + 1] = [qa, tf]
            qready = [qa, tf]
            bg.finish()
            qmT, kmT = Area(mix_base).take([96, 8, S]), Area(mix_base + 8192).take([96, 8, S])
            attn2 = Area(attn_start)

            def latent_attention():
                tr = []
                for src, dst, rd in ((km, kmT, kready), (qm, qmT, qready)):
                    for i0 in range(0, 8, 2):
                        b = bg_ring.take()
                        P.wait(free[b], *rd)
                        for i in (i0, i0 + 1):
                            for t in range(2):
                                o = ps[0:96, b, (i - i0) * S + t * 128:(i - i0) * S + (t + 1) * 128]
                                p = P.do(lambda: nc.tensor.transpose(o, src[t][:, i * 96:(i + 1) * 96],
                                                                     ident))
                        e, cp = ((A, nc.scalar.copy), (V, nc.vector.tensor_copy))[(i0 // 2) % 2]
                        done = e.do(lambda: cp(dst[:, i0:i0 + 2, :].rearrange("p a b -> p (a b)"),
                                               ps[0:96, b, :]), p)
                        free[b] = [done]
                        tr.append(done)
                    yield
                yield from attention(8, float(96) ** -0.5, lambda h: qmT[:, h, :], lambda h: kmT[:, h, :],
                                     lambda h, kt: vm[:, kt, h % 2, h // 2, :],
                                     lambda kt: XTh[:, 4 + kt, :], lambda kt: XTl[:, 4 + kt, :], attn2,
                                     tr + [va], lambda: [va], outs2)

            bg.tasks.append(latent_attention())
            bg.step()
            bg.rate = RATE_ODD_OUT

            def oready(kt):
                if kt < 4:
                    return outs[kt]
                bg.until(lambda: kt - 4 in outs2)
                return outs2[kt - 4]

            p = t_proj("odd_out", 4, xt(XTh), xt(XTl), HALVES, acc, acc_bank, oready, split_end=True)
            bg.finish()
            f_ring.banks = [4, 5, 6, 7]
            bg_ring.banks = [6, 7]
            return p

        rp = load_rows(1)
        xr, done = rms_end(None, rp, False)
        for layer in range(2):
            rp = load_rows(1, done)
            xr, done = rms_end((short_conv, moba)[layer](xr), rp, False)
            rp = load_rows(1, done)
            xr, done = rms_end(ffn(layer, True, xr), rp, layer == 1)
        for layer in range(2):
            rp = load_rows(2, done)
            xr, done = ln_end((even, odd)[layer](xr, done), rp)
            rp = load_rows(2, done)
            if layer == 0:
                xr, done = ln_end(ffn(layer, False, xr), rp)
        sem_out = [sem("s_out"), 0]
        stored = []

        def store(t, j, v):
            sl = slice(j * 512, (j + 1) * 512)
            stored.append(SP.dma(lambda: nc.sync.dma_start(out[0, t * 128:(t + 1) * 128, sl], X[:, t, sl]),
                                 sem_out, v))

        ln_end(ffn(1, False, xr), rp, store)
        SP.wait(stored[-1])
        assert W.i == len(plan)


def layout(i):
    plan = weight_plan()
    wts = np.zeros((len(plan), 128, CW), np.float32)
    for n, (_, _, name, layer, cols, width, nk, k0) in enumerate(plan):
        w = i[name][layer]
        dst = wts[n, :, 0:width * nk].reshape(128, nk, width)
        at = 0
        for c0, m in cols:
            blk = w[k0 * 128:(k0 + nk) * 128, c0:c0 + m]
            dst[:, :, at:at + m] = blk.reshape(nk, 128, m).transpose(1, 0, 2)
            at += m
    vec = np.zeros((128, NVEC), np.float32)
    for name, c in VEC.items():
        a = i[name].reshape(-1, 128)
        vec[:, c:c + a.shape[0]] = a.T
    rows = np.stack([i["mix_norm"][0], i["ffn_norm"][0], i["mix_norm"][1], i["ffn_norm"][1],
                     i["final_norm"], i["ln_mix_g_2"][0], i["ln_mix_b_2"][0], i["ln_ffn_g_2"][0],
                     i["ln_ffn_b_2"][0], i["ln_mix_g_2"][1], i["ln_mix_b_2"][1], i["ln_ffn_g_2"][1],
                     i["ln_ffn_b_2"][1]])
    small = np.concatenate([i["dt_bias_2"][0], i["a_log_2"][0], i["d_skip_2"][0], i["fgate_b_2"][0]])
    pw = np.ascontiguousarray(i["pool_w_2"][0].transpose(1, 0, 2))
    cst = constants()
    return dict(wts=wts, vec=vec, cst=cst, rows=rows, small=small, pw=pw,
                x_in=np.ascontiguousarray(i["x"]))


def kernel(**inputs):
    import concourse.bacc as _bacc
    from concourse.bass_utils import run_bass_kernel_spmd as _run

    nc = _bacc.Bacc("TRN2", target_bir_lowering=False, num_devices=1)
    arrays = layout({k: np.asarray(v) for k, v in inputs.items()})
    args = {k: nc.dram_tensor("in_" + k, a.shape, mybir.dt.from_np(a.dtype), kind="ExternalInput").ap()
            for k, a in arrays.items()}
    out = nc.dram_tensor("out_0", (1, S, D), F32, kind="ExternalOutput").ap()
    build(nc, out=out, **args)
    r = _run(nc, [{"in_" + k: a for k, a in arrays.items()}], core_ids=[0])
    return r.results[0]["out_0"]
```

```python
from contextlib import ExitStack

import numpy as np

import concourse.bass as bass
from concourse import mybir

F32 = mybir.dt.float32
F32R = mybir.dt.float32r
ACT = mybir.ActivationFunctionType
ALU = mybir.AluOpType
AX_X = mybir.AxisListType.X

D, S, FF = 1024, 256, 2816
CW = 2048
NRAW, NHI, NLO = 4, 5, 4
NEG = -1.0e30
LAG_ROPE = 5.0
N_WARM = 20
TURN_AT = (1, 2)
ALPHA = float((2 * 2) ** 0.25)
RMS_EPS, LN_EPS = 1e-6, 1e-5
RATE_MOBA_V, RATE_MOBA_O, RATE_EVEN, RATE_ODD, RATE_ODD_OUT = 0.65, 0.8, 0.7, 0.6, 1.1



def weight_plan():
    plan = []

    def f(tag, name, layer, c0, n=256, pad=None):
        plan.append((tag, "F", name, layer, [(c0, n)], pad or n, 8, 0))

    def t(tag, name, layer, c0, n, kts, per):
        for k in range(0, kts, per):
            plan.append((tag, "T", name, layer, [(c0, n)], n, per, k))

    def ffn(up_g, up_u, g0, u0, down, layer):
        for m in range(11):
            f("g", up_g, layer, g0 + 256 * m)
            f("u", up_u, layer, u0 + 256 * m)
        t("down", down, layer, 0, 1024, 22, 2)

    for m in range(4):
        f("c", "sc_w_in", 0, 1024 + 256 * m)
        f("v", "sc_w_in", 0, 2048 + 256 * m)
        f("b", "sc_w_in", 0, 256 * m)
    t("sc_out", "sc_w_out", 0, 0, 1024, 8, 2)
    ffn("ffn_w_up", "ffn_w_up", 0, FF, "ffn_w_down", 0)
    for half in range(2):
        for part in range(3):
            t("qkv", "moba_w_qkv", 0, 1024 * part + 512 * half, 512, 8, 4)
    t("moba_out", "moba_w_o", 0, 0, 1024, 8, 2)
    ffn("ffn_w_up", "ffn_w_up", 0, FF, "ffn_w_down", 1)

    f("dt", "even_w_in_2", 0, 3072, 16, 128)
    for m in range(6):
        f("xbc", "even_w_in_2", 0, 1536 + 256 * m)
    for m in range(2):
        f("pool", "even_w_in_2", 0, 256 * m)
    t("z", "even_w_in_2", 0, 512, 1024, 8, 2)
    t("even_out", "even_w_out_2", 0, 0, 1024, 12, 2)
    ffn("ffn_w_gate_2", "ffn_w_up_2", 0, 0, "ffn_w_down_2", 0)
    plan.append(("flkr", "F", "odd_w_in_2", 0, [(1536, 8), (2312, 32)], 128, 8, 0))
    for m in range(2):
        f("qf", "odd_w_in_2", 0, 256 * m)
    for m in range(2):
        f("kf", "odd_w_in_2", 0, 512 + 256 * m)
    t("ckv", "odd_w_in_2", 0, 2056, 256, 8, 8)
    t("cq", "odd_w_in_2", 0, 1544, 512, 8, 4)
    t("vf", "odd_w_in_2", 0, 1024, 512, 8, 4)
    t("ukv", "w_ukv_2", 0, 0, 1024, 2, 2)
    t("uq", "w_uq_2", 0, 0, 768, 4, 2)
    t("odd_out", "odd_w_out_2", 0, 0, 1024, 8, 2)
    ffn("ffn_w_gate_2", "ffn_w_up_2", 0, 0, "ffn_w_down_2", 1)
    return plan


VEC = {}
_n = 0
for _name, _cols in (("sc_w_conv", 24), ("ffn_w_conv", 264),
                     ("pool_scale_2", 4), ("conv_w_2", 48), ("conv_b_2", 12), ("ssm_norm_w_2", 8),
                     ("q_norm_w_2", 4), ("kv_norm_w_2", 2)):
    VEC[_name] = _n
    _n += _cols
NVEC = _n

CST = {}
_n = 0
for _name, _cols in (("ident", 128), ("uo", 256), ("gt", 128), ("mask", 256), ("rope", 128),
                     ("rope2", 64), ("cnt", 64)):
    CST[_name] = _n
    _n += _cols
NCST = _n


def constants():
    c = np.zeros((128, NCST), np.float32)
    i = np.arange(128)
    c[:, CST["ident"]:CST["ident"] + 128] = np.eye(128, dtype=np.float32)
    c[:, CST["uo"]:CST["uo"] + 128] = (i[:, None] <= i[None, :])
    c[:, CST["uo"] + 128:CST["uo"] + 256] = 1.0
    c[:, CST["gt"]:CST["gt"] + 128] = (i[:, None] > i[None, :])
    m = np.where(i[None, :] > i[:, None], np.float32(NEG), np.float32(0))
    c[:, CST["mask"]:CST["mask"] + 256] = np.concatenate([m, m], 1)
    for name, half in (("rope", 32), ("rope2", 16)):
        inv = np.power(np.float32(10000.0), -np.arange(half, dtype=np.float32) / np.float32(half),
                       dtype=np.float32)
        ang = np.arange(S, dtype=np.float32)[:, None] * inv[None, :]
        t = np.stack([np.cos(ang).reshape(2, 128, half), np.sin(ang).reshape(2, 128, half)], 1)
        c[:, CST[name]:CST[name] + 4 * half] = t.transpose(2, 0, 1, 3).reshape(128, 4 * half)
    for g in range(4):
        w = 2 << g
        c[:, CST["cnt"] + 16 * g:CST["cnt"] + 16 * g + 16] = (
            np.float32(1.0) / np.minimum(np.arange(16) + 1, w).astype(np.float32))
    return c




class Engine:

    def __init__(self, eng, sem):
        self.eng, self.sem, self.n, self.waited = eng, sem, 0, {}

    def wait(self, *points):
        for p in points:
            if isinstance(p, list):
                self.wait(*p)
            elif p is not None and self.waited.get(p[0].name, 0) < p[1]:
                self.waited[p[0].name] = p[1]
                self.eng.wait_ge(p[0], p[1])

    def do(self, fn, *points):
        self.wait(*points)
        self.n += 1
        fn().then_inc(self.sem, 1)
        return (self.sem, self.n)

    def quiet(self, fn, *points):
        self.wait(*points)
        fn()

    def dma(self, fn, sem, *points):
        self.wait(*points)
        fn().then_inc(sem[0], 16)
        sem[1] += 16
        return (sem[0], sem[1])


def build(nc, wts, vec, cst, rows, small, pw, x_in, out):
    plan = weight_plan()
    with ExitStack() as ctx:
        sem = lambda name: ctx.enter_context(nc.semaphore(name))
        base = (nc.sbuf_base + 63) // 64 * 64
        limit = nc.sbuf_usable_end

        P, A, V, G, SP = (Engine(e, sem(n)) for e, n in (
            (nc.tensor, "s_pe"), (nc.scalar, "s_act"), (nc.vector, "s_dve"), (nc.gpsimd, "s_pool"),
            (nc.sync, "s_sp")))
        names = [0]

        class Area:

            def __init__(self, start):
                self.at = start

            def take(self, shape, dt=F32):
                n = 4
                for d in shape[1:]:
                    n *= d
                names[0] += 1
                t = nc.alloc_sbuf_tensor_at(f"t{names[0]}", shape, dt, offset=self.at)
                self.at += (n + 31) // 32 * 32
                assert self.at <= limit, (self.at, limit)
                return t

        fixed = Area(base)
        wraw = fixed.take([128, NRAW, CW])
        wh = fixed.take([128, NHI, CW], F32R)
        wl = fixed.take([128, NLO, CW], F32R)
        X = fixed.take([128, 2, D])
        XN = fixed.take([128, 2, D])
        xt_at = [fixed.at, fixed.at + 8192]
        XTh = fixed.take([128, 8, S], F32R)
        XTl = fixed.take([128, 8, S], F32R)
        vecs = fixed.take([128, NVEC])
        cs_at = fixed.at
        cs = fixed.take([128, NCST])
        identr = Area(cs_at + 4 * CST["ident"]).take([128, 128], F32R)
        maskr = Area(cs_at + 4 * CST["mask"]).take([128, 256], F32R)
        sm = fixed.take([128, 56])
        grow = fixed.take([128, 1024])
        brow_at = fixed.at
        brow = fixed.take([128, 1024])
        st = fixed.take([128, 64])
        mhalf = fixed.take([128, 2])
        mix_base = fixed.at

        ps = ctx.enter_context(nc.psum_tensor("ps", [128, 8, 512], F32))
        free = [[] for _ in range(8)]

        class Ring:
            def __init__(self, banks):
                self.banks, self.i = banks, 0

            def take(self):
                b = self.banks[self.i % len(self.banks)]
                self.i += 1
                return b

        f_ring = Ring([4, 5, 6, 7])
        bg_ring = Ring([6, 7])

        ident = identr[:].bitcast(F32)
        UO = cs[:, CST["uo"]:CST["uo"] + 256]
        U = cs[:, CST["uo"]:CST["uo"] + 128]
        GT = cs[:, CST["gt"]:CST["gt"] + 128]
        MASK = cs[:, CST["mask"]:CST["mask"] + 256]
        ROPE = cs[:, CST["rope"]:CST["rope"] + 128].rearrange("p (t c d) -> p t c d", t=2, c=2)
        ROPE2 = cs[:, CST["rope2"]:CST["rope2"] + 64].rearrange("p (t c d) -> p t c d", t=2, c=2)

        def vcol(name, i, j=0):
            return vecs[:, VEC[name] + i + j:VEC[name] + i + j + 1]

        sem_in = [sem("s_in"), 0]
        sem_id = [sem("s_id"), 0]
        sem_x = [sem("s_x"), 0]
        x_loaded = [SP.dma(lambda t=t: nc.sync.dma_start(X[:, t, :], x_in[0, t * 128:(t + 1) * 128, :]),
                           s_) for t, s_ in ((0, sem_x), (1, [sem("s_x1"), 0]))]
        half = V.do(lambda: nc.vector.memset(mhalf[:], -0.5))
        sem_row = [sem("s_row"), 0]

        class Weights:
            def __init__(self):
                self.sems = [[sem(f"s_w{i}"), 0] for i in range(NRAW)]
                self.raw, self.hi, self.lo, self.used = [], [], [], []
                self.i, self.pumped = 0, 0

            def start(self):
                for i in range(NLO):
                    self.split_hi(i)
                    self.split_lo(i)
                for i in range(NLO, NHI):
                    self.split_hi(i)

            def width(self, i):
                return plan[i][5] * plan[i][6]

            def load(self, i):
                if i >= len(plan):
                    return
                w, k = self.width(i), i % NRAW
                old = [self.hi[i - NRAW], self.lo[i - NRAW]] if i >= NRAW else []
                self.raw.append(SP.dma(lambda: nc.sync.dma_start(wraw[:, k, 0:w], wts[i, :, 0:w]),
                                       self.sems[k], *old))

            def split_hi(self, i):
                if i >= len(plan):
                    return
                w, r, k = self.width(i), i % NRAW, i % NHI
                old = self.used[i - NHI] if i >= NHI else None
                self.hi.append(A.do(lambda: nc.scalar.copy(wh[:, k, 0:w], wraw[:, r, 0:w]),
                                    self.raw[i], old))

            def split_lo(self, i):
                if i >= len(plan):
                    return
                w, r, h, k = self.width(i), i % NRAW, i % NHI, i % NLO
                old = self.used[i - NLO] if i >= NLO else None
                self.lo.append(V.do(lambda: nc.vector.tensor_tensor(
                    wl[:, k, 0:w], wraw[:, r, 0:w], wh[:, h, 0:w].bitcast(F32), ALU.subtract),
                    self.hi[i], old))
                self.load(i + NRAW)

            def use(self, tag):
                i = self.i
                assert plan[i][0] == tag, (plan[i][0], tag)
                n, kk = plan[i][5], plan[i][6]
                view = lambda t, m: t[:, i % m, 0:n * kk].rearrange("p (k n) -> p k n", k=kk)
                self.i += 1
                return view(wh, NHI), view(wl, NLO), self.lo[i]

            def done(self, point, n=1):
                self.used += [point] * n

            def pump(self):
                if self.pumped < len(self.used):
                    self.split_hi(self.pumped + NHI)
                    self.split_lo(self.pumped + NLO)
                    self.pumped += 1

        W = Weights()

        def mm(o, a, b, start, stop):
            return lambda: nc.tensor.matmul(o, a, b, start=start, stop=stop)

        class Background:

            def __init__(self):
                self.tasks, self.rate, self.due, self.clock = [], 0.0, 0.0, 0.0

            def step(self):
                for task in list(self.tasks):
                    try:
                        if not next(task):
                            self.clock += 1.5
                            return True
                    except StopIteration:
                        self.tasks.remove(task)
                return False

            def tick(self, us):
                self.clock += us
                self.due += self.rate * us
                while self.due >= 1:
                    self.due -= 1
                    if not self.step():
                        self.due = 0

            def lag(self, us):
                end = self.clock + us
                while self.clock < end:
                    yield True

            def until(self, cond):
                n = 0
                while not cond():
                    if not self.step():
                        self.clock += 1.0
                        n += 1
                        assert n < 1000

            def finish(self):
                self.until(lambda: not self.tasks)
                self.rate = self.due = 0.0

        bg = Background()

        def f_chunk(tag, nblk, xready):
            H, L, ready = W.use(tag)
            b = f_ring.take()
            P.wait(ready, free[b])
            for blk in range(nblk):
                o = ps[:, b, blk * S:(blk + 1) * S]
                c = slice(blk * 128, (blk + 1) * 128)
                for k0 in (0, 4):
                    for kt in range(k0, k0 + 4):
                        P.quiet(mm(o, H[:, kt, c], XTh[:, kt, :], kt == 0, False), xready(kt, False))
                        P.quiet(mm(o, L[:, kt, c], XTh[:, kt, :], False, False))
                    for kt in range(k0, k0 + 4):
                        m = mm(o, H[:, kt, c], XTl[:, kt, :], False, kt == 7)
                        if kt == 7 and blk == nblk - 1:
                            point = P.do(m, xready(kt))
                        else:
                            P.quiet(m, xready(kt))
                if blk < nblk - 1:
                    bg.tick(2.6)
            W.done(point)
            return b, point

        HALVES = [(0, 512), (512, 1024)]

        def t_part(parts, hi, lo, t, js, dst, bank, xready):
            tt = slice(t * 128, (t + 1) * 128)
            for H, L, k, kt, cols, first, last in parts:
                P.wait(xready(kt))
                for n, (a, w) in enumerate(((hi, H), (hi, L), (lo, H))):
                    for j in js:
                        if first and n == 0:
                            P.wait(free[bank(t, j)])
                        m = mm(dst(t, j), a(kt)[:, tt], w[:, k, cols[j][0]:cols[j][1]], first and n == 0,
                               last and n == 2)
                        if n == 2 and j == js[-1]:
                            point = P.do(m)
                        else:
                            P.quiet(m)
            return point

        def t_proj(tag, nchunks, hi, lo, cols, dst, bank, xready, per=2, end=None):
            js = list(range(len(cols)))
            body = nchunks - 2 if end else nchunks
            us = sum(c[1] - c[0] for c in cols) * 1.3e-3
            for i in range(body):
                H, L, ready = W.use(tag)
                P.wait(ready)
                for k in range(per):
                    kt = i * per + k
                    for t in range(2):
                        point = t_part([(H, L, k, kt, cols, kt == 0, kt == nchunks * per - 1)], hi, lo, t,
                                       js, dst, bank, xready)
                        if (k, t) != (per - 1, 1):
                            bg.tick(us)
                W.done(point)
                W.pump()
                bg.tick(us)
            if not end:
                return {(t, j): point for t in range(2) for j in js}
            parts = []
            for i in range(body, nchunks):
                H, L, ready = W.use(tag)
                parts += [(H, L, k, i * per + k, cols, i * per + k == 0, i * per + k == nchunks * per - 1)
                          for k in range(per)]
            P.wait(ready)
            for t, j in ((0, 0), (0, 1), (1, 0)):
                end.got(t, j, t_part(parts, hi, lo, t, [j], dst, bank, xready))
            for n, part in enumerate(parts):
                point = t_part([part], hi, lo, 1, [1], dst, bank, xready)
                if n in TURN_AT:
                    end.turn(0, TURN_AT.index(n))
            end.got(1, 1, point)
            W.done(point, 2)
            W.pump()
            W.pump()
            return end.xready

        mask_done = []

        def acc(t, j):
            return ps[:, 2 * t + j, :]

        def acc_bank(t, j):
            return 2 * t + j

        def split_out(src, hi, lo, scale, *points):
            return split_bank([(src, hi, lo, scale)], *points)[0]

        def split_bank(parts, *points):
            for src, hi, lo, scale in parts:
                if scale is None:
                    a = A.do(lambda: nc.scalar.copy(hi, src), *points)
                else:
                    a = A.do(lambda: nc.scalar.activation(hi, src, ACT.Copy, scale=scale), *points)
            done = []
            for src, hi, lo, scale in parts:
                if scale is None:
                    done.append(V.do(lambda: nc.vector.tensor_tensor(
                        lo, src, hi.bitcast(F32), ALU.subtract), a, *points))
                else:
                    done.append(V.do(lambda: nc.vector.scalar_tensor_tensor(
                        out=lo, in0=src, scalar=scale, in1=hi.bitcast(F32), op0=ALU.mult,
                        op1=ALU.subtract), a, *points))
            return done

        def to_feature(src, nkt, hi, lo, scale, ready):
            points = []
            for k0 in range(0, nkt, 2):
                b = bg_ring.take()
                P.wait(free[b])
                for kt in (k0, k0 + 1):
                    for t in range(2):
                        o = ps[:, b, (kt - k0) * S + t * 128:(kt - k0) * S + (t + 1) * 128]
                        fn = lambda: nc.tensor.transpose(o, src(t, kt), ident)
                        if kt == k0 + 1 and t == 1:
                            p = P.do(fn, ready[t])
                        else:
                            P.quiet(fn, ready[t])
                points += split_bank(
                    [(ps[:, b, (kt - k0) * S:(kt - k0 + 1) * S], hi(kt), lo(kt), scale(kt))
                     for kt in (k0, k0 + 1)], p)
                free[b] = [points[-1]]
                yield
            return points

        def xt(t_):
            return lambda kt: t_[:, kt, :]

        def fill(parts, *points):
            done = []
            for dst, value in parts:
                done.append(G.do(lambda: nc.gpsimd.memset(dst, value), *points, *done[-1:]))
            return done

        def pow_rms(c, *points):
            return G.do(lambda: nc.gpsimd.tensor_tensor(c, c, mhalf[:, 0:1], ALU.pow), half, *points)

        def rms(src, dst, n, col, points):
            done = []
            for t in range(2):
                c = st[:, col + t:col + t + 1]
                a = A.do(lambda: nc.scalar.activation(dst(t), src(t), ACT.Square, accum_out=c), points[t])
                v = V.do(lambda: nc.vector.tensor_scalar(c, c, 1.0 / n, RMS_EPS, ALU.mult, ALU.add), a)
                g = pow_rms(c, v)
                done.append(V.do(lambda: nc.vector.tensor_scalar(dst(t), src(t), c, None, ALU.mult), g))
            return done

        rows_at = [0]

        def load_rows(n, *points):
            for dst in (grow, brow)[:n]:
                i = rows_at[0]
                rows_at[0] += 1
                p = SP.dma(lambda: nc.sync.dma_start(
                    dst[:], rows[i:i + 1, :].partition_broadcast(128)), sem_row, *points)
            return p

        class Boundary:

            def __init__(self, n_rows, after=None, store=None):
                self.store, self.v, self.h, self.r, self.g, self.done = store, {}, {}, {}, {}, []
                self.rp = load_rows(n_rows, after)

            def turn(self, t, j):
                if self.store:
                    return
                b = 4 + 2 * t + j
                P.wait(free[b])
                src = self.dst[:, t, j * 512:(j + 1) * 512]
                for i in range(4):
                    fn = lambda: nc.tensor.transpose(ps[:, b, i * 128:(i + 1) * 128],
                                                     src[:, i * 128:(i + 1) * 128], ident)
                    if i == 3:
                        p = P.do(fn, self.v[t, j])
                    else:
                        P.quiet(fn, self.v[t, j])
                self.h[t, j] = A.do(lambda: nc.scalar.copy(self.xt(XTh, t, j), self.turned(t, j)), p)

            def turned(self, t, j):
                return ps[:, 4 + 2 * t + j, :].rearrange("p (k s) -> p k s", k=4)

            def xt(self, x, t, j):
                return x[:, 4 * j:4 * j + 4, t * 128:(t + 1) * 128]

            def rest(self, t, j):
                if self.store:
                    return
                v = V.do(lambda: nc.vector.tensor_tensor(
                    self.xt(XTl, t, j), self.turned(t, j), self.xt(XTh, t, j).bitcast(F32),
                    ALU.subtract), self.h[t, j])
                self.r[t, j] = v
                free[4 + 2 * t + j] = [v]

            def xready(self, kt, lo=True):
                r = self.r if lo else self.h
                return [r[0, kt // 4], r[1, kt // 4]]

            def got(self, t, j, point):
                self.add(t, j, point)
                if (t, j) == (1, 1):
                    P.wait(mask_done)
                    for _ in range(N_WARM):
                        P.quiet(mm(ps[:, 6, 0:256], identr[:], maskr[:], True, True), free[6])
                if (t, j) == (0, 1):
                    self.stats(0)
                    self.norm(0, 0)
                    self.norm(0, 1)
                    self.done.append(self.v[0, 1])
                elif (t, j) == (1, 1):
                    self.last()
                    self.done.append(self.v[1, 1])

            def open(self, identity):
                for t in range(2):
                    for j in range(2):
                        self.add(t, j, None)
                    self.stats(t)
                P.wait(A.do(lambda: nc.scalar.copy(identr[:], cs[:, CST["ident"]:CST["ident"] + 128]),
                            identity))
                for t in range(2):
                    for j in range(2):
                        self.norm(t, j)
                        self.turn(t, j)
                    self.done.append(self.v[t, 1])
                for t in range(2):
                    for j in range(2):
                        self.rest(t, j)

        class RmsNorm(Boundary):

            def __init__(self, dst, after=None):
                super().__init__(1, after)
                self.dst = dst

            def add(self, t, j, point):
                c = st[:, 4 * t + j:4 * t + j + 1]
                xs = X[:, t, j * 512:(j + 1) * 512]
                b, v = acc_bank(t, j), None
                if point is not None:
                    v = V.do(lambda: nc.vector.tensor_tensor(xs, acc(t, j), xs, ALU.add), point)
                a = A.do(lambda: nc.scalar.activation(ps[:, b, :], xs, ACT.Square, accum_out=c), v,
                         x_loaded[t])
                free[b] = [a]
                if j == 0:
                    self.half = V.do(lambda: nc.vector.tensor_scalar(c, c, 1.0 / D, RMS_EPS, ALU.mult,
                                                                     ALU.add), a)
                self.a = a

            def stats(self, t):
                c = [st[:, 4 * t + i:4 * t + i + 1] for i in range(2)]
                v = V.do(lambda: nc.vector.scalar_tensor_tensor(
                    out=c[1], in0=c[1], scalar=1.0 / D, in1=c[0], op0=ALU.mult, op1=ALU.add), self.a,
                    self.half)
                self.g[t] = pow_rms(c[1], v)

            def norm(self, t, j):
                sl = slice(j * 512, (j + 1) * 512)
                c = st[:, 4 * t + 1:4 * t + 2]
                self.v[t, j] = V.do(lambda: nc.vector.scalar_tensor_tensor(
                    out=self.dst[:, t, sl], in0=X[:, t, sl], scalar=c, in1=grow[:, sl], op0=ALU.mult,
                    op1=ALU.mult), self.g[t], self.rp)

            def last(self):
                self.rest(0, 0)
                self.stats(1)
                self.rest(0, 1)
                for j in range(2):
                    self.norm(1, j)
                    self.turn(1, j)
                self.rest(1, 0)
                self.rest(1, 1)

        class LayerNorm(Boundary):

            def __init__(self, after=None, store=None):
                super().__init__(2, after, store)
                self.dst = X

            def add(self, t, j, point):
                xs, rs = (x[:, t, j * 512:(j + 1) * 512] for x in (X, XN))
                o = st[:, 16 * t + 6 * j:16 * t + 6 * j + 6]
                v = V.do(lambda: nc.vector.scalar_tensor_tensor(
                    out=rs, in0=xs, scalar=ALPHA, in1=acc(t, j), op0=ALU.mult, op1=ALU.add), point)
                free[acc_bank(t, j)] = [v]
                self.s = V.do(lambda: nc.vector.bn_stats(out=o, in_=rs), v)

            def stats(self, t):
                o = st[:, 16 * t:16 * t + 12]
                self.mean, self.sq = (st[:, 16 * t + i:16 * t + i + 1] for i in (12, 13))
                v = V.do(lambda: nc.vector.bn_aggr(out=st[:, 16 * t + 12:16 * t + 14], in_=o), self.s)
                self.m = v
                v = V.do(lambda: nc.vector.tensor_scalar(self.sq, self.sq, LN_EPS, None, ALU.add), v)
                self.g[t] = pow_rms(self.sq, v)

            def last(self):
                self.stats(1)
                for j in range(2):
                    self.norm(1, j)
                    self.turn(1, j)
                for j in range(2):
                    self.rest(0, j)
                    self.rest(1, j)

            def norm(self, t, j):
                sl = slice(j * 512, (j + 1) * 512)
                xs, rs = X[:, t, sl], XN[:, t, sl]
                v = V.do(lambda: nc.vector.scalar_tensor_tensor(
                    out=xs, in0=rs, scalar=self.mean, in1=grow[:, sl], op0=ALU.subtract, op1=ALU.mult),
                    self.m, self.rp)
                v = V.do(lambda: nc.vector.scalar_tensor_tensor(
                    out=xs, in0=xs, scalar=self.sq, in1=brow[:, sl], op0=ALU.mult, op1=ALU.add), v, self.g[t])
                self.v[t, j] = v
                if self.store:
                    self.store(t, j, v)

        def conv(src, dst, name, col, stride, taps, bias, *points):
            for blk in range(2):
                sl = slice(blk * S, (blk + 1) * S)
                w = vcol(name, col + blk + (taps - 1) * stride)
                if bias is None:
                    a = A.do(lambda: nc.scalar.activation(dst[:, sl], src[:, sl], ACT.Copy, scale=w),
                             *points)
                else:
                    a = A.do(lambda: nc.scalar.activation(dst[:, sl], src[:, sl], ACT.Identity, scale=w,
                                                          bias=vcol(*bias, blk)), *points)
            v = [a, a]
            for s_ in range(1, taps):
                for blk in range(2):
                    w = vcol(name, col + blk + (taps - 1 - s_) * stride)
                    o = dst[:, blk * S + s_:(blk + 1) * S]
                    v[blk] = V.do(lambda: nc.vector.scalar_tensor_tensor(
                        out=o, in0=src[:, blk * S:(blk + 1) * S - s_], scalar=w, in1=o, op0=ALU.mult,
                        op1=ALU.add), v[blk], *points)
            return v

        ffn_area = Area(mix_base)
        HTh = ffn_area.take([128, 22, S], F32R)
        HTl = ffn_area.take([128, 22, S], F32R)
        yg = ffn_area.take([128, 2, 512])
        yu = ffn_area.take([128, 2, 512])
        sg = ffn_area.take([128, 2, 512])

        def ffn(layer, with_conv, xready, end):
            ready = {}
            yg_read, yu_read, sg_read = [None, None], [None, None], [None, None]

            def product(k, m, a, v):
                v = V.do(lambda: nc.vector.tensor_tensor(yu[:, k, :], usrc, sg[:, k, :], ALU.mult), v, a,
                         yu_read[k])
                sg_read[k] = v
                h2, l2 = (t_[:, 2 * m:2 * m + 2, :].rearrange("p k s -> p (k s)") for t_ in (HTh, HTl))
                yu_read[k] = ready[2 * m] = ready[2 * m + 1] = split_out(yu[:, k, :], h2, l2, None, v)
                return v

            for m in range(11):
                k = m % 2
                b, p = f_chunk("g", 2, xready)
                if with_conv:
                    v = conv(ps[:, b, :], yg[:, k, :], "ffn_w_conv", 132 * layer + 2 * m, 44, 3, None, p,
                             yg_read[k])
                    free[b] = v
                    W.pump()
                    a = A.do(lambda: nc.scalar.activation(sg[:, k, :], yg[:, k, :], ACT.Silu), v,
                             sg_read[k])
                    yg_read[k] = a
                else:
                    a = A.do(lambda: nc.scalar.activation(sg[:, k, :], ps[:, b, :], ACT.Silu), p,
                             sg_read[k])
                    free[b] = [a]
                    W.pump()
                b, p = f_chunk("u", 2, xready)
                if with_conv:
                    v = conv(ps[:, b, :], yu[:, k, :], "ffn_w_conv", 132 * layer + 22 + 2 * m, 44, 3, None,
                             p, yu_read[k])
                    usrc, free[b] = yu[:, k, :], v
                    W.pump()
                    product(k, m, a, v)
                else:
                    usrc = ps[:, b, :]
                    free[b] = [product(k, m, a, p)]
                    W.pump()
            return t_proj("down", 11, xt(HTh), xt(HTl), HALVES, acc, acc_bank, lambda kt: ready[kt],
                          end=end)

        def value_of(vp, h, kt):
            return vp[:, kt, h // 2, 64 * (h % 2):64 * (h % 2) + 128]

        def value_columns(vp, t, pairs):
            v = vp[:, t, pairs, :]
            return v.rearrange("p h (c d) -> p h c d", d=64)[:, :, 0:3:2, :]

        def attention(n, scale, q_of, k_of, v_of, oh, ol, area, ready, vready, outs, prob=4, turned=3):
            Pb = area.take([128, prob, 384])
            PT = area.take([128, turned, 384])
            sc = area.take([128, prob, 8])
            normed, exps, trs, pvs = {}, {}, {}, {}

            def scores(h):
                k, b = h % prob, 4 + h % 2
                P.wait(free[b], ready(h))
                P.quiet(mm(ps[:, b, 0:256], identr[:], maskr[:], True, False))
                for c, tq, tk in ((0, 0, 0), (1, 1, 1), (2, 1, 0)):
                    m = mm(ps[:, b, c * 128:(c + 1) * 128], q_of(h)[:, tq * 128:(tq + 1) * 128],
                           k_of(h)[:, tk * 128:(tk + 1) * 128], c == 2, c > 0)
                    if c == 2:
                        p = P.do(m)
                    else:
                        P.quiet(m)
                V.do(lambda: nc.vector.reduce_max(sc[:, k, 0:1], ps[:, b, 0:128], AX_X), p,
                     normed.get(h - prob))
                v = V.do(lambda: nc.vector.reduce_max(sc[:, k, 1:2], ps[:, b, 128:384], AX_X))
                v = V.do(lambda: nc.vector.tensor_scalar(sc[:, k, 2:4], sc[:, k, 0:2], -scale, None,
                                                         ALU.mult), v)
                A.do(lambda: nc.scalar.activation(Pb[:, k, 0:128], ps[:, b, 0:128], ACT.Exp,
                                                  bias=sc[:, k, 2:3], scale=scale,
                                                  accum_out=sc[:, k, 4:5]), v, trs.get(h - prob))
                exps[h] = A.do(lambda: nc.scalar.activation(
                    Pb[:, k, 128:384], ps[:, b, 128:384], ACT.Exp, bias=sc[:, k, 3:4], scale=scale,
                    accum_out=sc[:, k, 5:6]))
                free[b] = [exps[h]]

            def normalise(h):
                k = h % prob
                v = V.do(lambda: nc.vector.reciprocal(sc[:, k, 6:8], sc[:, k, 4:6]), exps[h])
                V.do(lambda: nc.vector.tensor_scalar(Pb[:, k, 0:128], Pb[:, k, 0:128], sc[:, k, 6:7],
                                                     None, ALU.mult), v)
                normed[h] = V.do(lambda: nc.vector.tensor_scalar(
                    Pb[:, k, 128:384], Pb[:, k, 128:384], sc[:, k, 7:8], None, ALU.mult), v)

            def turn(h):
                k, k2, b = h % prob, h % turned, 6
                P.wait(free[b], normed[h])
                for c, src in ((0, 0), (1, 2), (2, 1)):
                    fn = lambda: nc.tensor.transpose(
                        ps[:, b, c * 128:(c + 1) * 128], Pb[:, k, src * 128:(src + 1) * 128], ident)
                    if c == 2:
                        trs[h] = P.do(fn)
                    else:
                        P.quiet(fn)
                a = A.do(lambda: nc.scalar.copy(PT[:, k2, :], ps[:, b, 0:384]), trs[h],
                         pvs.get(h - turned))
                free[b] = [a]
                return a

            def values(h, a):
                k2, b = h % turned, 7
                if h % 2 == 0:
                    P.wait(free[b], vready(h))
                P.quiet(mm(ps[:, b, 0:256], v_of(h, 0), PT[:, k2, 0:256], h % 2 == 0, False), a)
                pvs[h] = P.do(mm(ps[:, b, 128:256], v_of(h, 1), PT[:, k2, 256:384], False, h % 2 == 1))
                if h % 2 == 1:
                    outs[h // 2] = split_out(ps[:, b, 0:256], oh(h // 2), ol(h // 2), None, pvs[h])
                    free[b] = [outs[h // 2]]

            copied = {}
            for i in range(n + 6):
                if 1 <= i < n + 1:
                    normalise(i - 1)
                if 3 <= i < n + 3:
                    copied[i - 3] = turn(i - 3)
                if 5 <= i < n + 5:
                    while not vready(i - 5):
                        yield True
                    values(i - 5, copied[i - 5])
                if i < n:
                    while not ready(i):
                        yield True
                    scores(i)
                yield

        def rope_half(src, dst, heads, half, tab, t, points, tmp, tmp_free):
            x1, x2 = src[:, :, 0:half], src[:, :, half:2 * half]
            o1, o2 = dst[:, :, 0:half], dst[:, :, half:2 * half]
            cos = tab[:, t, 0, :].unsqueeze(1).to_broadcast([128, heads, half])
            sin = tab[:, t, 1, :].unsqueeze(1).to_broadcast([128, heads, half])
            t1, t2 = tmp[0][:, 0:heads, :], tmp[1][:, 0:heads, :]
            V.do(lambda: nc.vector.tensor_tensor(t1, x2, sin, ALU.mult), *points, tmp_free)
            V.do(lambda: nc.vector.tensor_tensor(o1, x1, cos, ALU.mult))
            V.do(lambda: nc.vector.tensor_tensor(t2, x1, sin, ALU.mult))
            v = V.do(lambda: nc.vector.tensor_tensor(o2, x2, cos, ALU.mult))
            V.do(lambda: nc.vector.tensor_tensor(o1, o1, t1, ALU.subtract), v)
            return V.do(lambda: nc.vector.tensor_tensor(o2, o2, t2, ALU.add))

        def short_conv(xready, end):
            area = Area(mix_base)
            Mh, Ml = area.take([128, 8, S], F32R), area.take([128, 8, S], F32R)
            cS, cv, y, prod = (area.take([128, 2, 512]) for _ in range(4))
            ready, prod_read = {}, [None, None]
            for m in range(4):
                k = m % 2
                b, p = f_chunk("c", 2, xready)
                a = A.do(lambda: nc.scalar.copy(cS[:, k, :], ps[:, b, :]), p, prod_read[k])
                free[b] = [a]
                W.pump()
                b, p = f_chunk("v", 2, xready)
                v = V.do(lambda: nc.vector.tensor_tensor(cv[:, k, :], ps[:, b, :], cS[:, k, :], ALU.mult),
                         a, p, prod_read[k])
                free[b] = [v]
                W.pump()
                c = conv(cv[:, k, :], y[:, k, :], "sc_w_conv", 2 * m, 8, 3, None, v, prod_read[k])
                b, p = f_chunk("b", 2, xready)
                v = V.do(lambda: nc.vector.tensor_tensor(prod[:, k, :], ps[:, b, :], y[:, k, :], ALU.mult),
                         c, p, prod_read[k])
                free[b] = [v]
                h2, l2 = (t_[:, 2 * m:2 * m + 2, :].rearrange("p k s -> p (k s)") for t_ in (Mh, Ml))
                v = split_out(prod[:, k, :], h2, l2, None, v)
                prod_read[k] = v
                ready[2 * m] = ready[2 * m + 1] = v
                W.pump()
            return t_proj("sc_out", 4, xt(Mh), xt(Ml), HALVES, acc, acc_bank, lambda kt: ready[kt],
                          end=end)

        def moba(xready, end):
            area = Area(mix_base)
            qT = area.take([128, 8, S])
            kT = area.take([128, 2, 8, S])
            vp = area.take([128, 2, 8, 192])
            rot = Area(brow_at)
            tmp = [rot.take([128, 8, 32]) for _ in range(2)]
            Mh, Ml = area.take([128, 4, S], F32R), area.take([128, 4, S], F32R)
            oh = lambda kt: (Mh if kt < 4 else XTh)[:, kt, :]
            ol = lambda kt: (Ml if kt < 4 else XTl)[:, kt, :]
            z = fill([(kT[64:128, 0], 0.0), (kT[0:64, 1], 0.0), (vp[:, :, :, 64:128], 0.0)], xready(7))
            turned, vready, outs, state = {}, {}, {}, {"tf": None}

            def rope_turn(points, bank0, half, is_q):
                dst = XN[:, :, (0 if is_q else 512):(512 if is_q else 1024)]
                for t in range(2):
                    src = ps[:, bank0 + t, :].rearrange("p (h d) -> p h d", d=64)
                    v = rope_half(src, dst[:, t, :].rearrange("p (h d) -> p h d", d=64), 8, 32, ROPE, t,
                                  [points[t, 0], turned.get((half - 1, is_q))], tmp, state["tf"])
                    state["tf"] = v
                    free[bank0 + t] = [v]
                    yield
                yield from bg.lag(LAG_ROPE)
                for i0 in range(0, 4, 2):
                    b = 6
                    P.wait(free[b], v)
                    for i in (i0, i0 + 1):
                        for t in range(2):
                            o = ps[:, b, (i - i0) * S + t * 128:(i - i0) * S + (t + 1) * 128]
                            p = P.do(lambda: nc.tensor.transpose(o, dst[:, t, i * 128:(i + 1) * 128],
                                                                 ident))
                    s3 = ps[:, b, :].rearrange("p (a b) -> p a b", a=2)
                    i1 = 4 * half + i0
                    if is_q:
                        done = A.do(lambda: nc.scalar.copy(qT[:, i1:i1 + 2, :], s3), p)
                    else:
                        A.do(lambda: nc.scalar.copy(kT[0:64, 0, i1:i1 + 2, :], s3[0:64]), p, *z)
                        done = A.do(lambda: nc.scalar.copy(kT[64:128, 1, i1:i1 + 2, :], s3[64:128]))
                    free[b] = [done]
                    yield
                turned[half, is_q] = done

            def ready(h):
                p = [turned.get((h // 8, is_q)) for is_q in (True, False)]
                return p if all(p) else None

            att = attention(16, 0.125, lambda h: qT[:, h // 2, :], lambda h: kT[:, h % 2, h // 2, :],
                            lambda h, kt: value_of(vp, h, kt), oh, ol, area, ready,
                            lambda h: vready.get(h // 8), outs)
            bank0 = 0
            for half in range(2):
                for is_q in (True, False):
                    p = t_proj("qkv", 2, xt(XTh), xt(XTl), [(0, 512)], lambda t, j: ps[:, bank0 + t, :],
                               lambda t, j: bank0 + t, xready, per=4)
                    bg.tasks.insert(half * (not is_q), rope_turn(p, bank0, half, is_q))
                    if half == 0 and not is_q:
                        bg.tasks.append(att)
                    bg.rate = RATE_MOBA_V
                    bank0 = 2 - bank0
                p = t_proj("qkv", 2, xt(XTh), xt(XTl), [(0, 512)], lambda t, j: ps[:, bank0 + t, :],
                           lambda t, j: bank0 + t, xready, per=4)
                for t in range(2):
                    v = A.do(lambda: nc.scalar.copy(
                        value_columns(vp, t, slice(4 * half, 4 * half + 4)),
                        ps[:, bank0 + t, :].rearrange("p (h c d) -> p h c d", c=2, d=64)), p[t, 0], *z)
                    free[bank0 + t] = [v]
                vready[half] = [v]
                bank0 = 2 - bank0
            bg.rate = RATE_MOBA_O

            def oready(kt):
                bg.until(lambda: min(kt + 1, 7) in outs)
                return outs[kt]

            t_proj("moba_out", 4, oh, ol, HALVES, acc, acc_bank, oready, end=end)
            bg.finish()

        def log1pexp(x, area, n, *points):
            e, u, d, z, l = (area.take([128, n]) for _ in range(5))
            v = V.do(lambda: nc.vector.tensor_scalar(e[:], x, -1.0, None, ALU.mult), *points)
            v = V.do(lambda: nc.vector.tensor_tensor(e[:], e[:], x, ALU.min), v)
            a = A.do(lambda: nc.scalar.activation(e[:], e[:], ACT.Exp), v)
            v = V.do(lambda: nc.vector.tensor_scalar(u[:], e[:], 1.0, None, ALU.add), a)
            a = A.do(lambda: nc.scalar.activation(l[:], u[:], ACT.Ln), v)
            v = V.do(lambda: nc.vector.tensor_scalar(d[:], u[:], -1.0, None, ALU.add), v)
            v = V.do(lambda: nc.vector.tensor_scalar(z[:], d[:], 0.0, None, ALU.is_equal), v)
            v = V.do(lambda: nc.vector.tensor_tensor(d[:], d[:], z[:], ALU.add), v)
            v = V.do(lambda: nc.vector.reciprocal(d[:], d[:]), v)
            v = V.do(lambda: nc.vector.tensor_tensor(d[:], d[:], e[:], ALU.mult), v)
            v = V.do(lambda: nc.vector.tensor_tensor(l[:], l[:], z[:], ALU.add), a, v)
            v = V.do(lambda: nc.vector.tensor_tensor(l[:], l[:], d[:], ALU.mult), v)
            return l, v

        def even(xready, end):
            area = Area(mix_base)
            xzS = area.at
            xb = area.take([128, 12, S])
            zS = Area(xzS).take([128, 2, D])
            xd_at = area.at
            Ph, Pl = area.take([128, 4, S], F32R), area.take([128, 4, S], F32R)
            xdec = Area(xd_at).take([128, D])
            xtok, xdt = (area.take([128, 2, D]) for _ in range(2))
            prev = area.take([128, D])
            Btok, CBm = area.take([128, 256]), area.take([128, 4, 128])
            gda, ex = area.take([128, 2, 4, 128]), area.take([128, 2, 4, 128])
            pwt = area.take([128, 4, 128])
            dtT = area.take([16, S])
            dt_, da, E1, D0 = (area.take([128, n]) for n in (32, 32, 16, 16))
            ah = area.take([128, 16])
            y = XN
            us = XN[:, 1, :].rearrange("p (g s) -> p g s", g=4)
            sem_p = [sem("s_pw"), 0]
            pwl = SP.dma(lambda: nc.sync.dma_start(pwt[:], pw), sem_p, xready(7))
            ready = {}
            two = lambda ap: ap.unsqueeze(1).to_broadcast([128, 2, 16])
            v3 = lambda t_: t_[:].rearrange("p (t e) -> p t e", t=2)
            bc = lambda ap, n=64: ap.unsqueeze(2).to_broadcast([128, ap.shape[1], n])
            by = lambda ap: ap.rearrange("p (e d) -> p e d", d=64)
            f_ring.banks = [4, 5]
            bg_ring.banks = [6, 7]
            st_ = {}

            b, p = f_chunk("dt", 1, xready)
            adt = A.do(lambda: nc.scalar.copy(dtT[:], ps[0:16, b, 0:S]), p)
            free[b] = [adt]
            W.pump()

            def dt_task():
                b = bg_ring.take()
                P.wait(adt, free[b])
                P.quiet(lambda: nc.tensor.transpose(ps[:, b, 0:16], dtT[:, 0:128], ident[0:16, 0:16]))
                p = P.do(lambda: nc.tensor.transpose(ps[:, b, 16:32], dtT[:, 128:256], ident[0:16, 0:16]))
                v = V.do(lambda: nc.vector.tensor_tensor(v3(da), ps[:, b, 0:32].rearrange(
                    "p (t e) -> p t e", t=2), two(sm[:, 0:16]), ALU.add), p)
                free[b] = [v]
                l, v2 = log1pexp(da[:], area, 32, v)
                v = V.do(lambda: nc.vector.tensor_scalar(dt_[:], da[:], 0.0, None, ALU.max), v2)
                v = V.do(lambda: nc.vector.tensor_tensor(dt_[:], dt_[:], l[:], ALU.add), v)
                a = A.do(lambda: nc.scalar.activation(ah[:], sm[:, 16:32], ACT.Exp))
                st_["dready"] = V.do(lambda: nc.vector.scalar_tensor_tensor(
                    out=v3(da), in0=v3(dt_), scalar=-1.0, in1=two(ah[:]), op0=ALU.mult, op1=ALU.mult),
                    v, a)
                yield

            bg.tasks.append(dt_task())
            bg.rate = 1.0
            for m in range(6):
                b, p = f_chunk("xbc", 2, xready)
                v = conv(ps[:, b, :], xb[:, 2 * m:2 * m + 2, :].rearrange("p a b -> p (a b)"), "conv_w_2",
                         2 * m, 12, 4, ("conv_b_2", 2 * m), p)
                free[b] = v
                W.pump()
                st_["xb"] = A.do(lambda: nc.scalar.activation(
                    xb[:, 2 * m:2 * m + 2, :], xb[:, 2 * m:2 * m + 2, :], ACT.Silu), v)

            def core():
                dready, xbr = st_["dready"], st_["xb"]
                xr = []
                for t in range(2):
                    for j in range(2):
                        b = bg_ring.take()
                        P.wait(free[b], xbr)
                        for i in range(4):
                            p = P.do(lambda: nc.tensor.transpose(
                                ps[:, b, i * 128:(i + 1) * 128], xb[:, 4 * j + i, t * 128:(t + 1) * 128],
                                ident))
                        a = A.do(lambda: nc.scalar.copy(xtok[:, t, j * 512:(j + 1) * 512], ps[:, b, :]), p)
                        free[b] = [a]
                        if j == 0:
                            yield
                    xr.append(V.do(lambda: nc.vector.tensor_tensor(
                        by(xdt[:, t, :]), by(xtok[:, t, :]), bc(dt_[:, 16 * t:16 * t + 16]), ALU.mult), a,
                        dready))
                    st_["turned"] = p
                    yield
                b = bg_ring.take()
                P.wait(free[b])
                for g in range(2):
                    p = P.do(lambda: nc.tensor.transpose(ps[:, b, g * 128:(g + 1) * 128], xb[:, 8 + g, 0:128],
                                                         ident))
                bt = A.do(lambda: nc.scalar.copy(Btok[:], ps[:, b, 0:256]), p)
                free[b] = [bt]
                b = bg_ring.take()
                P.wait(free[b])
                for c in range(2):
                    for g in range(2):
                        i, sl = 2 * c + g, slice(c * 128, (c + 1) * 128)
                        p = P.do(mm(ps[:, b, i * 128:(i + 1) * 128], xb[:, 8 + g, sl], xb[:, 10 + g, sl],
                                    True, True))
                cb = V.do(lambda: nc.vector.tensor_tensor(
                    CBm[:], ps[:, b, :].rearrange("p (i l) -> p i l", i=4),
                    U.unsqueeze(1).to_broadcast([128, 4, 128]), ALU.mult), p)
                free[b] = [cb]
                yield
                b = bg_ring.take()
                P.wait(free[b], dready)
                P.quiet(mm(ps[:, b, 0:16], GT, da[:, 0:16], True, True))
                p = P.do(mm(ps[:, b, 16:32], U, da[:, 16:32], True, True))
                A.do(lambda: nc.scalar.activation(D0[:], ps[:, b, 0:16], ACT.Exp), p)
                a = A.do(lambda: nc.scalar.activation(E1[:], ps[:, b, 16:32], ACT.Exp))
                free[b] = [a]
                xd = V.do(lambda: nc.vector.tensor_tensor(by(xdec[:]), by(xdt[:, 0, :]), bc(D0[:]),
                                                          ALU.mult), a, xr[0])
                yield
                for g in range(2):
                    b = bg_ring.take()
                    p = P.do(mm(ps[:, b, :], Btok[:, g * 128:(g + 1) * 128],
                                xdec[:, g * 512:(g + 1) * 512], True, True), xd, bt, free[b])
                    pv = A.do(lambda: nc.scalar.copy(prev[:, g * 512:(g + 1) * 512], ps[:, b, :]), p)
                    free[b] = [pv]
                st_["states"] = p
                yield
                gread, eread = [None, None], [None, None]
                quarters = [(c, g, q) for c in range(2) for g in range(2) for q in range(2)]
                made = {}

                def decays(n):
                    c, g, q = quarters[n]
                    k, e0 = n % 2, 8 * g + 4 * q
                    v = V.do(lambda: nc.vector.tensor_tensor(
                        gda[:, k], GT.unsqueeze(1).to_broadcast([128, 4, 128]),
                        bc(da[:, 16 * c + e0:16 * c + e0 + 4], 128), ALU.mult), dready, gread[k])
                    b = bg_ring.take()
                    P.wait(v, free[b])
                    for i in range(4):
                        p = P.do(mm(ps[:, b, i * 128:(i + 1) * 128], gda[:, k, i, :], U, True, True))
                    gread[k] = p
                    a = A.do(lambda: nc.scalar.activation(
                        ex[:, k], ps[:, b, :].rearrange("p (i l) -> p i l", i=4), ACT.Exp), p, eread[k])
                    free[b] = [a]
                    made[n] = V.do(lambda: nc.vector.tensor_tensor(
                        ex[:, k], ex[:, k], CBm[:, 2 * c + g, :].unsqueeze(1).to_broadcast([128, 4, 128]),
                        ALU.mult), a, cb)

                v = None
                for n in range(9):
                    if n < 8:
                        decays(n)
                    if n >= 1:
                        c, g, q = quarters[n - 1]
                        k = (n - 1) % 2
                        yb = bg_ring.take()
                        P.wait(free[yb], made[n - 1], xr[c])
                        for i in range(4):
                            h = 8 * g + 4 * q + i
                            p = P.do(mm(ps[:, yb, i * 64:(i + 1) * 64], ex[:, k, i, :],
                                        xdt[:, c, h * 64:(h + 1) * 64], True, True))
                        eread[k] = p
                        sl = slice(g * 512 + q * 256, g * 512 + (q + 1) * 256)
                        h0 = 8 * g + 4 * q
                        yc, xc = y[:, c, sl], xtok[:, c, sl]
                        v = V.do(lambda: nc.vector.tensor_tensor(
                            by(xc), by(xc), bc(sm[:, 32 + h0:36 + h0]), ALU.mult), xr[c])
                        v = V.do(lambda: nc.vector.tensor_tensor(yc, ps[:, yb, 0:256], xc, ALU.add), v, p,
                                 st_["pooled"] if c == 1 else None)
                        free[yb] = [v]
                        if c == 1:
                            b = bg_ring.take()
                            p = P.do(mm(ps[:, b, 0:256], xb[:, 10 + g, 128:256], prev[:, sl], True, True),
                                     pv, free[b])
                            v2 = V.do(lambda: nc.vector.tensor_tensor(
                                by(xc), by(ps[:, b, 0:256]), bc(E1[:, h0:h0 + 4]), ALU.mult), p, v)
                            free[b] = [v2]
                            v = V.do(lambda: nc.vector.tensor_tensor(yc, yc, xc, ALU.add), v2)
                        st_["y", c] = v
                        st_["xb_read"] = p
                    yield

            def pooling():
                last = [st_["states"], None]
                bufs = [gda2[:, 0:S], gda2[:, S:2 * S]]
                for g in range(4):
                    u, src = us[:, g, :], us[:, g, :]
                    v = st_["us"]
                    for i in range(g + 1):
                        sh, dst = 1 << i, bufs[i % 2]
                        V.do(lambda: nc.vector.tensor_copy(dst[:, 0:sh], src[:, 0:sh]), v, last)
                        v = V.do(lambda: nc.vector.tensor_tensor(
                            dst[:, sh:S], src[:, sh:S], src[:, 0:S - sh], ALU.add), v)
                        src = dst
                    cnt = cs[:, CST["cnt"] + 16 * g:CST["cnt"] + 16 * g + 16]
                    dst = bufs[(g + 1) % 2]
                    v = V.do(lambda: nc.vector.tensor_tensor(dst[:, 0:16], src[:, 0:16], cnt, ALU.mult), v,
                             last)
                    V.do(lambda: nc.vector.tensor_tensor(dst[:, 0:16], dst[:, 0:16], u[:, 0:16],
                                                         ALU.subtract), v)
                    v = V.do(lambda: nc.vector.scalar_tensor_tensor(
                        out=dst[:, 16:S], in0=src[:, 16:S], scalar=1.0 / (2 << g), in1=u[:, 16:S],
                        op0=ALU.mult, op1=ALU.subtract))
                    st_["pooled"] = v
                    yield
                    b2 = bg_ring.take()
                    p2 = P.do(mm(ps[:, b2, 0:S], pwt[:, g, :], dst, True, True), v, pwl, free[b2])
                    last = [p2]
                    ready[g] = split_out(ps[:, b2, 0:S], Ph[:, g, :], Pl[:, g, :],
                                         vcol("pool_scale_2", g), p2)
                    free[b2] = [ready[g]]
                    yield

            gda2 = gda[:].rearrange("p a b c -> p (a b c)")
            cg = core()
            bg.tasks.append(cg)
            bg.rate = 1.0
            for m in range(2):
                b, p = f_chunk("pool", 2, xready)
                st_["us"] = A.do(lambda: nc.scalar.copy(
                    us[:, 2 * m:2 * m + 2, :].rearrange("p a b -> p (a b)"), ps[:, b, :]), p)
                free[b] = [st_["us"]]
                W.pump()
                bg.tick(1.0)
            bg.until(lambda: "states" in st_)
            bg.tasks.insert(0, pooling())
            bg_ring.banks = [4, 5, 6, 7]
            bg.rate = RATE_EVEN
            p = t_proj("z", 4, xt(XTh), xt(XTl), HALVES, acc, acc_bank, xready)
            bg.finish()
            for t in range(2):
                zr = A.do(lambda: nc.scalar.activation(
                    zS[:, t, :], ps[:, 2 * t:2 * t + 2, :].rearrange("p a b -> p (a b)"), ACT.Silu),
                    p[1, 1], st_["turned"], st_["xb_read"])
                free[2 * t] = free[2 * t + 1] = [zr]

            def tail():
                ys = []
                for c in range(2):
                    ys.append(V.do(lambda: nc.vector.tensor_tensor(y[:, c, :], y[:, c, :], zS[:, c, :],
                                                                   ALU.mult), st_["y", c], zr))
                done = rms(lambda t: y[:, t, :], lambda t: xtok[:, t, :], D, 0, ys)
                yield
                r = yield from to_feature(lambda t, kt: xtok[:, t, kt * 128:(kt + 1) * 128], 8, xt(XTh),
                                          xt(XTl), lambda kt: vcol("ssm_norm_w_2", kt), done)
                for kt in range(8):
                    ready[4 + kt] = r[kt]

            bg.tasks.append(tail())
            bg.step()
            bg.rate = 0.0
            hi = lambda kt: Ph[:, kt, :] if kt < 4 else XTh[:, kt - 4, :]
            lo = lambda kt: Pl[:, kt, :] if kt < 4 else XTl[:, kt - 4, :]

            def yready(kt):
                if kt == 3:
                    bg.finish()
                return ready[kt]

            p = t_proj("even_out", 6, hi, lo, HALVES, acc, acc_bank, yready, end=end)
            f_ring.banks = [4, 5, 6, 7]
            bg_ring.banks = [6, 7]
            return p

        def odd(xready, end):
            area = Area(mix_base)
            qh, kh = area.take([66, 8, S]), area.take([66, 8, S])
            vf = area.take([128, 2, 4, 192])
            CQh, CQl = area.take([128, 4, S], F32R), area.take([128, 4, S], F32R)
            CKh, CKl = area.take([128, 2, S], F32R), area.take([128, 2, S], F32R)
            attn = Area(area.at)
            attn_start = area.at
            area = Area(area.at + 4 * 1536 + 3 * 1536 + 256)
            early = Area(area.at)
            vm = area.take([128, 2, 4, 192])
            krt, kr2, lf = area.take([128, 2, 32]), area.take([128, 2, 32]), area.take([128, 16])
            tmp = [area.take([128, 8, 16]) for _ in range(2)]
            fk = early.take([40, S])
            fc = early.take([8, S])
            fc2 = early.take([8, S])
            cq, ckv = (lambda t: XN[:, t, 0:512]), (lambda t: XN[:, t, 512:768])
            km_area = [Area(xt_at[0] + 4096), Area(xt_at[1] + 4096)]
            km = [km_area[i].take([128, 768]) for i in range(2)]
            qm = [XN[:, t, 0:768] for t in range(2)]
            f_ring.banks = [4, 5]
            bg_ring.banks = [6, 7]
            sem_f = [sem("s_fc"), 0]
            ones = fill([(qh[64:66], 1.0), (kh[64:66], 1.0)], xready(7))
            zf = fill([(vf[:, :, :, 64:128], 0.0)], *ones)
            b, p = f_chunk("flkr", 1, xready)
            afk = A.do(lambda: nc.scalar.copy(fk[:], ps[0:40, b, 0:S]), p)
            free[b] = [afk]
            W.pump()
            st_ = {}

            def forget():
                b = bg_ring.take()
                P.wait(afk, free[b])
                for t in range(2):
                    p = P.do(lambda: nc.tensor.transpose(ps[:, b, t * 40:t * 40 + 40],
                                                         fk[:, t * 128:(t + 1) * 128], ident[0:40, 0:40]))
                v80 = ps[:, b, 0:80].rearrange("p (t c) -> p t c", t=2)
                lf3 = lf[:].rearrange("p (t c) -> p t c", t=2)
                st_["krt"] = V.do(lambda: nc.vector.tensor_copy(krt[:], v80[:, :, 8:40]), p)
                v = V.do(lambda: nc.vector.tensor_tensor(
                    lf3, v80[:, :, 0:8], sm[:, 48:56].unsqueeze(1).to_broadcast([128, 2, 8]), ALU.add), p)
                free[b] = [v]
                yield
                l, v2 = log1pexp(lf[:], area, 16, v)
                v = V.do(lambda: nc.vector.tensor_scalar(lf[:], lf[:], 0.0, None, ALU.min), v2)
                v = V.do(lambda: nc.vector.tensor_tensor(lf[:], lf[:], l[:], ALU.subtract), v)
                yield
                b = bg_ring.take()
                P.wait(v, free[b])
                P.quiet(mm(ps[0:8, b, 0:S], lf[:, 0:8], UO, True, False))
                p = P.do(mm(ps[0:8, b, 128:S], lf[:, 8:16], U, False, True))
                V.do(lambda: nc.vector.tensor_scalar(fc[:], ps[0:8, b, 0:S], 8.0, None, ALU.mult), p)
                v = V.do(lambda: nc.vector.tensor_scalar(fc2[:], ps[0:8, b, 0:S], -8.0, None, ALU.mult))
                free[b] = [v]
                for h in range(8):
                    SP.dma(lambda: nc.sync.dma_start(qh[64:65, h, :], fc[h:h + 1, :]), sem_f, v, *ones)
                    st_["f"] = SP.dma(lambda: nc.sync.dma_start(kh[65:66, h, :], fc2[h:h + 1, :]), sem_f)
                yield

            bg.tasks.append(forget())
            bg.rate = 1.0
            for tag, dst in (("qf", qh), ("kf", kh)):
                for m in range(2):
                    b, p = f_chunk(tag, 2, xready)
                    s3 = ps[:, b, :].rearrange("p (a s) -> p a s", a=2)
                    d4 = dst[0:64, 4 * m:4 * m + 4, :].rearrange("p (a c) s -> p a c s", c=2)
                    A.do(lambda: nc.scalar.copy(d4[:, :, 0, :], s3[0:64]), p)
                    qk = A.do(lambda: nc.scalar.copy(d4[:, :, 1, :], s3[64:128]))
                    free[b] = [qk]
                    W.pump()
            bg.finish()
            bg_ring.banks = [4, 5, 6, 7]
            outs, outs2, vready = {}, {}, []
            bg.tasks.append(attention(
                8, 0.125, lambda h: qh[:, h, :], lambda h: kh[:, h, :],
                lambda h, kt: value_of(vf, h, kt), xt(XTh), xt(XTl), attn, lambda h: [qk, st_["f"]],
                lambda h: vready, outs))
            d = lambda t, j: ps[:, t, 0:256]
            p = t_proj("ckv", 1, xt(XTh), xt(XTl), [(0, 256)], d, lambda t, j: t, xready, per=8)
            d2 = rms(lambda t: ps[:, t, 0:256], ckv, 256, 10, [p[0, 0], p[1, 0]])
            free[0], free[1] = [d2[0]], [d2[1]]
            p = t_proj("cq", 2, xt(XTh), xt(XTl), [(0, 512)], lambda t, j: ps[:, 2 + t, :],
                       lambda t, j: 2 + t, xready, per=4)
            d1 = rms(lambda t: ps[:, 2 + t, :], cq, 512, 8, [p[0, 0], p[1, 0]])
            free[2], free[3] = [d1[0]], [d1[1]]

            def latents():
                st_["r2"] = yield from to_feature(
                    lambda t, kt: ckv(t)[:, kt * 128:(kt + 1) * 128], 2, xt(CKh), xt(CKl),
                    lambda kt: vcol("kv_norm_w_2", kt), d2)
                st_["r1"] = yield from to_feature(
                    lambda t, kt: cq(t)[:, kt * 128:(kt + 1) * 128], 4, xt(CQh), xt(CQl),
                    lambda kt: vcol("q_norm_w_2", kt), d1)

            bg.tasks.insert(0, latents())
            bg.rate = 1.0
            p = t_proj("vf", 2, xt(XTh), xt(XTl), [(0, 512)], lambda t, j: ps[:, t, :], lambda t, j: t,
                       xready, per=4)
            xused = p[1, 0]
            for t in range(2):
                v = A.do(lambda: nc.scalar.copy(
                    value_columns(vf, t, slice(0, 4)),
                    ps[:, t, :].rearrange("p (h c d) -> p h c d", c=2, d=64)), p[t, 0], *zf)
                free[t] = [v]
            vready.append(v)
            bg.until(lambda: "r1" in st_)
            bg.rate = RATE_ODD
            p = t_proj("ukv", 1, xt(CKh), xt(CKl), HALVES, acc, acc_bank, lambda kt: st_["r2"][kt])
            zm = fill([(vm[:, :, :, 64:128], 0.0)], st_["f"], *zf)
            tf = None
            for t in range(2):
                tf = rope_half(krt[:, t:t + 1, :], kr2[:, t:t + 1, :], 1, 16, ROPE2, t, [st_["krt"]], tmp,
                               tf)
                k3 = km[t][:].rearrange("p (h d) -> p h d", d=96)
                sv = ps[:, 2 * t:2 * t + 2, :].rearrange("p a (h c d) -> p (a h) c d", c=2, d=64)
                ka = A.do(lambda: nc.scalar.copy(k3[:, :, 0:64], sv[:, :, 0, :]), p[1, 1], xused)
                va = A.do(lambda: nc.scalar.copy(
                    value_columns(vm, t, slice(0, 4)), ps[:, 2 * t:2 * t + 2, :].rearrange(
                        "p a (h q c d) -> p (a h) q c d", q=2, c=2, d=64)[:, :, :, 1, :]), *zm)
                kv_ = V.do(lambda: nc.vector.tensor_copy(
                    k3[:, :, 64:96], kr2[:, t, :].unsqueeze(1).to_broadcast([128, 8, 32])), tf, xused)
                free[2 * t] = free[2 * t + 1] = [va]
            kready = [ka, kv_]
            p = t_proj("uq", 2, xt(CQh), xt(CQl), [(0, 384), (384, 768)],
                       lambda t, j: ps[:, 2 * t + j, 0:384], acc_bank, lambda kt: st_["r1"][kt])
            for t in range(2):
                q3 = qm[t].rearrange("p (h d) -> p h d", d=96)
                sv = ps[:, 2 * t:2 * t + 2, 0:384].rearrange("p a (h d) -> p a h d", d=96)
                qa = A.do(lambda: nc.scalar.copy(
                    qm[t].rearrange("p (a h d) -> p a h d", a=2, d=96)[:, :, :, 0:64],
                    sv[:, :, :, 0:64]), p[1, 1])
                for a_ in range(2):
                    tf = rope_half(sv[:, a_, :, 64:96], q3[:, 4 * a_:4 * a_ + 4, 64:96], 4, 16, ROPE2, t,
                                   [qa], tmp, tf)
                free[2 * t] = free[2 * t + 1] = [qa, tf]
            qready = [qa, tf]
            bg.finish()
            qmT, kmT = Area(mix_base).take([96, 8, S]), Area(mix_base + 8192).take([96, 8, S])
            attn2 = Area(attn_start)

            def latent_attention():
                tr = []
                for src, dst, rd in ((km, kmT, kready), (qm, qmT, qready)):
                    for i0 in range(0, 8, 2):
                        b = bg_ring.take()
                        P.wait(free[b], *rd)
                        for i in (i0, i0 + 1):
                            for t in range(2):
                                o = ps[0:96, b, (i - i0) * S + t * 128:(i - i0) * S + (t + 1) * 128]
                                p = P.do(lambda: nc.tensor.transpose(o, src[t][:, i * 96:(i + 1) * 96],
                                                                     ident))
                        e, cp = ((A, nc.scalar.copy), (V, nc.vector.tensor_copy))[(i0 // 2) % 2]
                        done = e.do(lambda: cp(dst[:, i0:i0 + 2, :].rearrange("p a b -> p (a b)"),
                                               ps[0:96, b, :]), p)
                        free[b] = [done]
                        tr.append(done)
                    yield
                yield from attention(8, float(96) ** -0.5, lambda h: qmT[:, h, :], lambda h: kmT[:, h, :],
                                     lambda h, kt: value_of(vm, h, kt),
                                     lambda kt: XTh[:, 4 + kt, :], lambda kt: XTl[:, 4 + kt, :], attn2,
                                     lambda h: tr + [va], lambda h: [va], outs2)

            bg.tasks.append(latent_attention())
            bg.step()
            bg.rate = RATE_ODD_OUT

            def oready(kt):
                if kt < 4:
                    return outs[kt]
                bg.until(lambda: kt - 4 in outs2)
                return outs2[kt - 4]

            p = t_proj("odd_out", 4, xt(XTh), xt(XTl), HALVES, acc, acc_bank, oready, end=end)
            bg.finish()
            f_ring.banks = [4, 5, 6, 7]
            bg_ring.banks = [6, 7]
            return p

        first = RmsNorm(XN)
        sl = slice(CST["ident"], CST["ident"] + 128)
        SP.dma(lambda: nc.sync.dma_start(cs[:, sl], cst[:, sl]), sem_id)
        identity = (sem_id[0], sem_id[1])
        W.load(0)
        W.load(1)
        for sl in (slice(0, CST["ident"]), slice(CST["ident"] + 128, NCST)):
            if sl.stop > sl.start:
                SP.dma(lambda: nc.sync.dma_start(cs[:, sl], cst[:, sl]), sem_in)
        SP.dma(lambda: nc.sync.dma_start(vecs[:], vec), sem_in)
        rest = SP.dma(lambda: nc.sync.dma_start(sm[:], small.partition_broadcast(128)), sem_in)
        for i in range(2, NRAW):
            W.load(i)
        first.open(identity)
        for _ in range(N_WARM):
            P.quiet(mm(ps[:, 0, 0:256], identr[:], XTh[:, 0, :], True, True), first.xready(0, False))
        W.start()
        A.wait(rest)
        V.wait(rest)
        mask_done.append(A.do(lambda: nc.scalar.copy(maskr[:], MASK)))
        end = first
        for layer in range(2):
            mixed = RmsNorm(XN, end.done)
            (short_conv, moba)[layer](end.xready, mixed)
            end = RmsNorm(X if layer == 1 else XN, mixed.done)
            ffn(layer, True, mixed.xready, end)
        sem_out = [sem("s_out"), 0]
        stored = []

        def store(t, j, v):
            sl = slice(j * 512, (j + 1) * 512)
            stored.append(SP.dma(lambda: nc.sync.dma_start(out[0, t * 128:(t + 1) * 128, sl], X[:, t, sl]),
                                 sem_out, v))

        for layer in range(2):
            mixed = LayerNorm(end.done)
            (even, odd)[layer](end.xready, mixed)
            end = LayerNorm(mixed.done, store if layer == 1 else None)
            ffn(layer, False, mixed.xready, end)
        SP.wait(stored[-1])
        assert W.i == len(plan)


def layout(i):
    plan = weight_plan()
    wts = np.zeros((len(plan), 128, CW), np.float32)
    for n, (_, _, name, layer, cols, width, nk, k0) in enumerate(plan):
        w = i[name][layer]
        dst = wts[n, :, 0:width * nk].reshape(128, nk, width)
        at = 0
        for c0, m in cols:
            blk = w[k0 * 128:(k0 + nk) * 128, c0:c0 + m]
            dst[:, :, at:at + m] = blk.reshape(nk, 128, m).transpose(1, 0, 2)
            at += m
    vec = np.zeros((128, NVEC), np.float32)
    for name, c in VEC.items():
        a = i[name].reshape(-1, 128)
        vec[:, c:c + a.shape[0]] = a.T
    rows = np.stack([i["mix_norm"][0], i["ffn_norm"][0], i["mix_norm"][1], i["ffn_norm"][1],
                     i["final_norm"], i["ln_mix_g_2"][0], i["ln_mix_b_2"][0], i["ln_ffn_g_2"][0],
                     i["ln_ffn_b_2"][0], i["ln_mix_g_2"][1], i["ln_mix_b_2"][1], i["ln_ffn_g_2"][1],
                     i["ln_ffn_b_2"][1]])
    small = np.concatenate([i["dt_bias_2"][0], i["a_log_2"][0], i["d_skip_2"][0], i["fgate_b_2"][0]])
    pw = np.ascontiguousarray(i["pool_w_2"][0].transpose(1, 0, 2))
    cst = constants()
    return dict(wts=wts, vec=vec, cst=cst, rows=rows, small=small, pw=pw,
                x_in=np.ascontiguousarray(i["x"]))


def kernel(**inputs):
    import concourse.bacc as _bacc
    from concourse.bass_utils import run_bass_kernel_spmd as _run

    nc = _bacc.Bacc("TRN2", target_bir_lowering=False, num_devices=1)
    arrays = layout({k: np.asarray(v) for k, v in inputs.items()})
    args = {k: nc.dram_tensor("in_" + k, a.shape, mybir.dt.from_np(a.dtype), kind="ExternalInput").ap()
            for k, a in arrays.items()}
    out = nc.dram_tensor("out_0", (1, S, D), F32, kind="ExternalOutput").ap()
    build(nc, out=out, **args)
    r = _run(nc, [{"in_" + k: a for k, a in arrays.items()}], core_ids=[0])
    return r.results[0]["out_0"]
```
